# Optimizing a Trainium2 kernel written in Bass

```python
import jax, jax.numpy as jnp
from jax import lax
import numpy as np
import math

D_MODEL = 1024
BATCH = 1
SEQ = 1024
DEPTH = 1

MEM_LEN = 256
EXPAND = 2
D_MIX = EXPAND * D_MODEL
GLA_HEADS = 4
GLA_HEAD_K = 128
GLA_HEAD_V = 256
GLA_KEY_WIDTH = GLA_HEADS * GLA_HEAD_K
GLA_VAL_WIDTH = GLA_HEADS * GLA_HEAD_V
GLA_LOWRANK = 16
GLA_GATE_TAU = 16.0
HGRN_HEADS = 4
HGRN_HEAD_DIM = 128
HGRN_WIDTH = HGRN_HEADS * HGRN_HEAD_DIM
LB_FLOOR = 1e-30
XATTN_HEADS = 4
XATTN_HEAD_DIM = 128
XATTN_WIDTH = XATTN_HEADS * XATTN_HEAD_DIM
SPLIT_SIZES = (GLA_KEY_WIDTH, GLA_KEY_WIDTH, GLA_VAL_WIDTH, GLA_LOWRANK,
               HGRN_WIDTH, HGRN_WIDTH, HGRN_WIDTH,
               XATTN_WIDTH,
               D_MIX)
D_IN_PROJ = 6160
CHUNK = 16
NORM_EPS = 1e-6


def rms_norm(x, w):
    xf = x.astype(jnp.float32)
    y = xf * lax.rsqrt(jnp.mean(xf * xf, axis=-1, keepdims=True) + NORM_EPS)
    return (y * w.astype(jnp.float32)).astype(x.dtype)

def split_heads(t, n_heads):
    b, s, w = t.shape
    return t.reshape(b, s, n_heads, w // n_heads).transpose(0, 2, 1, 3)

def merge_heads(t):
    b, h, s, d = t.shape
    return t.transpose(0, 2, 1, 3).reshape(b, s, h * d)

def chunked_gated_linear_attention(q, k, v, log_g):
    b_, h_, s_, dk = q.shape
    dv = v.shape[-1]
    n = s_ // CHUNK
    qf = q.astype(jnp.float32).reshape(b_, h_, n, CHUNK, dk)
    kf = k.astype(jnp.float32).reshape(b_, h_, n, CHUNK, dk)
    vf = v.astype(jnp.float32).reshape(b_, h_, n, CHUNK, dv)
    bcum = jnp.cumsum(log_g.astype(jnp.float32).reshape(b_, h_, n, CHUNK, dk), axis=3)
    b_last = bcum[..., CHUNK - 1:CHUNK, :]
    causal = jnp.tril(jnp.ones((CHUNK, CHUNK), dtype=bool))[:, :, None]
    diff = bcum[..., :, None, :] - bcum[..., None, :, :]
    decay = jnp.where(causal, jnp.exp(jnp.where(causal, diff, 0.0)), 0.0)
    scores = jnp.einsum('bhnid,bhnjd,bhnijd->bhnij', qf, kf, decay)
    o_intra = jnp.einsum('bhnij,bhnjv->bhniv', scores, vf)
    chunk_kv = jnp.einsum('bhncd,bhncv->bhndv', kf * jnp.exp(b_last - bcum), vf)
    chunk_decay = jnp.exp(b_last[..., 0, :])

    def step(state, inp):
        dec, kv = inp
        return dec[..., None] * state + kv, state

    init = jnp.zeros((b_, h_, dk, dv), jnp.float32)
    _, states_prev = lax.scan(step, init, (jnp.moveaxis(chunk_decay, 2, 0), jnp.moveaxis(chunk_kv, 2, 0)))
    o_inter = jnp.einsum('bhncd,nbhdv->bhncv', qf * jnp.exp(bcum), states_prev)
    return (o_intra + o_inter).reshape(b_, h_, s_, dv)

def first_inputs(seed: int = 0) -> dict:
    key = jax.random.key(seed)
    ks = jax.random.split(key, 14)
    f32 = jnp.float32
    nrm = lambda k, shape, scale: (jax.random.normal(k, shape, f32) * scale).astype(f32)
    return {
        "x": nrm(ks[0], (BATCH, SEQ, D_MODEL), 1.0),
        "mem": nrm(ks[1], (BATCH, MEM_LEN, D_MODEL), 1.0),
        "norm_w": 1.0 + nrm(ks[2], (DEPTH, D_MODEL), 0.1),
        "w_in": nrm(ks[3], (DEPTH, D_MODEL, D_IN_PROJ), D_MODEL ** -0.5),
        "gla_w_gate_up": nrm(ks[4], (DEPTH, GLA_LOWRANK, GLA_KEY_WIDTH), GLA_LOWRANK ** -0.5),
        "gla_b_gate": nrm(ks[5], (DEPTH, GLA_KEY_WIDTH), 0.1),
        "gla_norm_w": 1.0 + nrm(ks[6], (DEPTH, GLA_HEAD_V), 0.1),
        "hgrn_lower_bounds": nrm(ks[7], (DEPTH, HGRN_WIDTH), 0.5),
        "hgrn_norm_w": 1.0 + nrm(ks[8], (DEPTH, HGRN_HEAD_DIM), 0.1),
        "mem_norm_w": 1.0 + nrm(ks[9], (DEPTH, D_MODEL), 0.1),
        "w_mem_kv": nrm(ks[10], (DEPTH, D_MODEL, 2 * XATTN_WIDTH), D_MODEL ** -0.5),
        "xattn_norm_w": 1.0 + nrm(ks[11], (DEPTH, XATTN_HEAD_DIM), 0.1),
        "w_out": nrm(ks[12], (DEPTH, D_MIX, D_MODEL), D_MIX ** -0.5),
        "final_norm_w": 1.0 + nrm(ks[13], (D_MODEL,), 0.1),
    }

def first_block(x, mem, norm_w, w_in, gla_w_gate_up, gla_b_gate, gla_norm_w, hgrn_lower_bounds,
              hgrn_norm_w, mem_norm_w, w_mem_kv, xattn_norm_w, w_out, final_norm_w):
    dtype = x.dtype
    split_idx = [int(i) for i in np.cumsum(SPLIT_SIZES)[:-1]]
    lb_p = jax.nn.softmax(hgrn_lower_bounds.astype(jnp.float32), axis=0)
    lower_bounds = jnp.cumsum(lb_p, axis=0) - lb_p[0]

    for layer in range(DEPTH):
        h = rms_norm(x, norm_w[layer])
        proj = jnp.einsum('bsd,de->bse', h, w_in[layer])
        (gq, gk, gv, glr, hq, hf, hi, xq, gate) = jnp.split(proj, split_idx, axis=-1)

        glr_up = jnp.einsum('bsr,rk->bsk', glr, gla_w_gate_up[layer]) + gla_b_gate[layer]
        gla_log_a = jax.nn.log_sigmoid(glr_up.astype(jnp.float32)) / GLA_GATE_TAU
        gla_o = chunked_gated_linear_attention(
            split_heads(gq, GLA_HEADS) * (GLA_HEAD_K ** -0.5), split_heads(gk, GLA_HEADS),
            split_heads(gv, GLA_HEADS), split_heads(gla_log_a, GLA_HEADS))
        gla_o = merge_heads(rms_norm(gla_o, gla_norm_w[layer]))

        lb = lower_bounds[layer]
        zf = hf.astype(jnp.float32)
        hgrn_log_f = jnp.logaddexp(jnp.log(jnp.maximum(lb, LB_FLOOR)),
                                   jnp.log1p(-lb) + jax.nn.log_sigmoid(zf))
        hgrn_k = (1.0 - lb) * jax.nn.sigmoid(-zf)
        hgrn_o = chunked_gated_linear_attention(
            split_heads(hq, HGRN_HEADS), split_heads(hgrn_k, HGRN_HEADS),
            split_heads(hi, HGRN_HEADS), split_heads(hgrn_log_f, HGRN_HEADS))
        hgrn_o = merge_heads(rms_norm(hgrn_o, hgrn_norm_w[layer]))

        m = rms_norm(mem, mem_norm_w[layer])
        mkv = jnp.einsum('bmd,de->bme', m, w_mem_kv[layer])
        mk, mv = jnp.split(mkv, 2, axis=-1)
        s = jnp.einsum('bhsd,bhmd->bhsm', split_heads(xq, XATTN_HEADS).astype(jnp.float32),
                       split_heads(mk, XATTN_HEADS).astype(jnp.float32)) * (XATTN_HEAD_DIM ** -0.5)
        p = jax.nn.softmax(s, axis=-1)
        xo = jnp.einsum('bhsm,bhmd->bhsd', p, split_heads(mv, XATTN_HEADS).astype(jnp.float32))
        xo = merge_heads(rms_norm(xo, xattn_norm_w[layer]))

        mixed = jnp.concatenate([gla_o, hgrn_o, xo], axis=-1).astype(dtype)
        mixed = mixed * jax.nn.silu(gate)
        x = x + jnp.einsum('bse,ed->bsd', mixed, w_out[layer]).astype(dtype)

    return rms_norm(x, final_norm_w)


GRID_W = 64
CTX_LEN = 256
N_MIXERS = 2
N_CONV_LAYERS = (DEPTH + N_MIXERS - 1) // N_MIXERS
N_DELTA_LAYERS = DEPTH // N_MIXERS
CONV_WIDTH = 31
DN_HEADS = 8
DN_HEAD_DIM = D_MODEL // DN_HEADS
DN_SHORT_CONV = 5
DN_CHUNK = 64
N_DIRS = 2
DN_QKV = 3 * D_MODEL
DN_IN = 4 * D_MODEL + 2 * N_DIRS * DN_HEADS
FFN_HIDDEN = 4 * D_MODEL
EPS = 1e-6


def rms_norm_2(x, g):
    xf = x.astype(jnp.float32)
    y = xf * lax.rsqrt(jnp.mean(xf * xf, axis=-1, keepdims=True) + EPS)
    return (y * g.astype(jnp.float32)).astype(x.dtype)

def layer_norm(x, g, b):
    xf = x.astype(jnp.float32)
    mu = jnp.mean(xf, axis=-1, keepdims=True)
    xc = xf - mu
    y = xc * lax.rsqrt(jnp.mean(xc * xc, axis=-1, keepdims=True) + EPS)
    return (y * g.astype(jnp.float32) + b.astype(jnp.float32)).astype(x.dtype)

def l2_norm(x):
    xf = x.astype(jnp.float32)
    return xf * lax.rsqrt(jnp.sum(xf * xf, axis=-1, keepdims=True) + EPS)

def modulate(h, shift, scale):
    return h * (1.0 + scale) + shift

def dwconv(x, w):
    K, C = w.shape
    return lax.conv_general_dilated(
        x, w[:, None, :].astype(x.dtype), window_strides=(1,),
        padding=[(K // 2, K // 2)], dimension_numbers=('NWC', 'WIO', 'NWC'),
        feature_group_count=C)

def conformer_conv(h, n_seg, w_pw1, b_pw1, w_dw, b_dw, ln_g, ln_b, w_pw2, b_pw2):
    B, L, D = h.shape
    u = h @ w_pw1 + b_pw1
    a, gate = jnp.split(u, 2, axis=-1)
    u = a * jax.nn.sigmoid(gate)
    u = dwconv(u.reshape(B * n_seg, L // n_seg, D), w_dw).reshape(B, L, D) + b_dw
    u = jax.nn.silu(layer_norm(u, ln_g, ln_b))
    return u @ w_pw2 + b_pw2

def gated_delta_chunked(q, k, v, g, beta, state):
    B, H, L, DK = q.shape
    DV = v.shape[-1]
    C = DN_CHUNK
    NC = L // C
    q = q.reshape(B, H, NC, C, DK)
    k = k.reshape(B, H, NC, C, DK)
    v = v.reshape(B, H, NC, C, DV)
    g = g.reshape(B, H, NC, C)
    beta = beta.reshape(B, H, NC, C)
    G = jnp.cumsum(g, axis=-1)
    lower = jnp.tril(jnp.ones((C, C), dtype=bool))
    strict = jnp.tril(jnp.ones((C, C), dtype=bool), -1)
    decay = jnp.exp(jnp.where(lower, G[..., :, None] - G[..., None, :], -jnp.inf))
    kk = jnp.einsum('bhncd,bhnsd->bhncs', k, k)
    a_mat = jnp.where(strict, beta[..., :, None] * kk * decay, 0.0)
    eye = jnp.broadcast_to(jnp.eye(C, dtype=q.dtype), a_mat.shape)
    rhs = jnp.concatenate([beta[..., None] * v, (beta * jnp.exp(G))[..., None] * k], axis=-1)
    sol = lax.linalg.triangular_solve(a_mat + eye, rhs, left_side=True, lower=True,
                                      unit_diagonal=True)
    u, w = sol[..., :DV], sol[..., DV:]
    qk = jnp.einsum('bhncd,bhnsd->bhncs', q, k) * decay
    qg = q * jnp.exp(G)[..., None]
    kd = k * jnp.exp(G[..., -1:] - G)[..., None]
    chunk_decay = jnp.exp(G[..., -1])
    xs = tuple(jnp.moveaxis(t, 2, 0) for t in (u, w, qg, qk, kd, chunk_decay))

    def step(S, inp):
        u_c, w_c, qg_c, qk_c, kd_c, cd_c = inp
        v_new = u_c - jnp.einsum('bhcd,bhde->bhce', w_c, S)
        o_c = (jnp.einsum('bhcd,bhde->bhce', qg_c, S)
               + jnp.einsum('bhcs,bhse->bhce', qk_c, v_new))
        S = S * cd_c[..., None, None] + jnp.einsum('bhcd,bhce->bhde', kd_c, v_new)
        return S, o_c

    state, o = lax.scan(step, state, xs)
    o = jnp.moveaxis(o, 0, 2).reshape(B, H, L, DV)
    return o, state

def gdn_project(h, w_in, conv_w, a_log, dt_bias):
    B, L, _ = h.shape
    p = h @ w_in
    qkv = jax.nn.silu(dwconv(p[..., :DN_QKV], conv_w))
    z = p[..., DN_QKV:4 * D_MODEL].reshape(B, L, DN_HEADS, DN_HEAD_DIM)
    ab = p[..., 4 * D_MODEL:].astype(jnp.float32).reshape(B, L, 2, N_DIRS, DN_HEADS)
    to_heads = lambda t: t.reshape(B, L, DN_HEADS, DN_HEAD_DIM).transpose(0, 2, 1, 3)
    q, k, v = jnp.split(qkv, 3, axis=-1)
    q = l2_norm(to_heads(q)) * (DN_HEAD_DIM ** -0.5)
    k = l2_norm(to_heads(k))
    v = to_heads(v).astype(jnp.float32)
    g = -jnp.exp(a_log.astype(jnp.float32)) * jax.nn.softplus(ab[:, :, 0] + dt_bias.astype(jnp.float32))
    beta = jax.nn.sigmoid(ab[:, :, 1])
    return q, k, v, z, jnp.transpose(g, (2, 0, 3, 1)), jnp.transpose(beta, (2, 0, 3, 1))

def gdn_output(o, z, norm_g, w_o, dtype):
    B, H, L, DV = o.shape
    o = rms_norm_2(o.transpose(0, 2, 1, 3), norm_g) * jax.nn.silu(z.astype(jnp.float32))
    return o.reshape(B, L, H * DV).astype(dtype) @ w_o

def gated_deltanet_bidir(hc, hl, w_in, conv_w, a_log, dt_bias, norm_g, w_o):
    qc, kc, vc, zc, gc, bc = gdn_project(hc, w_in, conv_w, a_log, dt_bias)
    ql, kl, vl, zl, gl, bl = gdn_project(hl, w_in, conv_w, a_log, dt_bias)
    B = hl.shape[0]
    s0 = jnp.zeros((B, DN_HEADS, DN_HEAD_DIM, DN_HEAD_DIM), jnp.float32)
    fl = lambda t: jnp.flip(t, axis=2)
    oc_f, sc_f = gated_delta_chunked(qc, kc, vc, gc[0], bc[0], s0)
    ol_f, _ = gated_delta_chunked(ql, kl, vl, gl[0], bl[0], sc_f)
    oc_b, sc_b = gated_delta_chunked(fl(qc), fl(kc), fl(vc), fl(gc[1]), fl(bc[1]), s0)
    ol_b, _ = gated_delta_chunked(fl(ql), fl(kl), fl(vl), fl(gl[1]), fl(bl[1]), sc_b)
    yc = gdn_output(oc_f + fl(oc_b), zc, norm_g, w_o, hc.dtype)
    yl = gdn_output(ol_f + fl(ol_b), zl, norm_g, w_o, hl.dtype)
    return yc, yl

def sq_relu_mlp(h, w1, w2):
    return jnp.square(jax.nn.relu(h @ w1)) @ w2

def second_inputs(seed: int = 0) -> dict:
    key = jax.random.key(seed)
    ks = jax.random.split(key, 26)
    D = D_MODEL
    NA, NB = N_CONV_LAYERS, N_DELTA_LAYERS
    nrm = lambda k, shape, s: jax.random.normal(k, shape, jnp.float32) * s
    dt = jnp.exp(jax.random.uniform(ks[20], (NB, N_DIRS, DN_HEADS), jnp.float32,
                                    minval=math.log(1e-3), maxval=math.log(1e-1)))
    return {
        "x": nrm(ks[0], (BATCH, SEQ, D), 1.0),
        "c": nrm(ks[1], (BATCH, D), 1.0),
        "ctx": nrm(ks[2], (BATCH, CTX_LEN, D), 1.0),
        "c_ctx": nrm(ks[3], (D,), 1.0),
        "w_mod": nrm(ks[4], (DEPTH, D, 6 * D), 0.5 * D ** -0.5),
        "b_mod": nrm(ks[5], (DEPTH, 6 * D), 0.02),
        "norm1_g": 1.0 + nrm(ks[6], (DEPTH, D), 0.02),
        "norm2_g": 1.0 + nrm(ks[7], (DEPTH, D), 0.02),
        "final_g": 1.0 + nrm(ks[8], (D,), 0.02),
        "conv_w_pw1": nrm(ks[9], (NA, D, 2 * D), D ** -0.5),
        "conv_b_pw1": nrm(ks[10], (NA, 2 * D), 0.02),
        "conv_w_dw": nrm(ks[11], (NA, CONV_WIDTH, D), CONV_WIDTH ** -0.5),
        "conv_b_dw": nrm(ks[12], (NA, D), 0.02),
        "conv_ln_g": 1.0 + nrm(ks[13], (NA, D), 0.02),
        "conv_ln_b": nrm(ks[14], (NA, D), 0.02),
        "conv_w_pw2": nrm(ks[15], (NA, D, D), D ** -0.5),
        "conv_b_pw2": nrm(ks[16], (NA, D), 0.02),
        "dn_w_in": nrm(ks[17], (NB, D, DN_IN), D ** -0.5),
        "dn_conv_w": nrm(ks[18], (NB, DN_SHORT_CONV, DN_QKV), DN_SHORT_CONV ** -0.5),
        "dn_a_log": jnp.log(jax.random.uniform(ks[19], (NB, N_DIRS, DN_HEADS), jnp.float32,
                                               minval=1.0, maxval=16.0)),
        "dn_dt_bias": dt + jnp.log(-jnp.expm1(-dt)),
        "dn_norm_g": 1.0 + nrm(ks[21], (NB, DN_HEAD_DIM), 0.02),
        "dn_w_o": nrm(ks[22], (NB, D, D), D ** -0.5),
        "mlp_w1": nrm(ks[23], (DEPTH, D, FFN_HIDDEN), D ** -0.5),
        "mlp_w2": nrm(ks[24], (DEPTH, FFN_HIDDEN, D), FFN_HIDDEN ** -0.5),
    }

def second_block(x, c, ctx, c_ctx, w_mod, b_mod, norm1_g, norm2_g, final_g,
              conv_w_pw1, conv_b_pw1, conv_w_dw, conv_b_dw, conv_ln_g, conv_ln_b,
              conv_w_pw2, conv_b_pw2, dn_w_in, dn_conv_w, dn_a_log, dn_dt_bias,
              dn_norm_g, dn_w_o, mlp_w1, mlp_w2):
    rows = x.shape[1] // GRID_W
    xl, xc = x, ctx
    sc_l = jax.nn.silu(c)
    sc_c = jax.nn.silu(c_ctx)
    for i in range(DEPTH):
        last = i == DEPTH - 1
        j = i // N_MIXERS
        mod_l = (sc_l @ w_mod[i] + b_mod[i])[:, None, :]
        mod_c = (sc_c @ w_mod[i] + b_mod[i])[None, None, :]
        sh1_l, s1_l, g1_l, sh2_l, s2_l, g2_l = jnp.split(mod_l, 6, axis=-1)
        sh1_c, s1_c, g1_c, sh2_c, s2_c, g2_c = jnp.split(mod_c, 6, axis=-1)
        hl = modulate(rms_norm_2(xl, norm1_g[i]), sh1_l, s1_l)
        hc = modulate(rms_norm_2(xc, norm1_g[i]), sh1_c, s1_c)
        if i % N_MIXERS == 0:
            conv_p = (conv_w_pw1[j], conv_b_pw1[j], conv_w_dw[j], conv_b_dw[j],
                      conv_ln_g[j], conv_ln_b[j], conv_w_pw2[j], conv_b_pw2[j])
            yl = conformer_conv(hl, rows, *conv_p)
            if not last:
                yc = conformer_conv(hc, 1, *conv_p)
        else:
            yc, yl = gated_deltanet_bidir(hc, hl, dn_w_in[j], dn_conv_w[j], dn_a_log[j],
                                          dn_dt_bias[j], dn_norm_g[j], dn_w_o[j])
        xl = xl + g1_l * yl
        xl = xl + g2_l * sq_relu_mlp(modulate(rms_norm_2(xl, norm2_g[i]), sh2_l, s2_l),
                                     mlp_w1[i], mlp_w2[i])
        if not last:
            xc = xc + g1_c * yc
            xc = xc + g2_c * sq_relu_mlp(modulate(rms_norm_2(xc, norm2_g[i]), sh2_c, s2_c),
                                         mlp_w1[i], mlp_w2[i])
    return rms_norm_2(xl, final_g)


def setup_inputs(seed=0):
    out = dict(first_inputs(seed))
    for name, value in second_inputs(seed + 1).items():
        if name != "x":
            out[name + "_2"] = value
    return out


def reference(
    x, mem, norm_w, w_in, gla_w_gate_up, gla_b_gate, gla_norm_w, hgrn_lower_bounds, hgrn_norm_w,
    mem_norm_w, w_mem_kv, xattn_norm_w, w_out, final_norm_w, c_2, ctx_2, c_ctx_2, w_mod_2,
    b_mod_2, norm1_g_2, norm2_g_2, final_g_2, conv_w_pw1_2, conv_b_pw1_2, conv_w_dw_2,
    conv_b_dw_2, conv_ln_g_2, conv_ln_b_2, conv_w_pw2_2, conv_b_pw2_2, dn_w_in_2, dn_conv_w_2,
    dn_a_log_2, dn_dt_bias_2, dn_norm_g_2, dn_w_o_2, mlp_w1_2, mlp_w2_2,
):
    x = first_block(
        x, mem, norm_w, w_in, gla_w_gate_up, gla_b_gate, gla_norm_w, hgrn_lower_bounds,
        hgrn_norm_w, mem_norm_w, w_mem_kv, xattn_norm_w, w_out, final_norm_w,
    )
    return second_block(
        x, c_2, ctx_2, c_ctx_2, w_mod_2, b_mod_2, norm1_g_2, norm2_g_2, final_g_2, conv_w_pw1_2,
        conv_b_pw1_2, conv_w_dw_2, conv_b_dw_2, conv_ln_g_2, conv_ln_b_2, conv_w_pw2_2,
        conv_b_pw2_2, dn_w_in_2, dn_conv_w_2, dn_a_log_2, dn_dt_bias_2, dn_norm_g_2, dn_w_o_2,
        mlp_w1_2, mlp_w2_2,
    )


_drawn_inputs = setup_inputs


def setup_inputs(seed=0):
    import zlib

    import numpy as np

    out = dict(_drawn_inputs(seed))
    spreads = {}
    factors = {'gla_b_gate': 3.319,
     'norm1_g_2': 8.0,
     'norm2_g_2': 17.492,
     'final_g_2': 19.491,
     'conv_b_pw1_2': 8.0,
     'conv_b_dw_2': 8.0,
     'conv_ln_g_2': 23.051,
     'conv_ln_b_2': 23.63,
     'conv_b_pw2_2': 40.894}
    for name, (base, spread) in spreads.items():
        noise = np.random.default_rng([zlib.crc32(name.encode()), seed]).standard_normal(out[name].shape)
        drawn = base * np.exp(spread * noise) if base else spread * noise
        out[name] = __import__('jax').numpy.asarray(drawn.astype(out[name].dtype))
    for name, factor in factors.items():
        out[name] = (out[name] * factor).astype(out[name].dtype)
    return out
```

```python
from contextlib import ExitStack

import numpy as np
import concourse.bass as bass
from concourse import mybir

F32 = mybir.dt.float32
F32R = mybir.dt.float32r
U8 = mybir.dt.uint8
ALU = mybir.AluOpType
ACT = mybir.ActivationFunctionType
AXX = mybir.AxisListType.X

T = 1024
D = 1024
NT = T // 128
KT = D // 128
EPS = 1e-6
SCALE = 128.0 ** -0.5
FLOOR = 1e-30
SEG = 64
NSEG = T // SEG
TAPS = 31
PAD = TAPS // 2
SEGP = SEG + 2 * PAD
NG = 4
GT = 4
HG = 8

VECS = [("norm_w", 8), ("b_gate", 4), ("gla_nw", 2), ("lb", 4), ("hgrn_nw", 1), ("mem_nw", 8), ("x_nw", 1),
        ("fin_w", 8), ("c", 8), ("b_mod", 48), ("n1", 8), ("n2", 8), ("fin_g", 8), ("b_pw1", 16),
        ("w_dw", 8 * TAPS), ("b_dw", 8), ("ln_g", 8), ("ln_b", 8), ("b_pw2", 8)]
VOFF, _o = {}, 0
for _n, _c in VECS:
    VOFF[_n] = _o
    _o += _c
NV = _o


def unit_plan():
    plan = [("mk", i) for i in range(4)] + [("mv", i) for i in range(4)] + [("glr",)]
    for h in range(4):
        plan += [("gq", h), ("gk", h), ("gv", h, 0), ("gv", h, 1)]
    for p in range(2):
        for h in (2 * p, 2 * p + 1):
            plan += [("hq", h), ("hf", h)]
        plan += [("hi", p, 0), ("hi", p, 1)]
    plan += [("xq", h) for h in range(4)]
    plan += [("gate", e) for e in range(6)] + [("wo", 0, j) for j in range(4)]
    for g in range(1, NG):
        plan += [("gate", e) for e in range(4 * g + 2, min(4 * g + 6, 16))]
        plan += [("wo", g, j) for j in range(4)]
    for f in range(8):
        plan += [("pa", f), ("pg", f)]
    plan += [("pw2", f) for f in range(8)]
    plan += [("w1", i) for i in range(GT)]
    for g in range(HG):
        if g + 1 < HG:
            plan += [("w1", (g + 1) * GT + i) for i in range(GT)]
        plan += [("w2", g, j) for j in range(4)]
    return plan


UNITS = unit_plan()


class Op:
    def __init__(self, q, fn, waits):
        self.q, self.fn, self.waits, self.needed, self.count = q, fn, waits, False, 0


class Dma:
    def __init__(self, sem, count):
        self.sem, self.count = sem, count


def flat(ws):
    for w in ws:
        if w is None:
            continue
        if isinstance(w, (list, tuple)):
            yield from flat(w)
        else:
            yield w


class Queue:

    def __init__(self, sem):
        self.sem, self.ops = sem, []

    def __call__(self, fn, *waits):
        ws = list(flat(waits))
        for w in ws:
            if isinstance(w, Op):
                w.needed = True
        op = Op(self, fn, ws)
        self.ops.append((op, None))
        return op

    def dma(self, chan, fn, *waits):
        ws = list(flat(waits))
        for w in ws:
            if isinstance(w, Op):
                w.needed = True
        op = Op(self, fn, ws)
        chan.count += 16
        self.ops.append((op, chan.sem))
        return Dma(chan.sem, chan.count)

    def number(self):
        n = 0
        for op, sem in self.ops:
            if sem is None and op.needed:
                n += 1
            op.count = n

    def emit(self, eng):
        seen = {}
        for op, dsem in self.ops:
            for w in op.waits:
                sem = w.sem if isinstance(w, Dma) else w.q.sem
                if seen.get(id(sem), 0) < w.count:
                    eng.wait_ge(sem, w.count)
                    seen[id(sem)] = w.count
            ins = op.fn(eng)
            if dsem is not None:
                ins.then_inc(dsem, 16)
            elif op.needed:
                ins.then_inc(self.sem, 1)


class Chan:
    def __init__(self, sem):
        self.sem, self.count = sem, 0


class Ring:

    def __init__(self, items):
        self.items, self.n, self.free = items, 0, [None] * len(items)

    def take(self):
        i = self.n % len(self.items)
        self.n += 1
        return i, self.items[i], self.free[i]


def build_program(nc, wall, wmod, xT, memT, vecs, gup, ident_d, masks_d, out, oscr):
    es = ExitStack()
    with es:
        size = {F32: 4, F32R: 4, U8: 1}
        base = [16512]
        END = 229344

        def at(name, cols, dt, off):
            assert off + cols * size[dt] <= END, (name, off + cols * size[dt] - END)
            return nc.alloc_sbuf_tensor_at(name, [128, cols], dt, offset=off)

        def take(name, cols, dt=F32):
            o = base[0]
            base[0] += (cols * size[dt] + 31) // 32 * 32
            return at(name, cols, dt, o)

        hb0 = base[0]
        HB = take("HB", 2 * 8 * T, F32R)
        RAW = take("RAW", 3 * 1024)
        WH = take("WH", 3 * 1024, F32R)
        WL = take("WL", 3 * 1024, F32R)
        ident = take("ident", 128)
        ones = take("ones", 128)
        masks = take("masks", 7 * 512, U8)
        vec = take("vec", NV)
        small = take("small", 192)
        modv = take("modv", 64)
        res0 = base[0]
        RES = take("RES", 8 * T)
        x0 = base[0]
        K4 = 4096

        GB = [es.enter_context(nc.psum_tensor(f"G{i}", [128, 1024], F32)) for i in range(2)]
        SBK = [es.enter_context(nc.psum_tensor(f"S{i}", [128, 512], F32)) for i in range(2)]
        OBK = [es.enter_context(nc.psum_tensor(f"O{i}", [128, 512], F32)) for i in range(2)]

        def sem(name):
            return es.enter_context(nc.semaphore(name))

        PE, AC, DV, PO, SP = (Queue(sem(f"s_{n}")) for n in ("pe", "act", "dve", "pool", "sp"))
        G, S, O = Ring(GB), Ring(SBK), Ring(OBK)

        def chan(name):
            return Chan(sem(name))

        def vcol(name, i=0):
            o = VOFF[name] + i
            return vec[:, o:o + 1]

        def vcols(name, n):
            o = VOFF[name]
            return vec[:, o:o + n]

        def copy(o, i, *w, scale=None):
            if scale is None:
                return AC(lambda e: e.activation(o, i, ACT.Copy), *w)
            return AC(lambda e: e.activation(o, i, ACT.Copy, scale=scale), *w)

        def act(o, i, f, *w, **kw):
            return AC(lambda e: e.activation(o, i, f, **kw), *w)

        def tt(o, a, b, op, *w, q=None):
            return (q or DV)(lambda e: e.tensor_tensor(o, a, b, op), *w)

        def ts(o, a, s1, s2, op0, op1, *w, q=None):
            if s2 is None:
                return (q or DV)(lambda e: e.tensor_scalar(o, a, s1, None, op0), *w)
            return (q or DV)(lambda e: e.tensor_scalar(o, a, s1, s2, op0, op1), *w)

        def stt(o, a, s, b, op0, op1, *w):
            return DV(lambda e: e.scalar_tensor_tensor(out=o, in0=a, scalar=s, in1=b, op0=op0, op1=op1), *w)

        def mm(o, l, r, st, sp, *w, skip=False):
            return PE(lambda e: e.matmul(o, l, r, start=st, stop=sp, skip_group_check=skip), *w)

        def tr(o, i, *w):
            return PE(lambda e: e.transpose(o, i, ident[:, :]), *w)

        t_ident = SP.dma(chan("d_ident"), lambda e: e.dma_start(ident[:, :], ident_d))
        t_vec = SP.dma(chan("d_vec"), lambda e: e.dma_start(vec[:, :], vecs))
        t_ones = PO(lambda e: e.memset(ones[:, :], 1.0))
        mhalf = small[:, 0:8]
        t_mh = PO(lambda e: e.memset(mhalf, -0.5))

        raw_ch = [chan(f"d_raw{i}") for i in range(3)]
        n_units = len(UNITS)
        load_tok, split_tok, done_tok = {}, {}, {}
        at_unit = [0]

        def u_advance(j):
            while len(split_tok) < min(n_units, j + 3):
                q = len(split_tok)
                if q >= 3 and q - 3 not in done_tok:
                    break
                while len(load_tok) <= q:
                    u_load()
                s = slice(q % 3 * 1024, q % 3 * 1024 + 1024)
                raw, hi, lo = RAW[:, s], WH[:, s], WL[:, s]
                th = copy(hi, raw, load_tok[q], done_tok.get(q - 3))
                tl = tt(lo, raw, hi.bitcast(F32), ALU.subtract, load_tok[q], th, done_tok.get(q - 3), q=PO)
                split_tok[q] = (hi, lo, th, tl)
            while len(load_tok) < min(n_units, j + 6) and len(load_tok) - 3 in split_tok:
                u_load()

        def u_load():
            q = len(load_tok)
            raw = RAW[:, q % 3 * 1024:q % 3 * 1024 + 1024]
            w = split_tok[q - 3][2:] if q >= 3 else None
            load_tok[q] = SP.dma(raw_ch[q % 3], lambda e: e.dma_start(raw, wall[q, :, :]), w)

        def u_get(*kind):
            j = at_unit[0]
            assert UNITS[j] == kind, (UNITS[j], kind)
            at_unit[0] += 1
            u_advance(j)
            return (j,) + split_tok[j]

        def u_done(j, tok):
            done_tok[j] = tok
            u_advance(at_unit[0] - 1)

        bg = []
        credit = [0.0]
        rate = [0.5]

        def tick(n=1.0):
            credit[0] += rate[0] * n
            while credit[0] >= 1.0 and bg:
                credit[0] -= 1.0
                step()
            if not bg:
                credit[0] = min(credit[0], 1.0)

        def step():
            try:
                next(bg[0])
            except StopIteration:
                bg.pop(0)

        def drain(upto=0):
            while len(bg) > upto:
                step()

        def gemm(psum, w, wt, rhs, rt, nk, free, first=True, last=True, k0=0, halves=2):
            hi, lo, th, tl = w
            n = 0
            tok = None
            for k in range(nk):
                for a, b, ta, tb in ((hi, 0, th, 0), (hi, 1, th, 1), (lo, 0, tl, 0)):
                    for h in range(halves):
                        st = first and n == 0
                        sp = last and k == nk - 1 and a is lo
                        tok = mm(psum[:, h * 512:h * 512 + 512], wt(a, k), rhs(b, k0 + k, h),
                                 st, sp, ta, rt(k0 + k)[tb], free)
                    n += 1
                tick()
            return tok

        def unit_k(a, k):
            return a[:, k * 128:(k + 1) * 128]

        hbt = [None] * 8

        def hb(part, k):
            o = part * 8 * T + k * T
            return HB[:, o:o + T]

        def hb_rhs(part, k, h):
            o = part * 8 * T + k * T + h * 512
            return HB[:, o:o + 512]

        def hb_tok(k):
            return hbt[k]

        def gemm_hb(*kind):
            j, *w = u_get(*kind)
            i, ps, free = G.take()
            tok = gemm(ps, w, unit_k, hb_rhs, hb_tok, 8, free)
            u_done(j, tok)
            return i, ps, tok

        def sums(acc, tacc):
            i, bank, free = S.take()
            for t in range(NT):
                tok = mm(bank[:, t:t + 1], acc[:, t * 128:(t + 1) * 128], ones[:, 0:1], True, True,
                         tacc, t_ones, free)
            return i, bank[:, 0:NT], tok

        def inv_root(o, i, div, *w):
            a = ts(o, i, 1.0 / div, EPS, ALU.mult, ALU.add, *w)
            return PO(lambda e: e.tensor_tensor(o, o, mhalf[:, 0:8], ALU.pow), a, t_mh)

        def spread(r, tr_, dg, *w):
            td = tt(dg[:, :].rearrange("p (c n) -> p c n", c=8), ident[:, :].unsqueeze(1).to_broadcast([128, 8, 128]),
                    r.unsqueeze(2).to_broadcast([128, 8, 128]), ALU.mult, tr_, t_ident, *w)
            i, ps, free = G.take()
            for h in range(2):
                tok = mm(ps[:, h * 512:h * 512 + 512], ones[:, :], dg[:, h * 512:h * 512 + 512], True, True,
                         td, t_ones, free)
            return i, ps, tok

        xr = [RES[:, k * T:(k + 1) * T] for k in range(8)]
        o = x0
        sq = [at(f"p0sq{i}", 1024, F32, o + i * K4) for i in range(2)]
        acc0 = at("p0acc", 1024, F32, o + 2 * K4)
        dg0 = at("p0dg", 1024, F32, o + 3 * K4)
        tm0 = [at(f"p0t{i}", 1024, F32, o + (4 + i) * K4) for i in range(2)]
        mraw = at("mraw", 8 * 256, F32, o + 6 * K4)
        mem_end = o + 6 * K4 + 3 * 8192
        mhi = at("mhi", 8 * 256, F32R, o + 6 * K4 + 8192)
        mlo = at("mlo", 8 * 256, F32R, o + 6 * K4 + 16384)
        macc = at("macc0", 256, F32, mem_end)
        msq = at("msq", 256, F32, mem_end + 1024)
        mdg = at("mdg", 256, F32, mem_end + 2048)
        mtm = at("mtm", 256, F32, mem_end + 3072)

        t_mem = SP.dma(chan("d_mem"), lambda e: e.dma_start(mraw[:, :], memT))
        x_ch = [chan(f"d_x{k}") for k in range(8)]
        t_x = [SP.dma(x_ch[k], lambda e, k=k: e.dma_start(xr[k], xT[:, k, :])) for k in range(8)]
        mst = at("mst", 448, F32, x0 + 13 * K4)
        t_mst = SP.dma(chan("d_mask"), lambda e: e.dma_start(mst[:, :], masks_d))
        for l in range(7):
            t_mask = DV(lambda e, l=l: e.tensor_copy(masks[:, l * 512:(l + 1) * 512].rearrange("p (c n) -> p c n", c=8),
                                                     mst[:, l * 64:(l + 1) * 64].unsqueeze(1).to_broadcast([128, 8, 64])),
                        t_mst)
        gupt = at("gupt", 512, F32, x0 + 67 * 1024 - 2048)
        t_gup = SP.dma(chan("d_gup"), lambda e: e.dma_start(gupt[0:16, :], gup))

        ta = None
        for k in range(8):
            m = mraw[:, k * 256:(k + 1) * 256]
            if k == 0:
                ta = act(macc[:, :], m, ACT.Square, t_mem)
            else:
                tq = act(msq[:, :], m, ACT.Square, ta)
                ta = tt(macc[:, :], macc[:, :], msq[:, :], ALU.add, tq, ta)
        si, bank, free = S.take()
        for t in range(2):
            tp = mm(bank[:, t:t + 1], macc[:, t * 128:(t + 1) * 128], ones[:, 0:1], True, True, ta, t_ones, free)
        mr = small[:, 8:10]
        t1 = ts(mr, bank[:, 0:2], 1.0 / D, EPS, ALU.mult, ALU.add, tp)
        S.free[si] = t1
        t2 = PO(lambda e: e.tensor_tensor(mr, mr, mhalf[:, 0:2], ALU.pow), t1, t_mh)
        td = tt(mdg[:, :].rearrange("p (c n) -> p c n", c=2), ident[:, :].unsqueeze(1).to_broadcast([128, 2, 128]),
                mr.unsqueeze(2).to_broadcast([128, 2, 128]), ALU.mult, t2, t_ident)
        si, bank, free = S.take()
        tR = mm(bank[:, 0:256], ones[:, :], mdg[:, :], True, True, td, free)
        mt = [None] * 8
        tl = None
        for k in range(8):
            m = mraw[:, k * 256:(k + 1) * 256]
            h_, l_ = mhi[:, k * 256:(k + 1) * 256], mlo[:, k * 256:(k + 1) * 256]
            t1 = stt(mtm[:, :], m, vcol("mem_nw", k), bank[:, 0:256], ALU.mult, ALU.mult, tR, t_vec, tl)
            th = copy(h_, mtm[:, :], t1)
            tl = tt(l_, mtm[:, :], h_.bitcast(F32), ALU.subtract, th)
            mt[k] = (th, tl)
        S.free[si] = tl

        ta = act(acc0[:, :], xr[0], ACT.Square, t_x[0])
        sqf = [None, None]
        for k in range(1, 8):
            q = act(sq[k % 2][:, :], xr[k], ACT.Square, t_x[k], sqf[k % 2])
            ta = tt(acc0[:, :], acc0[:, :], sq[k % 2][:, :], ALU.add, q, ta)
            sqf[k % 2] = ta
        si, ss, tp = sums(acc0, ta)
        xr_r = small[:, 16:24]
        tr_ = inv_root(xr_r, ss, D, tp)
        S.free[si] = tr_
        gi, R, tR = spread(xr_r, tr_, dg0)
        tf = [None, None]
        last_x = None
        for k in range(8):
            tm = tm0[k % 2]
            t1 = stt(tm[:, :], xr[k], vcol("norm_w", k), R[:, :], ALU.mult, ALU.mult, tR, t_vec, tf[k % 2])
            th = copy(hb(0, k), tm[:, :], t1)
            tl = tt(hb(1, k), tm[:, :], hb(0, k).bitcast(F32), ALU.subtract, t1, th)
            tf[k % 2] = tl
            hbt[k] = (th, tl)
            last_x = t1
        G.free[gi] = last_x

        o = x0
        KT_ = at("KT", 1024, F32, o + 0 * K4)
        MACC = at("MACC", 1024, F32, o + 1 * K4)
        MRAW = at("MODRAW", 2048, F32, o + 2 * K4)
        VB = [at(f"VB{i}", 2048, F32, o + (4 + 2 * i) * K4) for i in range(2)]
        ST = at("ST", 768, F32, o + 8 * K4)
        GLR = at("GLR", 1024, F32, o + 8 * K4 + 3072)
        o += 9 * K4 + 3072
        OSB = at("OSB", 2048, F32, o)
        OT = [at(f"OT{i}", 1024, F32, o + 8192 + i * K4) for i in range(2)]
        MK = at("MK", 1024, F32, o + 4 * K4)
        MV = at("MV", 1024, F32, o + 5 * K4)
        PP = at("PP", 512, F32, o + 6 * K4)
        PT = at("PT", 512, F32, o + 6 * K4 + 2048)
        sets = [[at(f"set{i}{n}", 1024, F32, res0 + (3 * i + a) * K4) for a, n in enumerate("qkg")] for i in range(2)]
        TB = at("TB", 1024, F32, res0 + 6 * K4)
        AB = at("AB", 1024, F32, res0 + 7 * K4)

        def m_rhs(part, k):
            return (mhi, mlo)[part][:, k * 256:(k + 1) * 256]

        t_mk, t_mv = [], []
        for h in range(4):
            j, hi, lo, th, tl = u_get("mk", h)
            gi, ps, free = G.take()
            for k in range(8):
                for n, (a, b) in enumerate(((hi, 0), (hi, 1), (lo, 0))):
                    tok = mm(ps[:, 0:256], unit_k(a, k), m_rhs(b, k), k == 0 and n == 0, k == 7 and n == 2,
                             th if a is hi else tl, mt[k], free)
            u_done(j, tok)
            G.free[gi] = copy(MK[:, h * 256:(h + 1) * 256], ps[:, 0:256], tok, last_x)
            t_mk.append(G.free[gi])
        gi, ps, free = G.take()
        for u in range(4):
            j, hi, lo, th, tl = u_get("mv", u)
            for kk in range(2):
                k = 2 * u + kk
                for m in range(2):
                    for n, (a, b) in enumerate(((0, hi), (1, hi), (0, lo))):
                        tok = mm(ps[:, m * 512:(m + 1) * 512],
                                 (mhi, mlo)[a][:, k * 256 + m * 128:k * 256 + m * 128 + 128],
                                 b[:, kk * 512:(kk + 1) * 512], k == 0 and n == 0, k == 7 and n == 2,
                                 th if b is hi else tl, mt[k], free)
            u_done(j, tok)
        t_mv = copy(MV[:, :], ps[:, :], tok, last_x)
        G.free[gi] = t_mv
        p0_done = [last_x, hbt[7][1], tok, t_mask]

        modcol = modv[:, 0:48]
        t_mod = [None] * 6
        sc = small[:, 24:32]
        t_sc = act(sc, vcols("c", 8), ACT.Silu, t_vec)
        mod_ch = [chan("d_mod0"), chan("d_mod1")]
        mod_free = [p0_done, p0_done]
        mod_n = [0]
        mod_tok = {}

        def mod_load():
            n = mod_n[0]
            if n < 48:
                s = n % 2
                dst = MRAW[:, s * 1024:(s + 1) * 1024]
                mod_tok[n] = SP.dma(mod_ch[s], lambda e: e.dma_start(dst, wmod[n, :, :]), mod_free[s])
                mod_n[0] += 1

        mod_st = {"acc": p0_done}

        def mod_step(n):
            c, k = n // 8, n % 8
            src = MRAW[:, n % 2 * 1024:(n % 2 + 1) * 1024]
            if k == 0:
                t = ts(MACC[:, :], src, sc[:, k:k + 1], None, ALU.mult, None, mod_tok[n], t_sc, mod_st["acc"])
            else:
                t = stt(MACC[:, :], src, sc[:, k:k + 1], MACC[:, :], ALU.mult, ALU.add, mod_tok[n], mod_st["acc"])
            mod_st["acc"] = t
            mod_free[n % 2] = t
            mod_load()
            if k == 7:
                si, bank, free = S.take()
                for f in range(8):
                    tp = mm(bank[:, f:f + 1], MACC[:, f * 128:(f + 1) * 128], ones[:, 0:1], True, True, t, free)
                tm = tt(modcol[:, c * 8:c * 8 + 8], bank[:, 0:8], vec[:, VOFF["b_mod"] + c * 8:VOFF["b_mod"] + c * 8 + 8],
                        ALU.add, tp)
                S.free[si] = tm
                mod_st["acc"] = tp
                t_mod[c] = tm

        mod_at = [0]

        def mods(n):
            while mod_at[0] < min(48, n):
                mod_step(mod_at[0])
                mod_at[0] += 1

        ot_ring = Ring(OT)
        ot_ch = [chan("d_ot0"), chan("d_ot1")]
        ot_out = [None] * 16
        st = {"A": p0_done, "T": p0_done, "KT": p0_done, "OSB": p0_done, "ST": [p0_done] * 3, "SS": None,
              "PP": [p0_done] * 2, "PT": [p0_done] * 2, "OT": None}
        ot_ring.free = [p0_done, p0_done]
        SS = small[:, 32:40]
        RS = small[:, 40:48]

        def finish(dv, nw, e0, t_ss, t_o):
            a = ts(RS, SS, 1.0 / dv, EPS, ALU.mult, ALU.add, t_ss, st["SS"])
            tr_ = PO(lambda e: e.tensor_tensor(RS, RS, mhalf[:, 0:8], ALU.pow), a, t_mh)
            yield
            tsc = []
            for c in range(8):
                ob = OSB[:, c * dv:(c + 1) * dv]
                tsc.append(ts(ob, ob, RS[:, c:c + 1], None, ALU.mult, None, tr_, t_o[c], t_ss))
            st["SS"] = tsc[-1]
            yield
            for f in range(dv // 128):
                oi, ot, ofree = ot_ring.take()
                for hf in range(2):
                    si, bank, free = S.take()
                    for i in range(4):
                        c = 4 * hf + i
                        tp = tr(bank[:, i * 128:(i + 1) * 128], OSB[:, c * dv + f * 128:c * dv + f * 128 + 128],
                                tsc[c], t_ident, free)
                    te = copy(ot[:, hf * 512:(hf + 1) * 512], bank[:, :], tp, ofree, t_vec, scale=nw(f))
                    S.free[si] = te
                    yield
                e = e0 + f
                ot_out[e] = SP.dma(ot_ch[oi], lambda g, e=e, ot=ot: g.dma_start(oscr[e, :, :], ot[:, :]), te)
                ot_ring.free[oi] = ot_out[e]
            st["OSB"] = tp

        def linear(s, tq, tk, tg, vb, v0, dv, tv, nw, e0, freed):
            q, k, g = sets[s]

            def ch(b, c):
                return b[:, c * 128:(c + 1) * 128]

            for hf in range(2):
                si, bank, free = S.take()
                for i in range(4):
                    c = 4 * hf + i
                    tp = mm(ch(bank, i), ch(k, c), ch(q, c), True, True, tq, tk, free)
                t_a = tt(AB[:, hf * 512:(hf + 1) * 512].rearrange("p (c n) -> p c n", c=4),
                         bank[:, :].rearrange("p (c n) -> p c n", c=4),
                         ident[:, :].unsqueeze(1).to_broadcast([128, 4, 128]), ALU.mult, tp, t_ident, st["A"])
                S.free[si] = t_a
                yield
            t_q = tt(q[:, :], q[:, :], g[:, :], ALU.mult, tp, tg, tq)
            t_k = tk
            tcur, toff, t_t = g[:, :], 0, tg
            yield
            for l in range(7):
                H = 1 << l
                si, bank, free = S.take()
                for c in range(8):
                    rhs = ch(q, c).rearrange("p (n t h) -> p n t h", t=2, h=H)[:, :, 1, :]
                    tp = mm(bank[:, c * 64:(c + 1) * 64], ch(k, c), rhs, True, True, t_q, t_k, free)
                tv2 = tcur.rearrange("p (n t) -> p n t", t=2)
                qv = q[:, :].rearrange("p (n t h) -> p n t h", t=2, h=H)[:, :, 1, :]
                kv = k[:, :].rearrange("p (n t h) -> p n t h", t=2, h=H)[:, :, 0, :]
                nb = 512 // H
                t_q = tt(qv, qv, tv2[:, :, 0:1].to_broadcast([128, nb, H]), ALU.mult, tp, t_q, t_t)
                t_k = tt(kv, kv, tv2[:, :, 1:2].to_broadcast([128, nb, H]), ALU.mult, tp, t_k, t_t)
                nxt = TB[:, toff:toff + nb]
                t_t = tt(nxt.unsqueeze(2), tv2[:, :, 0:1], tv2[:, :, 1:2], ALU.mult, t_t, st["T"])
                tcur, toff = nxt, toff + nb
                av = AB[:, :].rearrange("p (n t h) -> p n t h", t=2, h=H)[:, :, 1, :]
                mv = masks[:, l * 512:(l + 1) * 512].rearrange("p (n h) -> p n h", h=H)
                bv = bank[:, :].rearrange("p (n h) -> p n h", h=H)
                t_a = DV(lambda e, av=av, mv=mv, bv=bv: e.copy_predicated(av, mv, bv), tp, t_a, t_mask)
                S.free[si] = t_a
                yield
            dec = tcur
            for hf in range(2):
                si, bank, free = S.take()
                for i in range(4):
                    tp = tr(ch(bank, i), ch(k, 4 * hf + i), t_k, t_ident, free)
                t_kt = copy(KT_[:, hf * 512:(hf + 1) * 512], bank[:, :], tp, st["KT"])
                S.free[si] = t_kt
                yield
            t_s, s_old, t_o, t_ss = None, None, [], None
            for c in range(8):
                vc = vb[:, c * 256 + v0:c * 256 + v0 + dv]
                if c < 7:
                    oi, kvb, free = O.take()
                    tkv = mm(kvb[:, 0:dv], ch(KT_, c), vc, True, True, t_kt, tv, free)
                    new = ST[:, (c % 3) * 256:(c % 3) * 256 + dv]
                    if c == 0:
                        t_n = DV(lambda e, new=new, kvb=kvb: e.tensor_copy(new, kvb[:, 0:dv]), tkv, st["ST"][0])
                    else:
                        t_n = stt(new, s_old, dec[:, c:c + 1], kvb[:, 0:dv], ALU.mult, ALU.add, tkv, t_s, t_t,
                                  st["ST"][c % 3])
                    O.free[oi] = t_n
                oi, ob, free = O.take()
                tp = mm(ob[:, 0:dv], ch(AB, c), vc, True, c == 0, t_a, tv, free)
                if c:
                    tp = mm(ob[:, 0:dv], ch(q, c), s_old, False, True, t_s, t_q)
                    st["ST"][(c - 1) % 3] = [tp, t_n if c < 7 else None]
                if c < 7:
                    s_old, t_s = new, t_n
                os_ = OSB[:, c * dv:(c + 1) * dv]
                t_c = copy(os_, ob[:, 0:dv], tp, st["OSB"])
                t_ss = AC(lambda e, ob=ob, c=c: e.activation(ob[:, 256:256 + dv], ob[:, 0:dv], ACT.Square,
                                                             accum_out=SS[:, c:c + 1]), tp, st["SS"])
                t_o.append(t_c)
                O.free[oi] = t_ss
                yield
            st["A"], st["KT"], st["T"] = tp, tkv, [t_t, t_n]
            freed(tp)
            yield from finish(dv, nw, e0, t_ss, t_o)

        def cross(h, s, tq):
            q = sets[s][0]
            NM = small[:, 48:56]
            SE = small[:, 56:64]
            t_o = []
            for t in range(8):
                si, bank, free = S.take()
                tp = mm(bank[:, 0:256], q[:, t * 128:(t + 1) * 128], MK[:, h * 256:(h + 1) * 256], True, True,
                        tq, t_mk[h], free)
                nm, se, rs = NM[:, t:t + 1], SE[:, t:t + 1], RS[:, t:t + 1]
                t1 = DV(lambda e, nm=nm, bank=bank: e.tensor_reduce(nm, bank[:, 0:256], AXX, ALU.max), tp, st["SS"])
                t2 = ts(nm, nm, -SCALE, None, ALU.mult, None, t1)
                p = PP[:, t % 2 * 256:t % 2 * 256 + 256]
                pt = PT[:, t % 2 * 256:t % 2 * 256 + 256]
                te = AC(lambda e, p=p, bank=bank, nm=nm, se=se: e.activation(p, bank[:, 0:256], ACT.Exp, bias=nm,
                                                                          scale=SCALE, accum_out=se),
                        t2, st["PP"][t % 2], st["SS"])
                S.free[si] = te
                yield
                si, bank, free = S.take()
                for m in range(2):
                    tp = tr(bank[:, m * 128:(m + 1) * 128], p[:, m * 128:(m + 1) * 128], te, t_ident, free)
                st["PP"][t % 2] = tp
                tpt = copy(pt, bank[:, 0:256], tp, st["PT"][t % 2])
                S.free[si] = tpt
                yield
                oi, ob, free = O.take()
                for m in range(2):
                    tp = mm(ob[:, 0:128], pt[:, m * 128:(m + 1) * 128], MV[:, m * 512 + h * 128:m * 512 + h * 128 + 128],
                            m == 0, m == 1, tpt, t_mv, free)
                st["PT"][t % 2] = tp
                t3 = DV(lambda e, se=se: e.reciprocal(se, se), te)
                os_ = OSB[:, t * 128:(t + 1) * 128]
                t4 = copy(os_, ob[:, 0:128], tp, t3, st["OSB"], scale=se)
                O.free[oi] = t4
                t_ss = AC(lambda e, os_=os_, p=p, t=t: e.activation(p[:, 0:128], os_, ACT.Square,
                                                                   accum_out=SS[:, t:t + 1]), t4, st["PP"][t % 2], st["SS"])
                st["PP"][t % 2] = t_ss
                t_o.append(t4)
                yield
            set_free[s] = tp
            yield from finish(128, lambda f: vcol("x_nw"), 12 + h, t_ss, t_o)

        set_free = [p0_done, p0_done]
        v_free = [p0_done, p0_done]
        mod_load()
        mod_load()
        n_main = [0]

        def counted():
            n_main[0] += 1
            mods(n_main[0] * 48 // 20)

        gi, ps, tok = gemm_hb("glr")
        t_glr = copy(GLR[0:16, :], ps[0:16, :], tok, p0_done)
        G.free[gi] = t_glr

        def values(name, i, vslot):
            ja, *wa = u_get(name, i, 0)
            jb, *wb = u_get(name, i, 1)
            vb = VB[vslot]
            for hf in range(2):
                gi, ps, free = G.take()
                for tl_ in range(4):
                    t = 4 * hf + tl_
                    for k in range(8):
                        hi, lo, th, tl = wa if k < 4 else wb
                        for n, (a, b, tb) in enumerate(((0, hi, th), (1, hi, th), (0, lo, tl))):
                            tok = mm(ps[:, tl_ * 256:(tl_ + 1) * 256], hb(a, k)[:, t * 128:(t + 1) * 128],
                                     b[:, (k % 4) * 256:(k % 4 + 1) * 256], k == 0 and n == 0, k == 7 and n == 2,
                                     tb, hbt[k][a], free)
                        if k % 2:
                            tick()
                if hf:
                    u_done(ja, tok)
                    u_done(jb, tok)
                tv = copy(vb[:, hf * 1024:(hf + 1) * 1024], ps[:, :], tok, v_free[vslot])
                G.free[gi] = tv
            counted()
            return tv

        def wait_bg(n):
            drain(n)

        rate[0] = 0.75
        nset = 0
        for h in range(4):
            s = nset % 2
            nset += 1
            q, k, g = sets[s]
            gi, ps, tok = gemm_hb("gq", h)
            wait_bg(1)
            tq = copy(q[:, :], ps[:, :], tok, set_free[s], scale=SCALE)
            G.free[gi] = tq
            counted()
            gi, ps, free = G.take()
            for hf in range(2):
                tok = mm(ps[:, hf * 512:(hf + 1) * 512], gupt[0:16, h * 128:(h + 1) * 128],
                         GLR[0:16, hf * 512:(hf + 1) * 512], True, True, t_glr, t_gup, free)
            b = vcol("b_gate", h)
            t1 = act(g[:, :], ps[:, :], ACT.Abs, tok, set_free[s], bias=b)
            t1 = act(g[:, :], g[:, :], ACT.Exp, t1, scale=-1.0)
            t1 = act(g[:, :], g[:, :], ACT.Ln, t1, bias=1.0)
            t2 = ts(ps[:, :], ps[:, :], b, 0.0, ALU.add, ALU.min, t1)
            t3 = tt(g[:, :], ps[:, :], g[:, :], ALU.subtract, t2, t1)
            G.free[gi] = t3
            tg = act(g[:, :], g[:, :], ACT.Exp, t3, scale=1.0 / 16.0)
            gi, ps, tok = gemm_hb("gk", h)
            tk = copy(k[:, :], ps[:, :], tok, set_free[s])
            G.free[gi] = tk
            counted()
            tv = values("gv", h, h % 2)

            def freed(tok, s=s, v=h % 2):
                set_free[s] = tok
                v_free[v] = tok

            bg.append(linear(s, tq, tk, tg, VB[h % 2], 0, 256, tv, lambda f: vcol("gla_nw", f), 2 * h, freed))

        lbw = small[:, 64:80]
        lb_ = vcols("lb", 4)
        ex, pr, om, fl = (lbw[:, 4 * i:4 * i + 4] for i in range(4))
        t1 = tt(ex, lb_, lb_, ALU.subtract, t_vec)
        t1 = act(ex, ex, ACT.Exp, t1)
        t2 = DV(lambda e: e.reciprocal(pr, ex), t1)
        t2 = tt(pr, pr, ex, ALU.mult, t2)
        t2 = tt(ex, pr, pr, ALU.subtract, t2)
        t_fl = ts(fl, ex, FLOOR, None, ALU.max, None, t2)
        t_om = ts(om, ex, -1.0, 1.0, ALU.mult, ALU.add, t2)
        for pr_ in range(2):
            got = []
            for i in range(2):
                h = 2 * pr_ + i
                s = nset % 2
                nset += 1
                q, k, g = sets[s]
                gi, ps, tok = gemm_hb("hq", h)
                wait_bg(1 if i == 0 else 0)
                tq = copy(q[:, :], ps[:, :], tok, set_free[s])
                G.free[gi] = tq
                counted()
                gi, ps, tok = gemm_hb("hf", h)
                t1 = act(g[:, :], ps[:, :], ACT.Sigmoid, tok, set_free[s])
                t2 = act(k[:, :], ps[:, :], ACT.Sigmoid, tok, set_free[s], scale=-1.0)
                G.free[gi] = t2
                tg = ts(g[:, :], g[:, :], om[:, h:h + 1], fl[:, h:h + 1], ALU.mult, ALU.add, t1, t_om, t_fl)
                tk = ts(k[:, :], k[:, :], om[:, h:h + 1], None, ALU.mult, None, t2, t_om)
                got.append((s, tq, tk, tg))
                counted()
            tv = values("hi", pr_, pr_)
            for i in range(2):
                s, tq, tk, tg = got[i]

                def freed(tok, s=s, v=pr_, i=i):
                    set_free[s] = tok
                    if i:
                        v_free[v] = tok

                bg.append(linear(s, tq, tk, tg, VB[pr_], i * 128, 128, tv, lambda f: vcol("hgrn_nw"),
                                 8 + 2 * pr_ + i, freed))
        rate[0] = 1.6
        for h in range(4):
            s = nset % 2
            nset += 1
            gi, ps, tok = gemm_hb("xq", h)
            wait_bg(1)
            tq = copy(sets[s][0][:, :], ps[:, :], tok, set_free[s])
            G.free[gi] = tq
            counted()
            bg.append(cross(h, s, tq))
        mods(48)

        while len(bg) > 1:
            step()
        p2_done = [mod_st["acc"], st["A"], st["KT"], st["T"], v_free, t_glr]
        p2_done_all = [None]
        xo = x0
        GA = [at(f"GA{i}", 1024, F32, xo + i * K4) for i in range(2)]
        OI = [at(f"OI{i}", 1024, F32, xo + (2 + i) * K4) for i in range(2)]
        MX = [(at(f"MXH{i}", 1024, F32R, xo + (4 + 2 * i) * K4), at(f"MXL{i}", 1024, F32R, xo + (5 + 2 * i) * K4))
              for i in range(6)]
        ga_ring, oi_ring, mx_ring = Ring(GA), Ring(OI), Ring(MX)
        ga_free, oi_free = [p2_done] * 2, [p2_done] * 2
        mx_free = [p2_done] * 2 + [None] * 4
        oi_ch = [chan("d_oi0"), chan("d_oi1")]
        mx_tok = {}

        def mixed(e):
            if e == 2:
                drain()
                tail = [ot_out[12:16], st["OSB"], st["PP"], st["PT"], set_free]
                p2_done_all[0] = tail
                for i in range(2, 6):
                    mx_free[i] = [p2_done, tail]
            gi, ps, tok = gemm_hb("gate", e)
            s = e % 2
            t_oi = SP.dma(oi_ch[s], lambda g: g.dma_start(OI[s][:, :], oscr[e, :, :]), oi_free[s], ot_out[e])
            ga = GA[s]
            t1 = act(ga[:, :], ps[:, :], ACT.Silu, tok, ga_free[s])
            G.free[gi] = t1
            t2 = tt(ga[:, :], ga[:, :], OI[s][:, :], ALU.mult, t1, t_oi)
            oi_free[s] = t2
            m = e % 6
            hi, lo = MX[m]
            th = copy(hi[:, :], ga[:, :], t2, mx_free[m])
            tl = tt(lo[:, :], ga[:, :], hi[:, :].bitcast(F32), ALU.subtract, t2, th, mx_free[m])
            ga_free[s] = tl
            mx_tok[e] = (th, tl)

        x_tok = [None] * 8
        res = [RES[:, f * T:(f + 1) * T] for f in range(8)]

        def load_res():
            for f in range(8):
                x_tok[f] = SP.dma(x_ch[f], lambda e, f=f: e.dma_start(res[f], xT[:, f, :]), p2_done, p2_done_all[0])

        res_tok = [None] * 8
        SQ = [at("SQ0", 1024, F32, xo), at("SQ1", 1024, F32, xo + K4)]
        ACC1 = at("ACC1", 1024, F32, xo + 2 * K4)
        ACC2 = at("ACC2", 1024, F32, xo + 3 * K4)
        sqn = {"free": [None, None], "n": 0}

        def add_sq(acc, x, f, t_acc, *w, scale=None):
            kw = {} if scale is None else {"scale": scale}
            if f == 0:
                return act(acc[:, :], x, ACT.Square, *w, **kw)
            i = sqn["n"] % 2
            sqn["n"] += 1
            q = act(SQ[i][:, :], x, ACT.Square, *w, sqn["free"][i], **kw)
            t = tt(acc[:, :], acc[:, :], SQ[i][:, :], ALU.add, q, t_acc)
            sqn["free"][i] = t
            return t

        stat = {"a": None, "b": None}

        def out_group(g):
            for j2 in range(4):
                j, hi, lo, th, tl = u_get("wo", g, j2)
                for ff in range(2):
                    f = 2 * j2 + ff
                    gi, ps, free = G.take()

                    def wt(a, k, ff=ff):
                        return a[:, k * 256 + ff * 128:k * 256 + ff * 128 + 128]

                    def rhs(part, k, h):
                        return MX[(4 * g + k) % 6][part][:, h * 512:(h + 1) * 512]

                    tok = gemm(ps, (hi, lo, th, tl), wt, rhs, lambda k: mx_tok[4 * g + k], 4, free)
                    t = tt(res[f], res[f], ps[:, :], ALU.add, tok, x_tok[f], res_tok[f])
                    G.free[gi] = t
                    res_tok[f] = t
                    if g == NG - 1:
                        stat["a"] = add_sq(ACC1, res[f], f, stat["a"], t, ga_free, oi_free)
                        stat["b"] = add_sq(ACC2, res[f], f, stat["b"], t, ga_free, oi_free, scale=vcol("fin_w", f))
                u_done(j, tok)
            for k in range(4):
                mx_free[(4 * g + k) % 6] = tok
            return tok

        rate[0] = 1.5
        for e in range(6):
            mixed(e)
        load_res()
        out_group(0)
        for g in range(1, NG):
            for e in range(4 * g + 2, min(4 * g + 6, 16)):
                mixed(e)
            t_pe = out_group(g)
        hb_free = t_pe

        R1, R2, RR, W1 = small[:, 80:88], small[:, 88:96], small[:, 96:104], small[:, 104:112]
        DG = at("DG", 1024, F32, xo + 4 * K4)
        TM = [at(f"TM{i}", 1024, F32, xo + (5 + i) * K4) for i in range(2)]
        si, ss, tp = sums(ACC1, stat["a"])
        tr1 = inv_root(R1, ss, D, tp)
        S.free[si] = tr1
        si, ss2, tp2 = sums(ACC2, stat["b"])
        t1 = tt(RR, R1, R1, ALU.mult, tr1)
        t2 = tt(R2, RR, ss2, ALU.mult, t1, tp2)
        S.free[si] = t2
        tr2 = inv_root(R2, R2, D, t2)
        t_rr = tt(RR, R1, R2, ALU.mult, tr2, t2)
        A1 = small[:, 112:120]
        ta = ts(A1, modcol[:, 8:16], 1.0, None, ALU.add, None, t_mod[1])
        ta = tt(A1, A1, vcols("n1", 8), ALU.mult, ta)
        ta = tt(W1, A1, vcols("fin_w", 8), ALU.mult, ta)
        gi, R, tR = spread(RR, t_rr, DG, t_pe)
        tm_free = [t_pe, t_pe]

        def modulated(k, src, scol, shift, R, tR, *w):
            tm = TM[k % 2]
            t1 = stt(tm[:, :], src, scol, R[:, :], ALU.mult, ALU.mult, tR, tm_free[k % 2], *w)
            th = act(hb(0, k), tm[:, :], ACT.Identity, t1, hb_free, bias=shift)
            tl = stt(hb(1, k), tm[:, :], shift, hb(0, k).bitcast(F32), ALU.add, ALU.subtract, t1, th, hb_free)
            tm_free[k % 2] = tl
            hbt[k] = (th, tl)
            return t1

        for k in range(8):
            t1 = modulated(k, res[k], W1[:, k:k + 1], modcol[:, k:k + 1], R, tR, ta, t_mod[0], res_tok[k])
        G.free[gi] = t1
        gi, R, tR = spread(R1, tr1, DG, tR)
        for k in range(8):
            res_tok[k] = stt(res[k], res[k], vcol("fin_w", k), R[:, :], ALU.mult, ALU.mult, tR, t1)
        G.free[gi] = res_tok[7]
        p4 = [res_tok[7], hbt[7], tm_free, tR]

        CO = [at(f"CO{f}", 1024, F32, xo + f * K4) for f in range(8)]
        UP = [at(f"UP{i}", NSEG * SEGP, F32, xo + 8 * K4 + i * NSEG * SEGP * 4) for i in range(3)]
        po = xo + 8 * K4 + 3 * NSEG * SEGP * 4
        SG = at("SG", 1024, F32, po)
        PR = [at(f"PR{i}", 1024, F32, po + (1 + i) * K4) for i in range(2)]
        DGR = [at(f"DGR{i}", 128, F32, po + 3 * K4 + i * 512) for i in range(3)]

        def seg(b):
            return b[:, :].rearrange("p (s t) -> p s t", s=NSEG)

        up_ring = Ring(UP)
        for i in range(3):
            up_ring.free[i] = PO(lambda e, i=i: e.memset(UP[i][:, :], 0.0), p4)
        sg_free = p4
        co_tok = [None] * 8
        ON = {0: "pool", 7: "pe"}

        def tap(up, k):
            return seg(up)[:, :, k:k + SEG]

        def wcol(f, k):
            return vcol("w_dw", f * TAPS + k)

        def conv_dve(f, ui, up, tu):
            co, other = seg(CO[f]), seg(PR[1])
            w0 = conv_state["dve"]
            ta = DV(lambda e: e.tensor_scalar(co, tap(up, 0), wcol(f, 0), vcol("b_dw", f), ALU.mult, ALU.add), tu, p4)
            tb = DV(lambda e: e.tensor_scalar(other, tap(up, 1), wcol(f, 1), None, ALU.mult), tu, w0)
            for k in range(2, TAPS):
                dst = co if k % 2 == 0 else other
                t = stt(dst, tap(up, k), wcol(f, k), dst, ALU.mult, ALU.add, ta if k % 2 == 0 else tb)
                if k % 2 == 0:
                    ta = t
                else:
                    tb = t
                if k % 4 == 3:
                    yield
            up_ring.free[ui] = t
            co_tok[f] = tt(co, co, other, ALU.add, ta, tb)
            conv_state["dve"] = co_tok[f]

        def conv_pool(f, ui, up, tu):
            co, pr = seg(CO[f]), PR[0]
            t0 = act(co, tap(up, 0), ACT.Identity, tu, p4, scale=wcol(f, 0), bias=vcol("b_dw", f))
            t = t0
            for k in range(1, TAPS):
                tp_ = act(seg(pr), tap(up, k), ACT.Copy, tu, conv_state["pool"], scale=wcol(f, k))
                t = tt(co, co, seg(pr), ALU.add, tp_, t, q=PO)
                conv_state["pool"] = t
                yield
            up_ring.free[ui] = tp_
            co_tok[f] = t

        conv_state = {"dve": p4, "pool": p4}

        def conv_pe(f, ui, up, tu):
            gi, ps, free = G.take()
            dfree = [p4] * 3
            for k in range(TAPS):
                dgk = DGR[k % 3]
                td = act(dgk[:, :], ident[:, :], ACT.Copy, dfree[k % 3], scale=wcol(f, k))
                for h in range(2):
                    tok = mm(ps[:, h * 512:(h + 1) * 512], dgk[:, :], tap(up, k)[:, h * 8:(h + 1) * 8, :],
                             k == 0, k == TAPS - 1, td, tu, free)
                dfree[k % 3] = tok
                tick(2.0)
            up_ring.free[ui] = tok
            co_tok[f] = act(CO[f][:, :], ps[:, :], ACT.Identity, tok, p4, bias=vcol("b_dw", f))
            G.free[gi] = co_tok[f]

        bg_dve, bg_pool = [], []
        rate[0] = 1.0

        def both():
            while True:
                if not bg_dve and not bg_pool:
                    return
                for lst in (bg_dve, bg_pool):
                    if lst:
                        try:
                            next(lst[0])
                        except StopIteration:
                            lst.pop(0)
                yield

        for f in range(8):
            gi_a, ps_a, tok_a = gemm_hb("pa", f)
            gi_g, ps_g, tok_g = gemm_hb("pg", f)
            ui, up, ufree = up_ring.take()
            while ufree is None:
                step()
                ufree = up_ring.free[ui]
            t1 = act(SG[:, :], ps_g[:, :], ACT.Sigmoid, tok_g, sg_free, bias=vcol("b_pw1", 8 + f))
            G.free[gi_g] = t1
            tu = stt(seg(up)[:, :, PAD:PAD + SEG], ps_a[:, :].rearrange("p (s t) -> p s t", s=NSEG), vcol("b_pw1", f),
                     seg(SG), ALU.add, ALU.mult, tok_a, t1, ufree)
            up_ring.free[ui] = None
            G.free[gi_a] = tu
            sg_free = tu
            where = ON.get(f, "dve")
            if where == "pe":
                conv_pe(f, ui, up, tu)
            elif where == "pool":
                bg_pool.append(conv_pool(f, ui, up, tu))
            else:
                bg_dve.append(conv_dve(f, ui, up, tu))
            if not bg:
                bg.append(both())
        drain()
        hb_free = [tok_g, co_tok[7]]

        DG2, SQ2 = UP[0], [PR[0], PR[1]]
        MU, RV = small[:, 120:128], small[:, 128:136]
        ACCM = at("ACCM", 1024, F32, xo + 8 * K4)
        ACCV = at("ACCV", 1024, F32, xo + 9 * K4)
        DGM = at("DGM", 1024, F32, xo + 10 * K4)
        YT = [at(f"YT{i}", 1024, F32, xo + (11 + i) * K4) for i in range(2)]
        ZT = [at(f"ZT{i}", 1024, F32, xo + (13 + i) * K4) for i in range(2)]
        c_all = co_tok
        order = [1, 2, 3, 4, 5, 6, 0, 7]
        ta = tt(ACCM[:, :], CO[order[0]][:, :], CO[order[1]][:, :], ALU.add, c_all)
        for f in order[2:]:
            ta = tt(ACCM[:, :], ACCM[:, :], CO[f][:, :], ALU.add, ta)
        si, ss, tp = sums(ACCM, ta)
        t1 = ts(MU, ss, 1.0 / D, None, ALU.mult, None, tp)
        S.free[si] = t1
        gi, R, tR = spread(MU, t1, DGM, c_all)
        tv_ = None
        yfree = [c_all, c_all]
        for f in range(8):
            co_tok[f] = tt(CO[f][:, :], CO[f][:, :], R[:, :], ALU.subtract, tR, ta)
            if f == 0:
                tv_ = act(ACCV[:, :], CO[f][:, :], ACT.Square, co_tok[f])
            else:
                y = YT[f % 2]
                q = act(y[:, :], CO[f][:, :], ACT.Square, co_tok[f], yfree[f % 2])
                tv_ = tt(ACCV[:, :], ACCV[:, :], y[:, :], ALU.add, q, tv_)
                yfree[f % 2] = tv_
        G.free[gi] = co_tok[7]
        si, ss, tp = sums(ACCV, tv_)
        tr_ = inv_root(RV, ss, D, tp)
        S.free[si] = tr_
        gi, R, tR = spread(RV, tr_, DGM, tR)
        zfree = [c_all, c_all]
        for f in range(8):
            y, z = YT[f % 2], ZT[f % 2]
            t1 = tt(y[:, :], CO[f][:, :], R[:, :], ALU.mult, tR, yfree[f % 2])
            t2 = act(z[:, :], y[:, :], ACT.Silu, t1, zfree[f % 2], scale=vcol("ln_g", f), bias=vcol("ln_b", f))
            yfree[f % 2] = t2
            th = copy(hb(0, f), z[:, :], t2, hb_free)
            tl = tt(hb(1, f), z[:, :], hb(0, f).bitcast(F32), ALU.subtract, th, hb_free)
            zfree[f % 2] = tl
            hbt[f] = (th, tl)
        G.free[gi] = t1
        p5 = [hbt[7], t1]

        GBV = small[:, 136:144]
        tgb = tt(GBV, modcol[:, 16:24], vcols("b_pw2", 8), ALU.mult, t_mod[2])
        ACC3 = at("ACC3", 1024, F32, xo)
        SQ = [at("SQ2", 1024, F32, xo + K4), at("SQ3", 1024, F32, xo + 2 * K4)]
        sqn["free"] = [p5, p5]
        EV = [at(f"EV{i}", 1024, F32, xo + (3 + i) * K4) for i in range(2)]
        ev_free = [p5, p5]
        t_a = None
        for f in range(8):
            gi, ps, tok = gemm_hb("pw2", f)
            ev = EV[f % 2]
            t1 = act(ev[:, :], ps[:, :], ACT.Identity, tok, ev_free[f % 2], tgb, scale=modcol[:, 16 + f:17 + f],
                     bias=GBV[:, f:f + 1])
            G.free[gi] = t1
            res_tok[f] = tt(res[f], res[f], ev[:, :], ALU.add, t1, res_tok[f])
            ev_free[f % 2] = res_tok[f]
            t_a = add_sq(ACC3, res[f], f, t_a, res_tok[f], p5)
        hb_free = tok
        R3, A2 = small[:, 144:152], small[:, 152:160]
        ta = ts(A2, modcol[:, 32:40], 1.0, None, ALU.add, None, t_mod[4])
        ta = tt(A2, A2, vcols("n2", 8), ALU.mult, ta)
        DG = at("DG3", 1024, F32, xo + 5 * K4)
        TM = [at(f"TN{i}", 1024, F32, xo + (6 + i) * K4) for i in range(2)]
        tm_free = [p5, p5]
        si, ss, tp = sums(ACC3, t_a)
        tr_ = inv_root(R3, ss, D, tp)
        S.free[si] = tr_
        gi, R, tR = spread(R3, tr_, DG, p5)
        for k in range(8):
            t1 = modulated(k, res[k], A2[:, k:k + 1], modcol[:, 24 + k:25 + k], R, tR, ta, t_mod[3], res_tok[k])
        G.free[gi] = t1
        p6 = [t1, hbt[7], tR, res_tok]

        NH = 2 * GT
        HID = [(at(f"HIDH{i}", 1024, F32R, xo + (2 * i) * K4), at(f"HIDL{i}", 1024, F32R, xo + (2 * i + 1) * K4))
               for i in range(NH)]
        hid_free = [p6] * NH
        hid_tok = {}
        RL = at("RL", 512, F32, xo + 2 * NH * K4)
        HT = [at(f"HT{i}", 512, F32, res0 - 0, ) for i in range(0)]
        rl_free = p6

        def hidden(i):
            nonlocal rl_free
            gi, ps, tok = gemm_hb("w1", i)
            s = i % NH
            hi, lo = HID[s]
            ths, tls = [], []
            for h in range(2):
                cs = slice(h * 512, (h + 1) * 512)
                t1 = act(RL[:, :], ps[:, cs], ACT.Relu, tok, rl_free)
                t2 = stt(ps[:, cs], ps[:, cs], 0.0, RL[:, :], ALU.max, ALU.mult, t1)
                th = copy(hi[:, cs], ps[:, cs], t2, hid_free[s])
                tl = tt(lo[:, cs], ps[:, cs], hi[:, cs].bitcast(F32), ALU.subtract, th, t2, hid_free[s])
                rl_free = t2
                ths.append(th)
                tls.append(tl)
            G.free[gi] = tls
            hid_tok[i] = (ths, tls)
            return tok

        hb_f = [at(f"FIN{i}", 1024, F32, hb0 + i * K4) for i in range(8)]
        SQ = [hb_f[0], hb_f[1]]
        ACC4 = hb_f[2]
        t_a = None

        def project(g):
            nonlocal t_a
            for j2 in range(4):
                j, hi, lo, th, tl = u_get("w2", g, j2)
                for ff in range(2):
                    f = 2 * j2 + ff
                    gi, ps, free = G.take()

                    def wt(a, k, ff=ff):
                        return a[:, k * 256 + ff * 128:k * 256 + ff * 128 + 128]

                    def rhs(part, k, h):
                        return HID[(GT * g + k) % NH][part][:, h * 512:(h + 1) * 512]

                    tok = gemm(ps, (hi, lo, th, tl), wt, rhs, lambda k: hid_tok[GT * g + k], GT, free)
                    t = stt(res[f], ps[:, :], modcol[:, 40 + f:41 + f], res[f], ALU.mult, ALU.add, tok, t_mod[5],
                            res_tok[f], p6)
                    G.free[gi] = t
                    res_tok[f] = t
                    if g == HG - 1:
                        t_a = add_sq(ACC4, res[f], f, t_a, t, hb_free)
                u_done(j, tok)
            for k in range(GT):
                hid_free[(GT * g + k) % NH] = tok

        for i in range(GT):
            t_w1 = hidden(i)
        for g in range(HG):
            if g + 1 < HG:
                for i in range(GT):
                    t_w1 = hidden((g + 1) * GT + i)
            else:
                hb_free = t_w1
                sqn["free"] = [t_w1, t_w1]
            project(g)

        R4 = small[:, 160:168]
        si, ss, tp = sums(ACC4, t_a)
        tr_ = inv_root(R4, ss, D, tp)
        gi, R, tR = spread(R4, tr_, hb_f[3], t_w1)
        outs = []
        o_ch = [chan(f"d_out{i}") for i in range(8)]
        for k in range(8):
            t1 = stt(res[k], res[k], vcol("fin_g", k), R[:, :], ALU.mult, ALU.mult, tR, res_tok[k], t_a)
            outs.append(SP.dma(o_ch[k], lambda e, k=k: e.dma_start(out[k * 128:(k + 1) * 128, :], res[k]), t1))

        for q in (PE, AC, DV, PO, SP):
            q.number()
        block = es.enter_context(nc.Block())

        @block.tensor
        def _(eng):
            PE.emit(eng)

        @block.scalar
        def _(eng):
            AC.emit(eng)

        @block.vector
        def _(eng):
            DV.emit(eng)

        @block.gpsimd
        def _(eng):
            PO.emit(eng)

        @block.sync
        def _(eng):
            SP.emit(eng)
            for w in ot_out + outs:
                eng.wait_ge(w.sem, w.count)


def lay_out(inputs):
    f = {n: np.asarray(a) for n, a in inputs.items()}
    w_in, w_out = f["w_in"][0], f["w_out"][0]
    kv, pw1, pw2 = f["w_mem_kv"][0], f["conv_w_pw1_2"][0], f["conv_w_pw2_2"][0]
    w1, w2 = f["mlp_w1_2"][0], f["mlp_w2_2"][0]
    OFF = {}
    at = 0
    for n, c in (("gq", 512), ("gk", 512), ("gv", 1024), ("glr", 16), ("hq", 512), ("hf", 512), ("hi", 512),
                 ("xq", 512), ("gate", 2048)):
        OFF[n] = at
        at += c

    def cols(w, c0, n, k0=0, nk=8):
        return w[k0 * 128:(k0 + nk) * 128, c0:c0 + n].reshape(nk, 128, n).transpose(1, 0, 2)

    wall = np.zeros((len(UNITS), 128, 1024), np.float32)
    for i, u in enumerate(UNITS):
        n = u[0]
        if n == "mk":
            t = cols(kv, u[1] * 128, 128)
        elif n == "mv":
            t = cols(kv, 512, 512, 2 * u[1], 2)
        elif n == "glr":
            wall[i].reshape(128, 8, 128)[:, :, 0:16] = cols(w_in, OFF["glr"], 16)
            continue
        elif n in ("gv", "hi"):
            t = cols(w_in, OFF[n] + u[1] * 256, 256, 4 * u[2], 4)
        elif n in OFF:
            t = cols(w_in, OFF[n] + u[1] * 128, 128)
        elif n == "wo":
            t = cols(w_out, u[2] * 256, 256, 4 * u[1], 4)
        elif n == "pa":
            t = cols(pw1, u[1] * 128, 128)
        elif n == "pg":
            t = cols(pw1, 1024 + u[1] * 128, 128)
        elif n == "pw2":
            t = cols(pw2, u[1] * 128, 128)
        elif n == "w1":
            t = cols(w1, u[1] * 128, 128)
        elif n == "w2":
            t = cols(w2, u[2] * 256, 256, GT * u[1], GT)
        wall[i].reshape(t.shape)[...] = t
    wm = f["w_mod_2"][0]
    wmod = np.ascontiguousarray(wm.reshape(8, 128, 6, 1024).transpose(2, 0, 1, 3)).reshape(48, 128, 1024)

    def col(a):
        return a.reshape(-1, 128).T

    dw = f["conv_w_dw_2"][0].T.reshape(8, 128, TAPS).transpose(1, 0, 2).reshape(128, 8 * TAPS)
    parts = {"norm_w": f["norm_w"], "b_gate": f["gla_b_gate"], "gla_nw": f["gla_norm_w"], "lb": f["hgrn_lower_bounds"],
             "hgrn_nw": f["hgrn_norm_w"], "mem_nw": f["mem_norm_w"], "x_nw": f["xattn_norm_w"],
             "fin_w": f["final_norm_w"], "c": f["c_2"], "b_mod": f["b_mod_2"], "n1": f["norm1_g_2"],
             "n2": f["norm2_g_2"], "fin_g": f["final_g_2"], "b_pw1": f["conv_b_pw1_2"], "b_dw": f["conv_b_dw_2"],
             "ln_g": f["conv_ln_g_2"], "ln_b": f["conv_ln_b_2"], "b_pw2": f["conv_b_pw2_2"]}
    vecs = np.concatenate([dw if n == "w_dw" else col(parts[n]) for n, _ in VECS], axis=1)
    xT = f["x"][0].T.reshape(8, 128, T).transpose(1, 0, 2)
    memT = f["mem"][0].T.reshape(8, 128, 256).transpose(1, 0, 2).reshape(128, 2048)
    ident = np.eye(128, dtype=np.float32)
    masks = np.zeros((128, 7, 64), np.float32)
    for l in range(7):
        H = 1 << l
        for b in range(64 // H):
            masks[b * 2 * H:b * 2 * H + H, l, b * H:(b + 1) * H] = 1
    masks = masks.reshape(128, 448)
    arrays = {"wall": wall, "wmod": wmod, "xT": xT, "memT": memT, "vecs": vecs, "gup": f["gla_w_gate_up"][0],
              "ident": ident, "masks": masks}
    return {n: np.ascontiguousarray(a) for n, a in arrays.items()}


def kernel(**inputs):
    import concourse.bacc as bacc
    from concourse.bass_utils import run_bass_kernel_spmd

    nc = bacc.Bacc("TRN2", target_bir_lowering=False, num_devices=1)
    arrays = lay_out(inputs)
    aps = [nc.dram_tensor(n, a.shape, mybir.dt.from_np(a.dtype), kind="ExternalInput").ap() for n, a in arrays.items()]
    out = nc.dram_tensor("outT", (D, T), F32, kind="ExternalOutput").ap()
    oscr = nc.dram_tensor("oscr", (16, 128, T), F32, kind="Internal").ap()
    build_program(nc, *aps, out, oscr)
    r = run_bass_kernel_spmd(nc, [arrays], core_ids=[0])
    return np.ascontiguousarray(r.results[0]["outT"].T)[None]
```

```python
from contextlib import ExitStack

import numpy as np
import concourse.bass as bass
from concourse import mybir

F32 = mybir.dt.float32
F32R = mybir.dt.float32r
U8 = mybir.dt.uint8
ALU = mybir.AluOpType
ACT = mybir.ActivationFunctionType
AXX = mybir.AxisListType.X

T = 1024
D = 1024
NT = T // 128
KT = D // 128
EPS = 1e-6
SCALE = 128.0 ** -0.5
FLOOR = 1e-30
SEG = 64
NSEG = T // SEG
TAPS = 31
PAD = TAPS // 2
SEGP = SEG + 2 * PAD
NG = 4
GT = 4
HG = 8
NW = 4
RATE = [0.9, 1.1, 2.0, 1.5, 0.85]
WAIT = [3, 9, 3]
CONV = ["dve", "pool", "dve", "dve", "pool", "dve", "dve", "pe"]
LN_AT = 14
AHEAD = 2.5

VECS = [("norm_w", 8), ("b_gate", 4), ("gla_nw", 2), ("lb", 4), ("hgrn_nw", 1), ("mem_nw", 8), ("x_nw", 1),
        ("fin_w", 8), ("c", 8), ("b_mod", 48), ("n1", 8), ("n2", 8), ("fin_g", 8), ("b_pw1", 16),
        ("w_dw", 8 * TAPS), ("b_dw", 8), ("ln_g", 8), ("ln_b", 8), ("b_pw2", 8)]
VOFF, _o = {}, 0
for _n, _c in VECS:
    VOFF[_n] = _o
    _o += _c
NV = _o


def unit_plan():
    plan = [("glr",)]
    for h in range(4):
        plan += [("gq", h), ("gk", h), ("gv", h, 0), ("gv", h, 1)]
        if h == 0:
            plan += [("mk", i) for i in range(4)] + [("mv", i) for i in range(4)]
    for p in range(2):
        for h in (2 * p, 2 * p + 1):
            plan += [("hq", h), ("hf", h)]
        plan += [("hi", p, 0), ("hi", p, 1)]
    plan += [("xq", h) for h in range(4)]
    plan += [("gate", e) for e in range(5)]
    for g in range(NG):
        plan += [("wo", g, j) for j in range(4)]
        plan += [("gate", e) for e in range(4 * g + 5, min(4 * g + 9, 16))]
    for f in range(8):
        plan += [("pa", f), ("pg", f)]
    plan += [("pw2", f) for f in range(8)]
    plan += [("w1", i) for i in range(GT)]
    for g in range(HG):
        if g + 1 < HG:
            plan += [("w1", (g + 1) * GT + i) for i in range(GT)]
        plan += [("w2", g, j) for j in range(4)]
    return plan


UNITS = unit_plan()


class Op:
    def __init__(self, q, fn, waits):
        self.q, self.fn, self.waits, self.needed, self.count = q, fn, waits, False, 0


class Dma:
    def __init__(self, sem, count):
        self.sem, self.count = sem, count


def flat(ws):
    for w in ws:
        if w is None:
            continue
        if isinstance(w, (list, tuple)):
            yield from flat(w)
        else:
            yield w


class Queue:

    def __init__(self, sem):
        self.sem, self.ops = sem, []

    def __call__(self, fn, *waits):
        ws = list(flat(waits))
        for w in ws:
            if isinstance(w, Op):
                w.needed = True
        op = Op(self, fn, ws)
        self.ops.append((op, None))
        return op

    def dma(self, chan, fn, *waits):
        ws = list(flat(waits))
        for w in ws:
            if isinstance(w, Op):
                w.needed = True
        op = Op(self, fn, ws)
        chan.count += 16
        self.ops.append((op, chan.sem))
        return Dma(chan.sem, chan.count)

    def number(self):
        n = 0
        for op, sem in self.ops:
            if sem is None and op.needed:
                n += 1
            op.count = n

    def emit(self, eng):
        seen = {}
        for op, dsem in self.ops:
            for w in op.waits:
                sem = w.sem if isinstance(w, Dma) else w.q.sem
                if seen.get(id(sem), 0) < w.count:
                    eng.wait_ge(sem, w.count)
                    seen[id(sem)] = w.count
            ins = op.fn(eng)
            if dsem is not None:
                ins.then_inc(dsem, 16)
            elif op.needed:
                ins.then_inc(self.sem, 1)


class Chan:
    def __init__(self, sem):
        self.sem, self.count = sem, 0


class Ring:

    def __init__(self, items):
        self.items, self.n, self.free = items, 0, [None] * len(items)

    def take(self):
        i = self.n % len(self.items)
        self.n += 1
        return i, self.items[i], self.free[i]


def build_program(nc, wall, wmod, xT, memT, vecs, gup, ident_d, masks_d, out, oscr):
    es = ExitStack()
    with es:
        size = {F32: 4, F32R: 4, U8: 1}
        base = [16512]
        END = 229344

        def at(name, cols, dt, off):
            assert off + cols * size[dt] <= END, (name, off + cols * size[dt] - END)
            return nc.alloc_sbuf_tensor_at(name, [128, cols], dt, offset=off)

        def take(name, cols, dt=F32):
            o = base[0]
            base[0] += (cols * size[dt] + 31) // 32 * 32
            return at(name, cols, dt, o)

        hb0 = base[0]
        HB = take("HB", 2 * 8 * T, F32R)
        WH = take("WH", NW * 1024, F32R)
        wl0 = base[0]
        WL = take("WL", NW * 1024, F32R)
        RAW = at("RAW", NW * 1024, F32, wl0)
        ident = take("ident", 128)
        ones = take("ones", 128)
        masks = take("masks", 7 * 256, U8)
        vec = take("vec", NV)
        small = take("small", 176)
        modv = take("modv", 48)
        res0 = base[0]
        RES = take("RES", 8 * T)
        x0 = base[0]
        K4 = 4096

        BANKS = [es.enter_context(nc.psum_tensor(f"B{i}", [128, 512], F32))[:, :] for i in range(8)]

        def sem(name):
            return es.enter_context(nc.semaphore(name))

        PE, AC, DV, PO, SP = (Queue(sem(f"s_{n}")) for n in ("pe", "act", "dve", "pool", "sp"))
        G, S, O = Ring(BANKS[0:3]), Ring(BANKS[3:6]), Ring(BANKS[6:8])

        def chan(name):
            return Chan(sem(name))

        def vcol(name, i=0):
            o = VOFF[name] + i
            return vec[:, o:o + 1]

        def vcols(name, n):
            o = VOFF[name]
            return vec[:, o:o + n]

        def copy(o, i, *w, scale=None):
            if scale is None:
                return AC(lambda e: e.activation(o, i, ACT.Copy), *w)
            return AC(lambda e: e.activation(o, i, ACT.Copy, scale=scale), *w)

        def act(o, i, f, *w, **kw):
            return AC(lambda e: e.activation(o, i, f, **kw), *w)

        def tt(o, a, b, op, *w, q=None):
            return (q or DV)(lambda e: e.tensor_tensor(o, a, b, op), *w)

        def ts(o, a, s1, s2, op0, op1, *w, q=None):
            if s2 is None:
                return (q or DV)(lambda e: e.tensor_scalar(o, a, s1, None, op0), *w)
            return (q or DV)(lambda e: e.tensor_scalar(o, a, s1, s2, op0, op1), *w)

        def stt(o, a, s, b, op0, op1, *w):
            return DV(lambda e: e.scalar_tensor_tensor(out=o, in0=a, scalar=s, in1=b, op0=op0, op1=op1), *w)

        def mm(o, l, r, st, sp, *w, skip=False):
            return PE(lambda e: e.matmul(o, l, r, start=st, stop=sp, skip_group_check=skip), *w)

        def tr(o, i, *w):
            return PE(lambda e: e.transpose(o, i, ident[:, :]), *w)

        t_ident = SP.dma(chan("d_ident"), lambda e: e.dma_start(ident[:, :], ident_d))
        t_vec = SP.dma(chan("d_vec"), lambda e: e.dma_start(vec[:, :], vecs))
        t_ones = PO(lambda e: e.memset(ones[:, :], 1.0))
        mhalf = small[:, 0:8]
        t_mh = PO(lambda e: e.memset(mhalf, -0.5))

        raw_ch = [chan(f"d_raw{i}") for i in range(NW)]
        n_units = len(UNITS)
        load_tok, split_tok, done_tok = {}, {}, {}
        hi_by = [AC]
        at_unit = [0]

        def u_split():
            q = len(split_tok)
            while len(load_tok) <= q:
                u_load()
            s = slice(q % NW * 1024, q % NW * 1024 + 1024)
            raw, hi, lo = RAW[:, s], WH[:, s], WL[:, s]
            if hi_by[0] is AC:
                th = copy(hi, raw, load_tok[q], done_tok.get(q - NW))
            else:
                th = ts(hi, raw, 1.0, 0.0, ALU.mult, ALU.add, load_tok[q], done_tok.get(q - NW), q=PO)
            tl = tt(lo, raw, hi.bitcast(F32), ALU.subtract, load_tok[q], th, q=PO)
            split_tok[q] = (hi, lo, th, tl)
            now["pool"] += 2.3

        def u_advance(j):
            while len(load_tok) < min(n_units, j + NW) and (len(load_tok) < NW or len(load_tok) - NW in done_tok):
                u_load()
            while len(split_tok) < min(n_units, j + 3, len(load_tok)):
                u_split()

        def u_load():
            q = len(load_tok)
            raw = RAW[:, q % NW * 1024:q % NW * 1024 + 1024]
            load_tok[q] = SP.dma(raw_ch[q % NW], lambda e: e.dma_start(raw, wall[q, :, :]), done_tok.get(q - NW))

        def u_get(*kind):
            j = at_unit[0]
            assert UNITS[j] == kind, (UNITS[j], kind)
            at_unit[0] += 1
            u_advance(j)
            return (j,) + split_tok[j]

        def u_done(j, tok):
            done_tok[j] = tok
            u_advance(at_unit[0] - 1)

        bg, bg2 = [], []
        credit = [0.0]
        rate = [0.5]
        turn = [0]

        def tick(us):
            credit[0] += rate[0] * us
            while credit[0] >= 1.0 and (bg or bg2):
                credit[0] -= 1.0
                step()
            if not (bg or bg2):
                credit[0] = min(credit[0], 1.0)
            now["pe"] += us
            for lane in lanes:
                while lanes[lane] and now[lane] < now["pe"] + AHEAD:
                    lane_step(lane)

        lanes = {"dve": [], "pool": []}
        now = {"pe": 0.0, "dve": 0.0, "pool": 0.0}
        COST = {"dve": 1.2, "pool": 2.35}

        def lane_add(lane, work):
            if not lanes[lane]:
                now[lane] = max(now[lane], now["pe"])
            lanes[lane].append(work)

        def lane_step(lane):
            now[lane] += COST[lane]
            step_in(lanes[lane])

        def lanes_step():
            lane = min((x for x in lanes if lanes[x]), key=lambda x: now[x])
            lane_step(lane)

        def step():
            turn[0] += 1
            lane = bg2 if (bg2 and turn[0] % 2) or not bg else bg
            step_in(lane)

        def step_in(lane):
            try:
                next(lane[0])
            except StopIteration:
                lane.pop(0)

        def drain(upto=0):
            while len(bg) > upto:
                step()
            while bg2 and not upto:
                step_in(bg2)

        PASS = 0.2133

        def gemm(outs, w, wt, rhs, rt, nk):
            hi, lo, th, tl = w
            toks = {}
            for k in range(nk):
                for n, (a, b, ta) in enumerate(((hi, 0, th), (hi, 1, th), (lo, 0, tl))):
                    for h, ps, free in outs:
                        toks[h] = mm(ps, wt(a, k), rhs(b, k, h), k == 0 and n == 0, k == nk - 1 and n == 2,
                                     ta, rt(b, k, h), free)
                tick(3 * PASS * len(outs))
            return toks

        def unit_k(a, k):
            return a[:, k * 128:(k + 1) * 128]

        hbt = {}

        def hb(part, k, h=None):
            o = part * 8 * T + k * T
            return HB[:, o:o + T] if h is None else HB[:, o + h * 512:o + h * 512 + 512]

        def hb_tok(part, k, h):
            return hbt[k, h][part]

        def gemm_units(ws, outs, wt, rhs, rt, nk):
            toks = [None] * len(ws)
            for k in range(nk):
                for u, ((hi, lo, th, tl), (h, ps, free)) in enumerate(zip(ws, outs)):
                    for n, (a, b, ta) in enumerate(((hi, 0, th), (hi, 1, th), (lo, 0, tl))):
                        toks[u] = mm(ps, wt(a, k), rhs(b, k, h), k == 0 and n == 0, k == nk - 1 and n == 2,
                                     ta, rt(b, k, h), free)
                    tick(3 * PASS)
            return toks

        def project(kind, evac, before=None):
            j, *w = u_get(*kind)
            held = []
            for h in range(2):
                i, bank, free = G.take()
                tok = gemm([(h, bank, free)], w, unit_k, hb, hb_tok, 8)[h]
                if before is None:
                    G.free[i] = evac(h, bank, tok)
                else:
                    held.append((h, bank, tok, i))
            u_done(j, tok)
            if before is not None:
                before()
                for h, bank, tok, i in held:
                    G.free[i] = evac(h, bank, tok)
            return tok

        def cut(x, h):
            return x[:, h * 512:(h + 1) * 512]

        def one_unit(kind, tiles, rhs, rt, nk, evac):
            j, *w = u_get(*kind)
            for f, wt in tiles:
                got = [(h,) + B.take() for h in range(2)]
                toks = gemm([(h, bank, free) for h, i, bank, free in got], w, wt, rhs, rt, nk)
                if (f, wt) == tiles[-1]:
                    u_done(j, toks[1])
                for h, i, bank, free in got:
                    B.free[i] = evac(f, h, bank, toks[h])
            return toks[1]

        def by_halves(units, rhs, rt, nk, evac, between=None, outer=False):
            got = [u_get(*kind) for kind, _ in units]
            for h in range(2):
                if outer:
                    bs = [B.take() for _ in got]
                    toks = gemm_units([w for j, *w in got], [(h, bank, free) for i, bank, free in bs], unit_k, rhs, rt, nk)
                    for (j, *w), (kind, tiles), (i, bank, free), tok in zip(got, units, bs, toks):
                        B.free[i] = evac(tiles[0][0], h, bank, tok)
                        if h:
                            u_done(j, tok)
                else:
                    for (j, *w), (kind, tiles) in zip(got, units):
                        for f, wt in tiles:
                            i, bank, free = B.take()
                            tok = gemm([(h, bank, free)], w, wt, rhs, rt, nk)[h]
                            B.free[i] = evac(f, h, bank, tok)
                        if h:
                            u_done(j, tok)
                if h == 0 and between:
                    between()
            return tok

        def sums(acc, tacc, tiles=range(NT), into=None, first=True, last=True):
            i, bank, free = into or S.take()
            for t in tiles:
                tok = mm(bank[:, t:t + 1], acc[:, t * 128:(t + 1) * 128], ones[:, 0:1],
                         first and (into is None or t == tiles[0]), last, tacc, t_ones, free, skip=True)
            return i, bank[:, tiles[0]:tiles[-1] + 1], tok

        def inv_root(o, i, div, *w):
            n = o.shape[1]
            a = ts(o, i, 1.0 / div, EPS, ALU.mult, ALU.add, *w)
            return a, PO(lambda e: e.tensor_tensor(o, o, mhalf[:, 0:n], ALU.pow), a, t_mh)

        def spread(r, tr_, dg, take, *w):
            n = r.shape[1]
            td = tt(dg.rearrange("p (c n) -> p c n", c=n), ident[:, :].unsqueeze(1).to_broadcast([128, n, 128]),
                    r.unsqueeze(2).to_broadcast([128, n, 128]), ALU.mult, tr_, t_ident, *w)
            i, ps, free = take()
            for h in range(n // 4):
                tok = mm(ps[:, h * 512:h * 512 + 512], ones[:, :], dg[:, h * 512:h * 512 + 512], True, True,
                         td, t_ones, free)
            return i, ps, tok

        xr = [RES[:, k * T:(k + 1) * T] for k in range(8)]
        o = x0
        R = at("R", 1024, F32, o)
        sq = [at(f"p0sq{i}", 1024, F32, o + i * K4) for i in (1, 2, 4, 5)]
        acc0, acc1 = at("p0acc0", 1024, F32, o + 3 * K4), at("p0acc1", 1024, F32, o + 6 * K4)
        dg0 = at("p0dg", 1024, F32, o + 4 * K4)
        macc, msq, mdg, mtm = (at(f"mem{i}", 256, F32, o + 8 * K4 + i * 1024) for i in range(4))
        mraw = at("mraw", 8 * 256, F32, o + 9 * K4)
        mhi = at("mhi", 8 * 256, F32R, o + 11 * K4)
        mlo = at("mlo", 8 * 256, F32R, o + 15 * K4)
        mst = at("mst", 448, F32, o + 17 * K4)
        gupt = at("gupt", 512, F32, o + 17 * K4 + 2048)

        x_ch = [chan(f"d_x{k}") for k in range(8)]
        t_x = [None] * 8

        def load_x(k):
            t_x[k] = SP.dma(x_ch[k], lambda e: e.dma_start(xr[k], xT[:, k, :]))

        load_x(0)
        u_load()
        load_x(1)
        load_x(2)
        u_load()
        for k in range(3, 8):
            load_x(k)
        t_mem = SP.dma(chan("d_mem"), lambda e: e.dma_start(mraw[:, :], memT))
        u_load()
        t_mst = SP.dma(chan("d_mask"), lambda e: e.dma_start(mst[:, :], masks_d))
        t_gup = SP.dma(chan("d_gup"), lambda e: e.dma_start(gupt[0:16, :], gup))
        u_load()

        sqf, ta = [None] * 4, [None, None]
        for k in range(8):
            w = vcol("norm_w", k)
            if k % 2:
                th = ts(hb(0, k), xr[k], w, 0.0, ALU.mult, ALU.add, t_x[k], t_vec, q=PO)
            else:
                th = copy(hb(0, k), xr[k], t_x[k], t_vec, scale=w)
            tl = stt(hb(1, k), xr[k], w, hb(0, k).bitcast(F32), ALU.mult, ALU.subtract, th)
            hbt[k, 0] = hbt[k, 1] = (th, tl)
            if k in (0, 2):
                u_split()
            a, q = k % 2, (DV, PO)[k % 2]
            acc = (acc0, acc1)[a]
            if k < 2:
                ta[a] = act(acc[:, :], xr[k], ACT.Square, t_x[k])
                continue
            i = 2 * a + k // 2 % 2
            t = act(sq[i][:, :], xr[k], ACT.Square, t_x[k], sqf[i])
            ta[a] = sqf[i] = tt(acc[:, :], acc[:, :], sq[i][:, :], ALU.add, t, ta[a], q=q)
        hi_by[0] = PO
        last_x = [hbt[6, 0], hbt[7, 0], ta]
        xr_r = small[:, 16:24]
        t_R = [None]

        def x_stats():
            into = S.take()
            sums(acc0, ta[0], range(8), into, True, False)
            i, ss, tp = sums(acc1, ta[1], range(8), into, False, True)
            S.free[i], tr_ = inv_root(xr_r, ss, D, tp)
            for _ in range(4):
                yield
            td = tt(dg0[:, :].rearrange("p (c n) -> p c n", c=8), ident[:, :].unsqueeze(1).to_broadcast([128, 8, 128]),
                    xr_r.unsqueeze(2).to_broadcast([128, 8, 128]), ALU.mult, tr_, t_ident)
            yield
            yield
            for h in range(2):
                oi, ob, free = S.take()
                tok = mm(ob[:, :], ones[:, :], dg0[:, h * 512:h * 512 + 512], True, True, td, t_ones, free)
                t_R[0] = S.free[oi] = copy(R[:, h * 512:h * 512 + 512], ob[:, :], tok)

        for l in range(7):
            t_mask = DV(lambda e, l=l: e.tensor_copy(masks[:, l * 256:(l + 1) * 256].rearrange("p (c n) -> p c n", c=4),
                                                     mst[:, l * 64:(l + 1) * 64].unsqueeze(1).to_broadcast([128, 4, 64])),
                        t_mst)

        mt = [None] * 8

        def mem_norm():
            ta = None
            for k in range(8):
                m = mraw[:, k * 256:(k + 1) * 256]
                if k == 0:
                    ta = act(macc[:, :], m, ACT.Square, t_mem)
                else:
                    tq = act(msq[:, :], m, ACT.Square, ta)
                    ta = tt(macc[:, :], macc[:, :], msq[:, :], ALU.add, tq, ta)
            yield
            yield
            si, bank, free = S.take()
            for t in range(2):
                tp = mm(bank[:, t:t + 1], macc[:, t * 128:(t + 1) * 128], ones[:, 0:1], True, True, ta, t_ones, free)
            mr = small[:, 8:10]
            t1 = ts(mr, bank[:, 0:2], 1.0 / D, EPS, ALU.mult, ALU.add, tp)
            S.free[si] = t1
            t2 = PO(lambda e: e.tensor_tensor(mr, mr, mhalf[:, 0:2], ALU.pow), t1, t_mh)
            yield
            yield
            yield
            td = tt(mdg[:, :].rearrange("p (c n) -> p c n", c=2), ident[:, :].unsqueeze(1).to_broadcast([128, 2, 128]),
                    mr.unsqueeze(2).to_broadcast([128, 2, 128]), ALU.mult, t2, t_ident)
            yield
            si, bank, free = S.take()
            tR = mm(bank[:, 0:256], ones[:, :], mdg[:, :], True, True, td, free)
            tl = None
            for k in range(8):
                m = mraw[:, k * 256:(k + 1) * 256]
                h_, l_ = mhi[:, k * 256:(k + 1) * 256], mlo[:, k * 256:(k + 1) * 256]
                t1 = stt(mtm[:, :], m, vcol("mem_nw", k), bank[:, 0:256], ALU.mult, ALU.mult, tR, t_vec, tl)
                th = copy(h_, mtm[:, :], t1)
                tl = tt(l_, mtm[:, :], h_.bitcast(F32), ALU.subtract, th)
                mt[k] = (th, tl)
            S.free[si] = tl

        o = x0 + K4
        KT_ = at("KT", 1024, F32, o + 0 * K4)
        VB = [at(f"VB{i}", 2048, F32, o + (1 + 2 * i) * K4) for i in range(2)]
        ST = at("ST", 768, F32, o + 5 * K4)
        GLR = at("GLR", 1024, F32, o + 6 * K4)
        DUMP = at("DUMP", 256, F32, x0 + 18 * K4)
        o = x0 + 36 * 1024
        OSB = at("OSB", 2048, F32, o)
        OT = [at(f"OT{i}", 512, F32, o + 8192 + i * 2048) for i in range(4)]
        MK = at("MK", 1024, F32, o + 4 * K4)
        MV = at("MV", 1024, F32, o + 5 * K4)
        PP = at("PP", 768, F32, o + 6 * K4)
        PT = at("PT", 512, F32, o + 6 * K4 + 3072)
        sets = [[at(f"set{i}{n}", 1024, F32, res0 + (3 * i + a) * K4) for a, n in enumerate("qkg")] for i in range(2)]
        TB = at("TB", 1024, F32, res0 + 6 * K4)
        AB = at("AB", 1024, F32, res0 + 7 * K4)

        S = Ring(BANKS[3:5])
        rate[0] = 0.8
        j0, *w0 = u_get("glr")
        j1, *w1 = u_get("gq", 0)
        got = [G.take(), G.take(), G.take(), O.take()]
        toks = gemm_units([w0, w0, w1, w1], [(n % 2, bank, free) for n, (i, bank, free) in enumerate(got)],
                          unit_k, hb, hb_tok, 8)
        u_done(j0, toks[1])
        u_done(j1, toks[3])
        bg2 += [x_stats(), mem_norm()]
        step()
        j2, *w2 = u_get("gk", 0)
        got += [O.take(), (2, BANKS[5], None)]
        for h in range(2):
            toks.append(gemm([(h,) + got[4 + h][1:]], w2, unit_k, hb, hb_tok, 8)[h])
        u_done(j2, toks[5])
        while t_R[0] is None or len(bg2) > 1:
            step()
        tq0, tk0 = [None] * 2, [None] * 2
        q, k, g = sets[0]
        for h in range(2):
            t_glr = G.free[h] = tt(cut(GLR[0:16, :], h), got[h][1][0:16, :], cut(R[0:16, :], h), ALU.mult, toks[h],
                                   t_R, last_x)
        for h in range(2):
            tq0[h] = stt(cut(q, h), got[2 + h][1], SCALE, cut(R, h), ALU.mult, ALU.mult, toks[2 + h], last_x)
            tk0[h] = tt(cut(k, h), got[4 + h][1], cut(R, h), ALU.mult, toks[4 + h], last_x)
        G.free[2], O.free[0], O.free[1] = tq0[0], tq0[1], tk0[0]
        S_free = S.free
        S = Ring(BANKS[3:6])
        S.free = S_free + [tk0[1]]
        p0_done = [last_x, t_R[0], t_glr]

        ot_ring = Ring(OT)
        ot_ch = [chan(f"d_ot{i}") for i in range(4)]
        ot_out = {}
        st = {"A": [p0_done] * 2, "T": [p0_done] * 2, "KT": p0_done, "OSB": [p0_done] * 2, "ST": [p0_done] * 3,
              "SS": [None] * 2, "PP": [p0_done] * 3, "PT": [p0_done] * 2}
        SS = small[:, 32:40]
        RS = small[:, 40:48]
        fin_n = [0, 0]

        def finish(hh, dv, nw, e0, t_ss, t_o):
            cs = slice(4 * hh, 4 * hh + 4)
            a, tr_ = inv_root(RS[:, cs], SS[:, cs], dv, t_ss, st["SS"][hh])
            yield
            yield
            tsc = []
            for i in range(4):
                c = 4 * hh + i
                ob = OSB[:, c * dv:(c + 1) * dv]
                tsc.append(ts(ob, ob, RS[:, c:c + 1], None, ALU.mult, None, tr_, t_o[i], t_ss))
            st["SS"][hh] = tsc[-1]
            yield
            for f in range(dv // 128):
                oi, ot, ofree = ot_ring.take()
                si, bank, free = S.take()
                for i in range(4):
                    c = 4 * hh + i
                    tp = tr(bank[:, i * 128:(i + 1) * 128], OSB[:, c * dv + f * 128:c * dv + f * 128 + 128],
                            tsc[i], t_ident, free)
                te = copy(ot[:, :], bank[:, :], tp, ofree, t_vec, scale=nw(f))
                S.free[si] = te
                e = e0 + f
                ot_out[e, hh] = SP.dma(ot_ch[oi], lambda g, e=e, ot=ot: g.dma_start(
                    oscr[e, :, hh * 512:(hh + 1) * 512], ot[:, :]), te)
                ot_ring.free[oi] = ot_out[e, hh]
                if f == dv // 128 - 1:
                    st["OSB"][hh] = tp
                    fin_n[hh] += 1
                yield

        started = [0, 0]

        def finish_later(hh, *a):
            started[hh] += 1
            bg2.append(finish(hh, *a))

        def osb_ready(hh):
            while fin_n[hh] < started[hh]:
                step_in(bg2)

        def linear(s, tq, tk, tg, vb, v0, dv, tv, nw, e0, freed):
            q, k, g = sets[s]

            def ch(b, c):
                return b[:, c * 128:(c + 1) * 128]

            def half(b, hh):
                return b[:, hh * 512:(hh + 1) * 512]

            t_a, t_q, t_k, t_t = [None] * 2, [None] * 2, list(tk), [tg, tg]
            tcur = [half(g, 0), half(g, 1)]
            toff = [0, 512]
            for hh in range(2):
                si, bank, free = S.take()
                for i in range(4):
                    c = 4 * hh + i
                    tp = mm(ch(bank, i), ch(k, c), ch(q, c), True, True, tq[hh], tk[hh], free)
                t_q[hh] = tt(half(q, hh), half(q, hh), half(g, hh), ALU.mult, tp, tg, tq[hh])
                t_a[hh] = tt(half(AB, hh).rearrange("p (c n) -> p c n", c=4),
                             bank[:, :].rearrange("p (c n) -> p c n", c=4),
                             ident[:, :].unsqueeze(1).to_broadcast([128, 4, 128]), ALU.mult, tp, t_ident, st["A"][hh])
                S.free[si] = t_a[hh]
                yield
            for l in range(7):
                H = 1 << l
                nb = 256 // H
                for hh in range(2):
                    si, bank, free = S.take()
                    for i in range(4):
                        c = 4 * hh + i
                        rhs = ch(q, c).rearrange("p (n t h) -> p n t h", t=2, h=H)[:, :, 1, :]
                        tp = mm(bank[:, i * 64:(i + 1) * 64], ch(k, c), rhs, True, True, t_q[hh], t_k[hh], free)
                    tv2 = tcur[hh].rearrange("p (n t) -> p n t", t=2)
                    qv = half(q, hh).rearrange("p (n t h) -> p n t h", t=2, h=H)[:, :, 1, :]
                    kv = half(k, hh).rearrange("p (n t h) -> p n t h", t=2, h=H)[:, :, 0, :]
                    t_q[hh] = tt(qv, qv, tv2[:, :, 0:1].to_broadcast([128, nb, H]), ALU.mult, tp, t_q[hh], t_t[hh])
                    t_k[hh] = tt(kv, kv, tv2[:, :, 1:2].to_broadcast([128, nb, H]), ALU.mult, tp, t_k[hh], t_t[hh])
                    nxt = TB[:, toff[hh]:toff[hh] + nb]
                    t_t[hh] = tt(nxt.unsqueeze(2), tv2[:, :, 0:1], tv2[:, :, 1:2], ALU.mult, t_t[hh], st["T"][hh])
                    tcur[hh], toff[hh] = nxt, toff[hh] + nb
                    av = half(AB, hh).rearrange("p (n t h) -> p n t h", t=2, h=H)[:, :, 1, :]
                    mv = masks[:, l * 256:(l + 1) * 256].rearrange("p (n h) -> p n h", h=H)
                    bv = bank[:, 0:256].rearrange("p (n h) -> p n h", h=H)
                    t_a[hh] = DV(lambda e, av=av, mv=mv, bv=bv: e.copy_predicated(av, mv, bv), tp, t_a[hh], t_mask)
                    S.free[si] = t_a[hh]
                    yield
            t_kt = [None] * 2
            for hh in range(2):
                si, bank, free = S.take()
                for i in range(4):
                    tp = tr(ch(bank, i), ch(k, 4 * hh + i), t_k[hh], t_ident, free)
                t_kt[hh] = copy(half(KT_, hh), bank[:, :], tp, st["KT"])
                S.free[si] = t_kt[hh]
                yield
            t_s, s_old, t_o, t_ss = None, None, [], None
            for c in range(8):
                hh = c // 4
                if c % 4 == 0:
                    osb_ready(hh)
                    t_o = []
                vc = vb[:, c * 256 + v0:c * 256 + v0 + dv]
                if c < 7:
                    oi, kvb, free = O.take()
                    tkv = mm(kvb[:, 0:dv], ch(KT_, c), vc, True, True, t_kt[hh], tv, free)
                    new = ST[:, (c % 3) * 256:(c % 3) * 256 + dv]
                    if c == 0:
                        t_n = DV(lambda e, new=new, kvb=kvb: e.tensor_copy(new, kvb[:, 0:dv]), tkv, st["ST"][0])
                    else:
                        t_n = stt(new, s_old, tcur[hh][:, c % 4:c % 4 + 1], kvb[:, 0:dv], ALU.mult, ALU.add, tkv, t_s,
                                  t_t[hh], st["ST"][c % 3])
                    O.free[oi] = t_n
                oi, ob, free = O.take()
                tp = mm(ob[:, 0:dv], ch(AB, c), vc, True, c == 0, t_a[hh], tv, free)
                if c:
                    tp = mm(ob[:, 0:dv], ch(q, c), s_old, False, True, t_s, t_q[hh])
                    st["ST"][(c - 1) % 3] = [tp, t_n if c < 7 else None]
                if c < 7:
                    s_old, t_s = new, t_n
                os_ = OSB[:, c * dv:(c + 1) * dv]
                t_c = copy(os_, ob[:, 0:dv], tp, st["OSB"])
                O.free[oi] = t_c
                t_ss = AC(lambda e, os_=os_, c=c: e.activation(DUMP[:, 0:dv], os_, ACT.Square,
                                                               accum_out=SS[:, c:c + 1]), t_c, st["SS"][hh], p0_done)
                t_o.append(t_c)
                st["A"][hh] = tp
                if c % 4 == 3:
                    finish_later(hh, dv, nw, e0, t_ss, t_o)
                yield
            st["KT"], st["T"] = tkv, [[t_t, t_n]] * 2
            freed(tp)

        def cross(h, s, tq):
            q = sets[s][0]
            NM = small[:, 48:56]
            SE = small[:, 56:64]
            got = {}

            def scores(t):
                si, bank, free = S.take()
                tp = mm(bank[:, 0:256], q[:, t * 128:(t + 1) * 128], MK[:, h * 256:(h + 1) * 256], True, True,
                        tq[t // 4], t_mk[h], free)
                nm, se = NM[:, t:t + 1], SE[:, t:t + 1]
                t1 = DV(lambda e: e.tensor_reduce(nm, bank[:, 0:256], AXX, ALU.max), tp, st["SS"])
                t2 = ts(nm, nm, -SCALE, None, ALU.mult, None, t1)
                p = PP[:, t % 3 * 256:t % 3 * 256 + 256]
                te = AC(lambda e: e.activation(p, bank[:, 0:256], ACT.Exp, bias=nm, scale=SCALE, accum_out=se),
                        t2, st["PP"][t % 3], st["SS"])
                S.free[si] = te
                t3 = DV(lambda e: e.reciprocal(se, se), te)
                got[t] = (p, te, t3, se)
                return tp

            def turned(t):
                p, te, t3, se = got[t]
                pt = PT[:, t % 2 * 256:t % 2 * 256 + 256]
                si, bank, free = S.take()
                for m in range(2):
                    tp = tr(bank[:, m * 128:(m + 1) * 128], p[:, m * 128:(m + 1) * 128], te, t_ident, free)
                st["PP"][t % 3] = tp
                tpt = copy(pt, bank[:, 0:256], tp, st["PT"][t % 2])
                S.free[si] = tpt
                got[t] = (pt, tpt, t3, se)

            def values_of(t, t_o):
                pt, tpt, t3, se = got[t]
                oi, ob, free = O.take()
                for m in range(2):
                    tp = mm(ob[:, 0:128], pt[:, m * 128:(m + 1) * 128], MV[:, m * 512 + h * 128:m * 512 + h * 128 + 128],
                            m == 0, m == 1, tpt, t_mv, free)
                st["PT"][t % 2] = tp
                os_ = OSB[:, t * 128:(t + 1) * 128]
                t4 = copy(os_, ob[:, 0:128], tp, t3, st["OSB"], scale=se)
                O.free[oi] = t4
                t_ss = AC(lambda e: e.activation(DUMP[:, 0:128], os_, ACT.Square, accum_out=SS[:, t:t + 1]),
                          t4, st["SS"])
                t_o.append(t4)
                return t_ss

            for t in range(10):
                if t >= 2:
                    if t in (2, 6):
                        osb_ready((t - 2) // 4)
                        t_o = []
                    t_ss = values_of(t - 2, t_o)
                    if t in (5, 9):
                        finish_later(t // 6, 128, lambda f: vcol("x_nw"), 12 + h, t_ss, t_o)
                    yield
                if 1 <= t < 9:
                    turned(t - 1)
                if t < 8:
                    tp = scores(t)
                yield
            set_free[s] = tp

        set_free = [p0_done, p0_done]
        v_free = [p0_done, p0_done]

        def values(name, i, vslot):
            ja, *wa = u_get(name, i, 0)
            jb, *wb = u_get(name, i, 1)
            vb = VB[vslot]
            for hf in range(4):
                gi, ps, free = G.take()
                for tl_ in range(2):
                    t = 2 * hf + tl_
                    for k in range(8):
                        hi, lo, th, tl = wa if k < 4 else wb
                        for n, (a, b, tb) in enumerate(((0, hi, th), (1, hi, th), (0, lo, tl))):
                            tok = mm(ps[:, tl_ * 256:(tl_ + 1) * 256], hb(a, k)[:, t * 128:(t + 1) * 128],
                                     b[:, (k % 4) * 256:(k % 4 + 1) * 256], k == 0 and n == 0, k == 7 and n == 2,
                                     tb, hbt[k, 0][a], free)
                        tick(3 * PASS / 2)
                if hf == 3:
                    u_done(ja, tok)
                    u_done(jb, tok)
                for tl_ in range(2):
                    t = 2 * hf + tl_
                    tv = copy(vb[:, t * 256:(t + 1) * 256], ps[:, tl_ * 256:(tl_ + 1) * 256], tok, v_free[vslot], t_R,
                              scale=xr_r[:, t:t + 1])
                G.free[gi] = tv
            return tv

        t_mk, t_mv = [], []

        def memory():
            while bg2:
                step_in(bg2)
            def m_rhs(part, k):
                return (mhi, mlo)[part][:, k * 256:(k + 1) * 256]

            
            mk_w = [mt, t_mask]
            for h in range(4):
                j, hi, lo, th, tl = u_get("mk", h)
                gi, ps, free = G.take()
                for k in range(8):
                    tick(3 * PASS / 2)
                    for n, (a, b) in enumerate(((hi, 0), (hi, 1), (lo, 0))):
                        tok = mm(ps[:, 0:256], unit_k(a, k), m_rhs(b, k), k == 0 and n == 0, k == 7 and n == 2,
                                 th if a is hi else tl, mt[k], free)
                u_done(j, tok)
                G.free[gi] = copy(MK[:, h * 256:(h + 1) * 256], ps[:, 0:256], tok, last_x, mk_w)
                t_mk.append(G.free[gi])
            mv_b = [G.take() for m in range(2)]
            for u in range(4):
                j, hi, lo, th, tl = u_get("mv", u)
                for kk in range(2):
                    k = 2 * u + kk
                    for m in range(2):
                        tick(3 * PASS)
                        for n, (a, b) in enumerate(((0, hi), (1, hi), (0, lo))):
                            tok = mm(mv_b[m][1],
                                     (mhi, mlo)[a][:, k * 256 + m * 128:k * 256 + m * 128 + 128],
                                     b[:, kk * 512:(kk + 1) * 512], k == 0 and n == 0, k == 7 and n == 2,
                                     th if b is hi else tl, mt[k], mv_b[m][2])
                u_done(j, tok)
            for m in range(2):
                G.free[mv_b[m][0]] = copy(cut(MV, m), mv_b[m][1], tok, last_x, mk_w)
            mem_done = [tok, mt]
            t_mv.append([G.free[i] for i, bank, free in mv_b])
            ot_ring.free = [[p0_done, mem_done]] * 4
            st["OSB"] = [[p0_done, mem_done]] * 2
            st["PP"], st["PT"] = [mem_done] * 3, [mem_done] * 2

        rate[0] = RATE[0]
        nset = 0
        for h in range(4):
            s = nset % 2
            nset += 1
            q, k, g = sets[s]

            def q_out(hf, bank, tok):
                return stt(cut(q, hf), bank, SCALE, cut(R, hf), ALU.mult, ALU.mult, tok, set_free[s], t_R)

            def k_out(hf, bank, tok):
                return tt(cut(k, hf), bank, cut(R, hf), ALU.mult, tok, set_free[s], t_R)

            tqs, tks, ups = [None] * 2, [None] * 2, []

            def keep(into, f):
                def evac(hf, bank, tok):
                    into[hf] = f(hf, bank, tok)
                    return into[hf]
                return evac

            if h == 0:
                tqs, tks = tq0, tk0
            else:
                project(("gq", h), keep(tqs, q_out), lambda: drain(1))
            b = vcol("b_gate", h)
            for hf in range(2):
                gi, ps, free = G.take()
                tok = mm(ps, gupt[0:16, h * 128:(h + 1) * 128], GLR[0:16, hf * 512:(hf + 1) * 512], True, True,
                         t_glr, t_gup, free)
                t1 = act(cut(g, hf), ps, ACT.Abs, tok, set_free[s], bias=b)
                t2 = ts(ps, ps, b, 0.0, ALU.add, ALU.min, tok, t1)
                ups.append((gi, ps, t1, t2))
            t1 = act(g[:, :], g[:, :], ACT.Exp, ups[0][2], t1, scale=-1.0)
            t1 = act(g[:, :], g[:, :], ACT.Ln, t1, bias=1.0)
            for hf, (gi, ps, _, t2) in enumerate(ups):
                t3 = G.free[gi] = tt(cut(g, hf), ps, cut(g, hf), ALU.subtract, t2, t1)
            tg = act(g[:, :], g[:, :], ACT.Exp, t3, scale=1.0 / 16.0)
            if h:
                project(("gk", h), keep(tks, k_out))
            tv = values("gv", h, h % 2)
            if h == 0:
                memory()

            def freed(tok, s=s, v=h % 2):
                set_free[s] = tok
                v_free[v] = tok

            bg.append(linear(s, tqs, tks, tg, VB[h % 2], 0, 256, tv, lambda f: vcol("gla_nw", f), 2 * h, freed))

        lbw = small[:, 64:80]
        lb_ = vcols("lb", 4)
        ex, pr, om, fl = (lbw[:, 4 * i:4 * i + 4] for i in range(4))
        t1 = tt(ex, lb_, lb_, ALU.subtract, t_vec)
        t1 = act(ex, ex, ACT.Exp, t1)
        t2 = DV(lambda e: e.reciprocal(pr, ex), t1)
        t2 = tt(pr, pr, ex, ALU.mult, t2)
        t2 = tt(ex, pr, pr, ALU.subtract, t2)
        t_fl = ts(fl, ex, FLOOR, None, ALU.max, None, t2)
        t_om = ts(om, ex, -1.0, 1.0, ALU.mult, ALU.add, t2)
        rate[0] = RATE[1]
        for pr_ in range(2):
            got = []
            for i in range(2):
                h = 2 * pr_ + i
                s = nset % 2
                nset += 1
                q, k, g = sets[s]
                tqs, tzs = [None] * 2, [None] * 2

                def h_out(o, into):
                    def evac(hf, bank, tok):
                        into[hf] = tt(cut(o, hf), bank, cut(R, hf), ALU.mult, tok, set_free[s], t_R)
                        return into[hf]
                    return evac

                project(("hq", h), h_out(q, tqs), lambda: drain(1 if i == 0 else 0))
                project(("hf", h), h_out(g, tzs))
                tz = tzs
                t2 = act(k[:, :], g[:, :], ACT.Sigmoid, tz, set_free[s], scale=-1.0)
                t1 = act(g[:, :], g[:, :], ACT.Sigmoid, tz, t2)
                tg = ts(g[:, :], g[:, :], om[:, h:h + 1], fl[:, h:h + 1], ALU.mult, ALU.add, t1, t_om, t_fl)
                tk = ts(k[:, :], k[:, :], om[:, h:h + 1], None, ALU.mult, None, t2, t_om)
                got.append((s, tqs, [tk, tk], tg))
            tv = values("hi", pr_, pr_)
            for i in range(2):
                s, tq, tk, tg = got[i]

                def freed(tok, s=s, v=pr_, i=i):
                    set_free[s] = tok
                    if i:
                        v_free[v] = tok

                bg.append(linear(s, tq, tk, tg, VB[pr_], i * 128, 128, tv, lambda f: vcol("hgrn_nw"),
                                 8 + 2 * pr_ + i, freed))
        rate[0] = RATE[2]
        for h in range(4):
            s = nset % 2
            nset += 1
            tqs = [None] * 2

            def xq_out(hf, bank, tok):
                tqs[hf] = tt(cut(sets[s][0], hf), bank, cut(R, hf), ALU.mult, tok, set_free[s], t_R)
                return tqs[hf]

            project(("xq", h), xq_out, lambda: drain(1))
            bg.append(cross(h, s, tqs))

        while len(bg) > 1:
            step()
        p2_done = [st["A"], st["KT"], st["T"], v_free, t_glr]
        tail = [None]
        xo = x0 + K4
        NM_ = 5
        GA = [at(f"GA{i}", 1024, F32, xo + i * K4) for i in range(2)]
        OI = [at(f"OI{i}", 1024, F32, xo + (2 + i) * K4) for i in range(2)]
        MX = [(at(f"MXH{i}", 1024, F32R, xo + (4 + 2 * i) * K4), at(f"MXL{i}", 1024, F32R, xo + (5 + 2 * i) * K4))
              for i in range(NM_)]
        MACC = [at(f"MACC{i}", 512, F32, xo + 14 * K4 + i * 2048) for i in range(2)]
        MRAW = at("MODRAW", 1536, F32, xo + 14 * K4 + 4096)
        ga_free, oi_free = [p2_done] * 2, [p2_done] * 2
        mx_free = [p2_done] * 2 + [None] * 3
        oi_ch = [chan("d_oi0"), chan("d_oi1")]
        mx_tok = {}

        def after_cross():
            drain()
            tail[0] = [list(ot_out.values()), st["OSB"], st["PP"], st["PT"], st["SS"], set_free]
            for i in range(2, NM_):
                mx_free[i] = [p2_done, tail[0]]

        oi_tok = {}

        def oi_load(e):
            if e < 16:
                s = e % 2
                oi_tok[e] = SP.dma(oi_ch[s], lambda g: g.dma_start(OI[s][:, :], oscr[e, :, :]), oi_free[s],
                                   ot_out[e, 0], ot_out[e, 1])

        def mixed(e, ring):
            j, *w = u_get("gate", e)
            s, m = e % 2, e % NM_
            t_oi = oi_tok[e]
            ga, oi, (hi, lo) = GA[s], OI[s], MX[m]
            freed, used = [], []
            for h in range(2):
                i, bank, free = ring.take()
                tok = gemm([(h, bank, free)], w, unit_k, hb, hb_tok, 8)[h]
                t1 = ring.free[i] = tt(cut(ga, h), bank, cut(R, h), ALU.mult, tok, ga_free[s], t_R)
                t1 = act(cut(ga, h), cut(ga, h), ACT.Silu, t1)
                t2 = tt(cut(ga, h), cut(ga, h), cut(oi, h), ALU.mult, t1, t_oi)
                th = copy(cut(hi, h), cut(ga, h), t2, mx_free[m])
                tl = tt(cut(lo, h), cut(ga, h), cut(hi, h).bitcast(F32), ALU.subtract, t2, th, mx_free[m], q=PO)
                used.append(t2)
                freed.append(tl)
                mx_tok[e, h] = (th, tl)
            u_done(j, tok)
            oi_free[s], ga_free[s] = used, freed
            oi_load(e + 2)
            return tok

        modcol = modv[:, 0:48]
        t_mod = {}
        sc = small[:, 24:32]
        mod_ch = [chan(f"d_mod{i}") for i in range(3)]
        mod_free = [None] * 3
        mod_tok = {}
        mod_st = {"acc": [None, None], "n": 0, "done": None}

        def mod_load(n):
            if n < 96:
                dst = MRAW[:, n % 3 * 512:n % 3 * 512 + 512]
                mod_tok[n] = SP.dma(mod_ch[n % 3], lambda e: e.dma_start(dst, wmod[n, :, :]), mod_free[n % 3])

        def mod_sum(last=1):
            if mod_st["done"] is None:
                return
            c, t, n = mod_st["done"]
            if n < last:
                mod_st["done"] = (c, t, n + 1)
                return
            mod_st["done"] = None
            si, bank, free = S.take()
            for f in range(4):
                tp = mm(bank[:, f:f + 1], MACC[c % 2][:, f * 128:(f + 1) * 128], ones[:, 0:1], True, True, t, free)
            cs = slice(c * 4, c * 4 + 4)
            S.free[si] = t_mod[c] = tt(modcol[:, cs], bank[:, 0:4], vcols("b_mod", 48)[:, cs], ALU.add, tp)
            mod_st["acc"][c % 2] = tp

        def mods(count):
            mod_sum()
            for n in range(mod_st["n"], min(96, mod_st["n"] + count)):
                c, k = n // 8, n % 8
                src = MRAW[:, n % 3 * 512:n % 3 * 512 + 512]
                acc, old = MACC[c % 2], mod_st["acc"][c % 2]
                if k == 0:
                    t = ts(acc[:, :], src, sc[:, 0:1], None, ALU.mult, None, mod_tok[n], t_sc, old)
                else:
                    t = stt(acc[:, :], src, sc[:, k:k + 1], acc[:, :], ALU.mult, ALU.add, mod_tok[n], old)
                mod_st["acc"][c % 2] = mod_free[n % 3] = t
                mod_load(n + 3)
                if k == 7:
                    mod_st["done"] = (c, t, 0)
            mod_st["n"] = min(96, mod_st["n"] + count)

        x_tok = [None] * 8
        res = [RES[:, f * T:(f + 1) * T] for f in range(8)]

        def rh(f, h):
            return RES[:, f * T + h * 512:f * T + h * 512 + 512]

        rt_ = {}

        def load_res(f):
            rt_[f, 0] = rt_[f, 1] = SP.dma(x_ch[f], lambda e, f=f: e.dma_start(res[f], xT[:, f, :]), p2_done, tail[0])

        sqn = {"free": [None] * 4, "n": 0, "buf": None}

        def add_sq(acc, f, h, t_acc, *w, scale=None):
            kw = {} if scale is None else {"scale": scale}
            cs = slice(h * 512, (h + 1) * 512)
            if t_acc[h] is None:
                t_acc[h] = act(acc[:, cs], rh(f, h), ACT.Square, *w, **kw)
                return
            i = sqn["n"] % len(sqn["buf"])
            sqn["n"] += 1
            b = sqn["buf"][i]
            q = act(b[:, :], rh(f, h), ACT.Square, *w, sqn["free"][i], **kw)
            sqn["free"][i] = t_acc[h] = tt(acc[:, cs], acc[:, cs], b[:, :], ALU.add, q, t_acc[h])

        def pair(j2):
            return [(2 * j2 + ff, lambda a, k, ff=ff: a[:, k * 256 + ff * 128:k * 256 + ff * 128 + 128]) for ff in range(2)]

        ACC1 = at("ACC1", 1024, F32, xo + 2 * K4)
        ACC2 = at("ACC2", 1024, F32, xo + 3 * K4)
        SQP = [at(f"SQP{i}", 512, F32, xo + i * 2048) for i in range(4)]
        sta, stb = [None, None], [None, None]

        def wo_rhs(g):
            return lambda part, k, h: MX[(4 * g + k) % NM_][part][:, h * 512:(h + 1) * 512]

        def wo_tok(g):
            return lambda part, k, h: mx_tok[4 * g + k, h][part]

        def wo_evac(g):
            def evac(f, h, bank, tok):
                t = rt_[f, h] = tt(rh(f, h), rh(f, h), bank, ALU.add, tok, rt_[f, h])
                if g == NG - 1:
                    add_sq(ACC1, f, h, sta, t, ga_free, oi_free)
                    add_sq(ACC2, f, h, stb, t, ga_free, oi_free, scale=vcol("fin_w", f))
                return t
            return evac

        rate[0] = RATE[3]
        t_sc = act(sc, vcols("c", 8), ACT.Silu, t_vec)
        oi_load(0)
        oi_load(1)
        mixed(0, G)
        mixed(1, G)
        after_cross()
        mod_free[:] = [tail[0]] * 3
        mod_st["acc"] = [tail[0], tail[0]]
        for n in range(3):
            mod_load(n)
        for e in range(2, 5):
            for f in range(3 * e - 6, min(8, 3 * e - 3)):
                load_res(f)
            mods(4)
            mixed(e, G)
        B = Ring(BANKS[0:6])
        B.free = G.free + S.free
        S = O

        R1, R2, RR, W1 = small[:, 80:88], small[:, 88:96], small[:, 96:104], small[:, 104:112]
        DG = at("DG", 1024, F32, xo + 14 * K4)
        TM = [at(f"TM{i}", 512, F32, xo + 6 * K4 + i * 2048) for i in range(4)]
        A1 = small[:, 112:120]
        tm_free, tm_n = [None] * 4, [0]
        hb_free = [None]

        def hs(x, h):
            return x[:, 4 * h:4 * h + 4]

        def modulated(k, h, TM, scol, shift, Rb, tR, *w):
            i = tm_n[0] % len(TM)
            tm_n[0] += 1
            tm = TM[i]
            t1 = stt(tm[:, :], rh(k, h), scol, Rb, ALU.mult, ALU.mult, tR, tm_free[i], rt_[k, h], *w)
            th = act(hb(0, k, h), tm[:, :], ACT.Identity, t1, hb_free[0], bias=shift)
            tl = stt(hb(1, k, h), tm[:, :], shift, hb(0, k, h).bitcast(F32), ALU.add, ALU.subtract, t1, th, hb_free[0])
            tm_free[i] = tl
            hbt[k, h] = (th, tl)
            return t1

        def between_blocks(h):
            for _ in range(WAIT[0]):
                yield
            si, ss, tp = sums(ACC1, sta[h], range(4 * h, 4 * h + 4))
            S.free[si], tr1 = inv_root(hs(R1, h), ss, D, tp)
            si, ss2, tp2 = sums(ACC2, stb[h], range(4 * h, 4 * h + 4))
            t1 = tt(hs(RR, h), hs(R1, h), hs(R1, h), ALU.mult, tr1)
            t2 = tt(hs(R2, h), hs(RR, h), ss2, ALU.mult, t1, tp2)
            S.free[si] = t2
            _, tr2 = inv_root(hs(R2, h), hs(R2, h), D, t2)
            t_rr = tt(hs(RR, h), hs(R1, h), hs(R2, h), ALU.mult, tr2, t2)
            for _ in range(WAIT[1]):
                yield
            si, Rb, tR = spread(hs(RR, h), t_rr, DG[:, h * 512:(h + 1) * 512], S.take, mod_st["acc"])
            for k in range(8):
                if k:
                    yield
                t1 = modulated(k, h, TM, W1[:, k:k + 1], modcol[:, k:k + 1], Rb, tR, t_w1, t_mod[0], t_mod[1], mx_free[1])
            S.free[si] = t1
            t_r1[h] = tr1

        t_r1 = [None] * 2

        for g in range(NG):
            if g == NG - 1:
                sqn["buf"], sqn["free"] = SQP, [None] * 4
            if g < NG - 1:
                for j2 in range(4):
                    tok = one_unit(("wo", g, j2), pair(j2), wo_rhs(g), wo_tok(g), 4, wo_evac(g))
                    mods(4)
            else:
                mods(96)
                mod_sum(0)
                ta = ts(A1, modcol[:, 8:16], 1.0, None, ALU.add, None, t_mod[2], t_mod[3])
                ta = tt(A1, A1, vcols("n1", 8), ALU.mult, ta)
                t_w1 = tt(W1, A1, vcols("fin_w", 8), ALU.mult, ta)
                one_unit(("wo", g, 0), pair(0), wo_rhs(g), wo_tok(g), 4, wo_evac(g))
                rate[0] = 1.0
                tok = by_halves([(("wo", g, j2), pair(j2)) for j2 in (1, 2, 3)], wo_rhs(g), wo_tok(g), 4, wo_evac(g),
                                lambda: bg.append(between_blocks(0)))
            for k in range(4):
                mx_free[(4 * g + k) % NM_] = tok
            for e in range(4 * g + 5, min(4 * g + 9, 16)):
                hb_free[0] = mixed(e, B)
                mods(4)
        drain()

        p4 = [None]
        xo = x0
        CO = [at(f"CO{f}", 1024, F32, xo + f * K4) for f in range(8)]
        UPW = NSEG * SEGP
        UP = [at(f"UP{i}", UPW, F32, xo + 8 * K4 + i * UPW * 4) for i in range(4)]
        po = xo + 8 * K4 + 4 * UPW * 4
        SG = CO[7]
        PR = [at(f"PR{i}", 1024, F32, po + i * K4) for i in range(3)]
        UPH, UPL = at("UPH", UPW, F32R, hb0), at("UPL", UPW, F32R, hb0 + UPW * 4)
        DGH = [at(f"DGH{i}", 128, F32R, hb0 + 12 * 1024 + i * 1024) for i in range(4)]
        DGL = [at(f"DGL{i}", 128, F32R, hb0 + 12 * 1024 + i * 1024 + 512) for i in range(4)]
        WTH, WTL = at("WTH", 32, F32R, hb0 + 4 * K4), at("WTL", 32, F32R, hb0 + 4 * K4 + 128)
        M6B, DG6 = at("M6B", 1024, F32, hb0 + 5 * K4), at("DG6", 1024, F32, hb0 + 6 * K4)
        YT = [at(f"YT{i}", 1024, F32, hb0 + (8 + i) * K4) for i in range(3)]

        def seg(b):
            return b[:, :].rearrange("p (s t) -> p s t", s=NSEG)

        up_ring = Ring(UP)
        co_tok = [None] * 8
        conv_state = {}

        def tap(up, k):
            return seg(up)[:, :, k:k + SEG]

        def wcol(f, k):
            return vcol("w_dw", f * TAPS + k)

        def conv_dve(f, ui, up, tu):
            co, other = seg(CO[f]), seg(PR[2])
            ta = DV(lambda e: e.tensor_scalar(co, tap(up, 0), wcol(f, 0), vcol("b_dw", f), ALU.mult, ALU.add), tu, p4)
            tb = DV(lambda e: e.tensor_scalar(other, tap(up, 1), wcol(f, 1), None, ALU.mult), tu, conv_state["dve"])
            for k in range(2, TAPS):
                yield
                dst = co if k % 2 == 0 else other
                t = stt(dst, tap(up, k), wcol(f, k), dst, ALU.mult, ALU.add, ta if k % 2 == 0 else tb)
                if k % 2 == 0:
                    ta = t
                else:
                    tb = t
            up_ring.free[ui] = t
            co_tok[f] = tt(co, co, other, ALU.add, ta, tb)
            conv_state["dve"] = co_tok[f]

        def conv_pool(f, ui, up, tu):
            co = seg(CO[f])
            t = act(co, tap(up, 0), ACT.Identity, tu, p4, scale=wcol(f, 0), bias=vcol("b_dw", f))
            for k in range(1, TAPS):
                i = k % 2
                tp_ = act(seg(PR[i]), tap(up, k), ACT.Copy, tu, conv_state["pool"][i], scale=wcol(f, k))
                t = tt(co, co, seg(PR[i]), ALU.add, tp_, t, q=PO)
                conv_state["pool"][i] = t
                yield
            up_ring.free[ui] = tp_
            co_tok[f] = t

        def conv_pe(f, up, tus, free_hb, at_tap):
            w = vcols("w_dw", 8 * TAPS)[:, f * TAPS:(f + 1) * TAPS]
            tw = copy(WTH[:, 0:TAPS], w, t_vec, free_hb)
            twl = tt(WTL[:, 0:TAPS], w, WTH[:, 0:TAPS].bitcast(F32), ALU.subtract, tw)
            tu = []
            for h in range(2):
                sl = slice(h * UPW // 2, (h + 1) * UPW // 2)
                th = copy(UPH[:, sl], up[:, sl], tus, free_hb)
                tu.append((th, tt(UPL[:, sl], up[:, sl], UPH[:, sl].bitcast(F32), ALU.subtract, th)))
            got = [B.take() for _ in range(2)]
            dfree = [None] * 4
            for k in range(TAPS):
                dh, dl = DGH[k % 4], DGL[k % 4]
                tdh = act(dh[:, :], ident[:, :], ACT.Copy, tw, dfree[k % 4], scale=WTH[:, k:k + 1].bitcast(F32))
                tdl = act(dl[:, :], ident[:, :], ACT.Copy, twl, dfree[k % 4], scale=WTL[:, k:k + 1].bitcast(F32))
                for n, (d, u, td) in enumerate(((dh, UPH, tdh), (dh, UPL, tdh), (dl, UPH, tdl))):
                    for h in range(2):
                        tok = mm(got[h][1], d[:, :], tap(u, k)[:, h * 8:(h + 1) * 8, :], k == 0 and n == 0,
                                 k == TAPS - 1 and n == 2, td, tu[h], got[h][2])
                dfree[k % 4] = tok
                tick(6 * PASS)
                if k in at_tap:
                    at_tap[k]()
            return got, tok

        DGR1 = at("DGR1", 1024, F32, hb0 + 7 * K4)
        R1B = at("R1B", 1024, F32, xo + 17 * K4 + 2048)
        t_r1b = []

        def first_norm_rows():
            for h in range(2):
                i, Rb, tR = spread(hs(R1, h), t_r1[h], cut(DGR1, h), S.take, last_pw1)
                t_r1b.append(copy(cut(R1B, h), Rb, tR, p4))
                S.free[i] = t_r1b[-1]


        def take_up():
            ui, up, ufree = up_ring.take()
            while ufree is None:
                lanes_step()
                ufree = up_ring.free[ui]
            up_ring.free[ui] = None
            return ui, up, ufree

        rate[0] = 1.0
        got = [u_get("pa", 0), u_get("pg", 0), u_get("pa", 1)]
        banks = {}
        bg.append(between_blocks(1))
        for h in range(2):
            if h == 1:
                drain()
            bs = [B.take() for _ in got]
            toks = gemm_units([w for j, *w in got], [(h, bank, free) for i, bank, free in bs], unit_k, hb, hb_tok, 8)
            for n, ((j, *w), (i, bank, free)) in enumerate(zip(got, bs)):
                banks[n, h] = (i, bank, toks[n])
                if h:
                    u_done(j, toks[n])
        p4[0] = [rt_[7, 0], rt_[7, 1], hbt[7, 0], hbt[7, 1], tm_free, sqn["free"], sta, stb, t_r1]
        conv_state.update(sg=p4, dve=p4, pool=[p4, p4])
        for i in range(4):
            pads = [seg(UP[i])[:, :, 0:PAD], seg(UP[i])[:, :, PAD + SEG:SEGP]]
            up_ring.free[i] = [DV(lambda e, p=p: e.memset(p, 0.0), p4) for p in pads]
        hi_by[0] = AC

        def product(*kind):
            j, *w = u_get(*kind)
            out_ = []
            for h in range(2):
                i, bank, free = B.take()
                out_.append((i, bank, gemm([(h, bank, free)], w, unit_k, hb, hb_tok, 8)[h]))
            u_done(j, out_[1][2])
            return out_

        for f in range(8):
            ui, up, ufree = take_up()
            a_b = [banks[2 * f, h] for h in range(2)] if f < 2 else product("pa", f)
            g_b = [banks[1, h] for h in range(2)] if f == 0 else product("pg", f)
            tus = []
            for h in range(2):
                (ai, ab, atok), (gi, gb, gtok) = a_b[h], g_b[h]
                t1 = B.free[gi] = act(cut(SG, h), gb, ACT.Sigmoid, gtok, conv_state["sg"], bias=vcol("b_pw1", 8 + f))
                tu = B.free[ai] = stt(seg(up)[:, 8 * h:8 * h + 8, PAD:PAD + SEG], ab.rearrange("p (s t) -> p s t", s=8),
                                      vcol("b_pw1", f), seg(SG)[:, 8 * h:8 * h + 8, :], ALU.add, ALU.mult,
                                      atok, t1, ufree)
                tus.append(tu)
            conv_state["sg"] = tus
            if CONV[f] != "pe":
                now["dve"] += 1.4
                lane_add(CONV[f], {"dve": conv_dve, "pool": conv_pool}[CONV[f]](f, ui, up, tus))
        last_pw1 = g_b[1][2]
        hi_by[0] = PO

        M6, DL, RV, D2, DR = (small[:, 120 + 8 * i:128 + 8 * i] for i in range(5))
        ln = {"y": [last_pw1] * 3, "n": 0}

        vsum, dsum = [], []

        def first_mean():
            vsum.extend(S.take())
            dsum.extend(S.take())
            while not all(co_tok[:6]):
                lanes_step()
            into = B.take()
            for f in range(6):
                i, ss, tp = sums(CO[f], co_tok[f], range(8), into, f == 0, f == 5)
            ln["mu"] = B.free[into[0]] = ts(M6, into[1][:, 0:8], 1.0 / (6 * 128), None, ALU.mult, None, tp)

        def shift_rows():
            ln["m6b"] = []
            for h in range(2):
                i, Rb, tR = spread(hs(M6, h), ln["mu"], cut(DG6, h), B.take, last_pw1)
                B.free[i] = copy(cut(M6B, h), Rb, tR, last_pw1)
                ln["m6b"].append(B.free[i])

        def squares(f, t_y, h=None):
            i = ln["n"] % 3
            ln["n"] += 1
            ws = range(2) if h is None else (h,)
            src, y = (CO[f][:, :], YT[i][:, :]) if h is None else (cut(CO[f], h), cut(YT[i], h))
            q = act(y, src, ACT.Square, t_y, ln["y"][i])
            for t in [4 * hh + n for hh in ws for n in range(4)]:
                ln["v"] = tp = mm(vsum[1][:, t:t + 1], YT[i][:, t * 128:(t + 1) * 128], ones[:, 0:1],
                                  f == 0 and t == 0, f == 7, q, vsum[2], skip=True)
            ln["y"][i] = tp

        def shifted(f):
            co_tok[f] = tt(CO[f][:, :], CO[f][:, :], M6B[:, :], ALU.subtract, ln["m6b"], ln["mu"], co_tok[f], q=PO)

        sched = {LN_AT - 8: first_norm_rows, LN_AT: first_mean, LN_AT + 2: lambda: (shift_rows(), shifted(0), shifted(1))}
        for f in range(2, 6):
            sched[LN_AT + 3 + 2 * (f - 2)] = lambda f=f: (shifted(f), squares(f - 2, co_tok[f - 2]))
        pe_banks, t_pe = conv_pe(7, up, tus, last_pw1, sched)
        while lanes["dve"] or lanes["pool"]:
            lanes_step()
        squares(4, co_tok[4])
        squares(5, co_tok[5])
        c6 = co_tok[6]
        done = [[], []]
        for f in (6, 7):
            for h in range(2):
                ch_ = cut(CO[f], h)
                if f == 6:
                    t = tt(ch_, ch_, cut(M6B, h), ALU.subtract, ln["m6b"], c6)
                else:
                    i, bank, _ = pe_banks[h]
                    t = B.free[i] = stt(ch_, bank, vcol("b_dw", 7), cut(M6B, h), ALU.add, ALU.subtract, t_pe,
                                        ln["m6b"], conv_state["sg"])
                done[h].append(t)
        for f in (6, 7):
            for h in range(2):
                t = done[h][f - 6]
                for c in range(4 * h, 4 * h + 4):
                    td_ = mm(dsum[1][:, c:c + 1], CO[f][:, c * 128:(c + 1) * 128], ones[:, 0:1],
                             f == 6 and c == 0, f == 7, t, dsum[2], skip=True)
                squares(f, t, h)
        co_tok[6], co_tok[7] = [done[h][0] for h in range(2)], [done[h][1] for h in range(2)]
        c_all = list(co_tok)
        lo_ = xo + 8 * K4
        DGV = at("DGV", 1024, F32, lo_)
        DGD = at("DGD", 1024, F32, lo_ + K4)
        ZT = [at(f"ZT{i}", 512, F32, lo_ + 2 * K4 + i * 2048) for i in range(6)]
        t1 = S.free[dsum[0]] = ts(DL, dsum[1][:, 0:8], 1.0 / D, None, ALU.mult, None, td_)
        t2 = S.free[vsum[0]] = ts(RV, vsum[1][:, 0:8], 1.0 / D, EPS, ALU.mult, ALU.add, ln["v"])
        t1 = tt(D2, DL, DL, ALU.mult, t1)
        t2 = tt(RV, RV, D2, ALU.subtract, t1, t2)
        t_rv = PO(lambda e: e.tensor_tensor(RV, RV, mhalf, ALU.pow), t2, t_mh)
        t_dr = tt(DR, DL, RV, ALU.mult, t_rv)
        hb_free[0] = [last_pw1, t_pe, ln["v"], c_all]
        zf, n_z = [c_all] * 6, 0
        sp = [[spread(hs(RV, h), t_rv, cut(DGV, h), B.take, c_all), spread(hs(DR, h), t_dr, cut(DGD, h), B.take, c_all)]
              for h in range(2)]
        for h in range(2):
            (ri, Rb, tR), (di, Db, tD) = sp[h]
            for f in range(8):
                ch_, i = cut(CO[f], h), n_z % 6
                z = ZT[i]
                n_z += 1
                t1 = tt(ch_, ch_, Rb, ALU.mult, tR, co_tok[f])
                t2 = tt(ch_, ch_, Db, ALU.subtract, tD, t1)
                t3 = act(z[:, :], ch_, ACT.Silu, t2, zf[i], scale=vcol("ln_g", f), bias=vcol("ln_b", f))
                th = copy(hb(0, f, h), z[:, :], t3, hb_free[0])
                tl = tt(hb(1, f, h), z[:, :], hb(0, f, h).bitcast(F32), ALU.subtract, th, hb_free[0], q=PO)
                zf[i] = tl
                hbt[f, h] = (th, tl)
            B.free[ri], B.free[di] = t1, t2
        p5 = [hbt[7, 0], hbt[7, 1], t2, t3]

        GBV = small[:, 136:144]
        tgb = tt(GBV, modcol[:, 16:24], vcols("b_pw2", 8), ALU.mult, t_mod[4], t_mod[5])
        ACC3 = at("ACC3", 1024, F32, xo)
        sqn["buf"], sqn["free"], sqn["n"] = [at(f"SQ3{i}", 512, F32, xo + K4 + i * 2048) for i in range(4)], [p5] * 4, 0
        EV = [at(f"EV{i}", 512, F32, xo + 3 * K4 + i * 2048) for i in range(4)]
        ev_free, ev_n = [p5] * 4, [0]
        st3 = [None, None]

        def pw2_evac(f, h, bank, tok):
            i = ev_n[0] % 4
            ev_n[0] += 1
            ev = EV[i]
            t1 = act(ev[:, :], bank, ACT.Identity, tok, ev_free[i], tgb, scale=modcol[:, 16 + f:17 + f],
                     bias=GBV[:, f:f + 1])
            t2 = stt(rh(f, h), rh(f, h), vcol("fin_w", f), cut(R1B, h), ALU.mult, ALU.mult, t_r1b, rt_[f, h])
            ev_free[i] = rt_[f, h] = tt(rh(f, h), rh(f, h), ev[:, :], ALU.add, t1, t2)
            add_sq(ACC3, f, h, st3, rt_[f, h], p5)
            return t1

        R3, A2 = small[:, 160:168], small[:, 168:176]
        ta = ts(A2, modcol[:, 32:40], 1.0, None, ALU.add, None, t_mod[8], t_mod[9])
        t_a2 = tt(A2, A2, vcols("n2", 8), ALU.mult, ta)
        DG3 = at("DG3", 1024, F32, xo + 5 * K4)
        TN = [at(f"TN{i}", 512, F32, xo + 6 * K4 + i * 2048) for i in range(4)]

        def before_mlp(h):
            for _ in range(WAIT[0]):
                yield
            si, ss, tp = sums(ACC3, st3[h], range(4 * h, 4 * h + 4))
            S.free[si], tr_ = inv_root(hs(R3, h), ss, D, tp)
            for _ in range(WAIT[2]):
                yield
            si, Rb, tR = spread(hs(R3, h), tr_, DG3[:, h * 512:(h + 1) * 512], S.take, p5)
            for k in range(8):
                if k:
                    yield
                t1 = modulated(k, h, TN, A2[:, k:k + 1], modcol[:, 24 + k:25 + k], Rb, tR, t_a2, t_mod[6], t_mod[7], p5)
            S.free[si] = t1
            mlp_in[h] = t1

        mlp_in = [None, None]

        def plain(f):
            return [(f, unit_k)]

        rate[0] = 1.0
        tok = by_halves([(("pw2", f), plain(f)) for f in range(3)], hb, hb_tok, 8, pw2_evac, outer=True)
        for f in (3, 4):
            one_unit(("pw2", f), plain(f), hb, hb_tok, 8, pw2_evac)

        def first_half_done():
            hb_half[0] = PE.ops[-1][0]
            hb_free[0] = hb_half[0]
            bg.append(before_mlp(0))

        hb_half = [None]
        tok = by_halves([(("pw2", f), plain(f)) for f in (5, 6, 7)], hb, hb_tok, 8, pw2_evac, first_half_done)
        drain()
        hb_free[0] = tok

        NH = 2 * GT
        HID = [(at(f"HIDH{i}", 1024, F32R, xo + (2 * i) * K4), at(f"HIDL{i}", 1024, F32R, xo + (2 * i + 1) * K4))
               for i in range(NH)]
        RL = at("RL", 512, F32, xo + 2 * NH * K4)
        hid_tok = {}
        rl_free = [None]
        p6 = [None]
        hid_free = [None] * NH

        def hid_evac(i, h, bank, tok):
            s = i % NH
            hi, lo = HID[s]
            cs = slice(h * 512, (h + 1) * 512)
            t1 = act(RL[:, :], bank, ACT.Relu, tok, rl_free[0], p6)
            t2 = stt(bank, bank, 0.0, RL[:, :], ALU.max, ALU.mult, t1)
            th = copy(hi[:, cs], bank, t2, hid_free[s], p6)
            tl = tt(lo[:, cs], bank, hi[:, cs].bitcast(F32), ALU.subtract, th, t2, hid_free[s], p6)
            rl_free[0] = t2
            hid_tok[i, h] = (th, tl)
            return tl

        FIN = [at(f"FIN{i}", 1024, F32, hb0 + i * K4) for i in range(8)]
        SQ4 = [at(f"SQ4{i}", 512, F32, hb0 + i * 2048) for i in range(4)]
        ACC4, DG4 = FIN[2], FIN[3]
        st4 = [None, None]
        t_w1 = None

        def w2_rhs(g):
            return lambda part, k, h: HID[(GT * g + k) % NH][part][:, h * 512:(h + 1) * 512]

        def w2_tok(g):
            return lambda part, k, h: hid_tok[GT * g + k, h][part]

        def w2_evac(g):
            def evac(f, h, bank, tok):
                t = rt_[f, h] = stt(rh(f, h), bank, modcol[:, 40 + f:41 + f], rh(f, h), ALU.mult, ALU.add, tok,
                                    t_mod[10], t_mod[11], rt_[f, h], mlp_in)
                if g == HG - 1:
                    add_sq(ACC4, f, h, st4, t, hb_free[0])
                return t
            return evac

        R4 = small[:, 160:168]
        o_ch = [chan(f"d_out{i}") for i in range(16)]
        outs = []

        def last_norm(h):
            for _ in range(WAIT[0]):
                yield
            si, ss, tp = sums(ACC4, st4[h], range(4 * h, 4 * h + 4))
            S.free[si], tr_ = inv_root(hs(R4, h), ss, D, tp)
            for _ in range(WAIT[2]):
                yield
            si, Rb, tR = spread(hs(R4, h), tr_, DG4[:, h * 512:(h + 1) * 512], S.take, hb_free[0])
            for k in range(8):
                t1 = stt(rh(k, h), rh(k, h), vcol("fin_g", k), Rb, ALU.mult, ALU.mult, tR, rt_[k, h], st4[h])
                outs.append(SP.dma(o_ch[8 * h + k], lambda e, k=k: e.dma_start(
                    out[k * 128:(k + 1) * 128, h * 512:(h + 1) * 512], rh(k, h)), t1))

        bg.append(before_mlp(1))
        got = [u_get("w1", i) for i in range(3)]
        held = []
        for h in range(2):
            if h == 1:
                drain()
                p6[0] = [mlp_in, hbt[7, 0], hbt[7, 1], tm_free, st3, sqn["free"], ev_free]
                for i, hh, bank, bi, tok in held:
                    B.free[bi] = hid_evac(i, hh, bank, tok)
            bs = [B.take() for _ in got]
            toks = gemm_units([w for j, *w in got], [(h, bank, free) for bi, bank, free in bs], unit_k, hb, hb_tok, 8)
            for n, ((j, *w), (bi, bank, free), tok) in enumerate(zip(got, bs, toks)):
                if h == 0:
                    held.append((n, h, bank, bi, tok))
                else:
                    B.free[bi] = hid_evac(n, h, bank, tok)
                    u_done(j, tok)
        for i in range(3, GT):
            t_w1 = one_unit(("w1", i), plain(i), hb, hb_tok, 8, hid_evac)
        for g in range(HG):
            if g + 1 < HG:
                for i in range(GT):
                    n = (g + 1) * GT + i
                    t_w1 = one_unit(("w1", n), plain(n), hb, hb_tok, 8, hid_evac)
                for j2 in range(4):
                    tok = one_unit(("w2", g, j2), pair(j2), w2_rhs(g), w2_tok(g), GT, w2_evac(g))
            else:
                hb_free[0] = t_w1
                sqn["buf"], sqn["free"] = SQ4, [t_w1] * 4
                one_unit(("w2", g, 0), pair(0), w2_rhs(g), w2_tok(g), GT, w2_evac(g))
                by_halves([(("w2", g, j2), pair(j2)) for j2 in (1, 2, 3)], w2_rhs(g), w2_tok(g), GT, w2_evac(g),
                          lambda: bg.append(last_norm(0)))
                drain()
                bg.append(last_norm(1))
                drain()
            for k in range(GT):
                hid_free[(GT * g + k) % NH] = tok

        for q in (PE, AC, DV, PO, SP):
            q.number()
        block = es.enter_context(nc.Block())

        @block.tensor
        def _(eng):
            PE.emit(eng)

        @block.scalar
        def _(eng):
            AC.emit(eng)

        @block.vector
        def _(eng):
            DV.emit(eng)

        @block.gpsimd
        def _(eng):
            PO.emit(eng)

        @block.sync
        def _(eng):
            SP.emit(eng)
            for w in list(ot_out.values()) + outs:
                eng.wait_ge(w.sem, w.count)


def lay_out(inputs):
    f = {n: np.asarray(a) for n, a in inputs.items()}
    w_in, w_out = f["w_in"][0], f["w_out"][0]
    kv, pw1, pw2 = f["w_mem_kv"][0], f["conv_w_pw1_2"][0], f["conv_w_pw2_2"][0]
    w1, w2 = f["mlp_w1_2"][0], f["mlp_w2_2"][0]
    OFF = {}
    at = 0
    for n, c in (("gq", 512), ("gk", 512), ("gv", 1024), ("glr", 16), ("hq", 512), ("hf", 512), ("hi", 512),
                 ("xq", 512), ("gate", 2048)):
        OFF[n] = at
        at += c

    def cols(w, c0, n, k0=0, nk=8):
        return w[k0 * 128:(k0 + nk) * 128, c0:c0 + n].reshape(nk, 128, n).transpose(1, 0, 2)

    wall = np.zeros((len(UNITS), 128, 1024), np.float32)
    for i, u in enumerate(UNITS):
        n = u[0]
        if n == "mk":
            t = cols(kv, u[1] * 128, 128)
        elif n == "mv":
            t = cols(kv, 512, 512, 2 * u[1], 2)
        elif n == "glr":
            wall[i].reshape(128, 8, 128)[:, :, 0:16] = cols(w_in, OFF["glr"], 16)
            continue
        elif n in ("gv", "hi"):
            t = cols(w_in, OFF[n] + u[1] * 256, 256, 4 * u[2], 4)
        elif n in OFF:
            t = cols(w_in, OFF[n] + u[1] * 128, 128)
        elif n == "wo":
            t = cols(w_out, u[2] * 256, 256, 4 * u[1], 4)
        elif n == "pa":
            t = cols(pw1, u[1] * 128, 128)
        elif n == "pg":
            t = cols(pw1, 1024 + u[1] * 128, 128)
        elif n == "pw2":
            t = cols(pw2, u[1] * 128, 128)
        elif n == "w1":
            t = cols(w1, u[1] * 128, 128)
        elif n == "w2":
            t = cols(w2, u[2] * 256, 256, GT * u[1], GT)
        wall[i].reshape(t.shape)[...] = t
    wm = f["w_mod_2"][0]
    wmod = np.ascontiguousarray(wm.reshape(8, 128, 12, 512).transpose(2, 0, 1, 3)).reshape(96, 128, 512)

    def col(a):
        return a.reshape(-1, 128).T

    dw = f["conv_w_dw_2"][0].T.reshape(8, 128, TAPS).transpose(1, 0, 2).reshape(128, 8 * TAPS)
    parts = {"norm_w": f["norm_w"], "b_gate": f["gla_b_gate"], "gla_nw": f["gla_norm_w"], "lb": f["hgrn_lower_bounds"],
             "hgrn_nw": f["hgrn_norm_w"], "mem_nw": f["mem_norm_w"], "x_nw": f["xattn_norm_w"],
             "fin_w": f["final_norm_w"], "c": f["c_2"], "b_mod": f["b_mod_2"], "n1": f["norm1_g_2"],
             "n2": f["norm2_g_2"], "fin_g": f["final_g_2"], "b_pw1": f["conv_b_pw1_2"], "b_dw": f["conv_b_dw_2"],
             "ln_g": f["conv_ln_g_2"], "ln_b": f["conv_ln_b_2"], "b_pw2": f["conv_b_pw2_2"]}
    vecs = np.concatenate([dw if n == "w_dw" else col(parts[n]) for n, _ in VECS], axis=1)
    xT = f["x"][0].T.reshape(8, 128, T).transpose(1, 0, 2)
    memT = f["mem"][0].T.reshape(8, 128, 256).transpose(1, 0, 2).reshape(128, 2048)
    ident = np.eye(128, dtype=np.float32)
    masks = np.zeros((128, 7, 64), np.float32)
    for l in range(7):
        H = 1 << l
        for b in range(64 // H):
            masks[b * 2 * H:b * 2 * H + H, l, b * H:(b + 1) * H] = 1
    masks = masks.reshape(128, 448)
    arrays = {"wall": wall, "wmod": wmod, "xT": xT, "memT": memT, "vecs": vecs, "gup": f["gla_w_gate_up"][0],
              "ident": ident, "masks": masks}
    return {n: np.ascontiguousarray(a) for n, a in arrays.items()}


def kernel(**inputs):
    import concourse.bacc as bacc
    from concourse.bass_utils import run_bass_kernel_spmd

    nc = bacc.Bacc("TRN2", target_bir_lowering=False, num_devices=1)
    arrays = lay_out(inputs)
    aps = [nc.dram_tensor(n, a.shape, mybir.dt.from_np(a.dtype), kind="ExternalInput").ap() for n, a in arrays.items()]
    out = nc.dram_tensor("outT", (D, T), F32, kind="ExternalOutput").ap()
    oscr = nc.dram_tensor("oscr", (16, 128, T), F32, kind="Internal").ap()
    build_program(nc, *aps, out, oscr)
    r = run_bass_kernel_spmd(nc, [arrays], core_ids=[0])
    return np.ascontiguousarray(r.results[0]["outT"].T)[None]
```

```python
from contextlib import ExitStack

import numpy as np
import concourse.bass as bass
from concourse import mybir

F32 = mybir.dt.float32
F32R = mybir.dt.float32r
U8 = mybir.dt.uint8
ALU = mybir.AluOpType
ACT = mybir.ActivationFunctionType
AXX = mybir.AxisListType.X

T = 1024
D = 1024
NT = T // 128
KT = D // 128
EPS = 1e-6
SCALE = 128.0 ** -0.5
FLOOR = 1e-30
SEG = 64
NSEG = T // SEG
TAPS = 31
PAD = TAPS // 2
SEGP = SEG + 2 * PAD
NG = 4
GT = 4
HG = 8
NW = 4
RATE = [0.9, 1.1, 2.5, 2.2, 0.85]
WAIT = [4, 11, 3]
CONV = ["dve", "pool", "dve", "dve", "pool", "dve", "dve", "pe"]
BY_HALVES, FROM_MEAN, MEAN_OF, SHIFT_AT = (4, 6), (6,), (0, 1, 2), 7
LN_AT = (18, 20, 9)
AHEAD = 2.5
SKEW = (2, 4)
LATER = (3, 2)

VECS = [("norm_w", 8), ("b_gate", 4), ("gla_nw", 2), ("lb", 4), ("hgrn_nw", 1), ("mem_nw", 8), ("x_nw", 1),
        ("fin_w", 8), ("c", 8), ("b_mod", 48), ("n1", 8), ("n2", 8), ("fin_g", 8), ("b_pw1", 16),
        ("w_dw", 8 * TAPS), ("b_dw", 8), ("ln_g", 8), ("ln_b", 8), ("b_pw2", 8)]
VOFF, _o = {}, 0
for _n, _c in VECS:
    VOFF[_n] = _o
    _o += _c
NV = _o


def unit_plan():
    plan = [("glr",)]
    for h in range(4):
        plan += [("gq", h), ("gk", h), ("gv", h, 0), ("gv", h, 1)]
        if h == 0:
            plan += [("mk", i) for i in range(4)] + [("mv", i) for i in range(4)]
    for p in range(2):
        for h in (2 * p, 2 * p + 1):
            plan += [("hq", h), ("hf", h)]
        plan += [("hi", p, 0), ("hi", p, 1)]
    plan += [("xq", h) for h in range(4)]
    plan += [("gate", e) for e in range(5)]
    for g in range(NG):
        plan += [("wo", g, j) for j in range(4)]
        plan += [("gate", e) for e in range(4 * g + 5, min(4 * g + 9, 16))]
    for f in range(8):
        plan += [("pa", f), ("pg", f)]
    plan += [("pw2", f) for f in range(8)]
    plan += [("w1", i) for i in range(GT)]
    for g in range(HG):
        if g + 1 < HG:
            plan += [("w1", (g + 1) * GT + i) for i in range(GT)]
        plan += [("w2", g, j) for j in range(4)]
    return plan


UNITS = unit_plan()


class Op:
    def __init__(self, q, fn, waits):
        self.q, self.fn, self.waits, self.needed, self.count = q, fn, waits, False, 0


class Dma:
    def __init__(self, sem, count):
        self.sem, self.count = sem, count


def flat(ws):
    for w in ws:
        if w is None:
            continue
        if isinstance(w, (list, tuple)):
            yield from flat(w)
        else:
            yield w


class Queue:

    def __init__(self, sem):
        self.sem, self.ops = sem, []

    def __call__(self, fn, *waits):
        ws = list(flat(waits))
        for w in ws:
            if isinstance(w, Op):
                w.needed = True
        op = Op(self, fn, ws)
        self.ops.append((op, None))
        return op

    def dma(self, chan, fn, *waits):
        ws = list(flat(waits))
        for w in ws:
            if isinstance(w, Op):
                w.needed = True
        op = Op(self, fn, ws)
        chan.count += 16
        self.ops.append((op, chan.sem))
        return Dma(chan.sem, chan.count)

    def number(self):
        n = 0
        for op, sem in self.ops:
            if sem is None and op.needed:
                n += 1
            op.count = n

    def emit(self, eng):
        seen = {}
        for op, dsem in self.ops:
            for w in op.waits:
                sem = w.sem if isinstance(w, Dma) else w.q.sem
                if seen.get(id(sem), 0) < w.count:
                    eng.wait_ge(sem, w.count)
                    seen[id(sem)] = w.count
            ins = op.fn(eng)
            if dsem is not None:
                ins.then_inc(dsem, 16)
            elif op.needed:
                ins.then_inc(self.sem, 1)


class Chan:
    def __init__(self, sem):
        self.sem, self.count = sem, 0


class Ring:

    def __init__(self, items):
        self.items, self.n, self.free = items, 0, [None] * len(items)

    def take(self):
        i = self.n % len(self.items)
        self.n += 1
        return i, self.items[i], self.free[i]


def build_program(nc, wall, wmod, xT, memT, vecs, gup, ident_d, masks_d, out, oscr):
    es = ExitStack()
    with es:
        size = {F32: 4, F32R: 4, U8: 1}
        base = [16512]
        END = 229344

        def at(name, cols, dt, off):
            assert off + cols * size[dt] <= END, (name, off + cols * size[dt] - END)
            return nc.alloc_sbuf_tensor_at(name, [128, cols], dt, offset=off)

        def take(name, cols, dt=F32):
            o = base[0]
            base[0] += (cols * size[dt] + 31) // 32 * 32
            return at(name, cols, dt, o)

        hb0 = base[0]
        HB = take("HB", 2 * 8 * T, F32R)
        WH = take("WH", NW * 1024, F32R)
        wl0 = base[0]
        WL = take("WL", NW * 1024, F32R)
        RAW = at("RAW", NW * 1024, F32, wl0)
        ident = take("ident", 128)
        ones = take("ones", 128)
        masks = take("masks", 7 * 256, U8)
        vec = take("vec", NV)
        small = take("small", 176)
        modv = take("modv", 48)
        res0 = base[0]
        RES = take("RES", 8 * T)
        x0 = base[0]
        K4 = 4096

        BANKS = [es.enter_context(nc.psum_tensor(f"B{i}", [128, 512], F32))[:, :] for i in range(8)]

        def sem(name):
            return es.enter_context(nc.semaphore(name))

        PE, AC, DV, PO, SP = (Queue(sem(f"s_{n}")) for n in ("pe", "act", "dve", "pool", "sp"))
        G, S, O = Ring(BANKS[0:3]), Ring(BANKS[3:6]), Ring(BANKS[6:8])

        def chan(name):
            return Chan(sem(name))

        def vcol(name, i=0):
            o = VOFF[name] + i
            return vec[:, o:o + 1]

        def vcols(name, n):
            o = VOFF[name]
            return vec[:, o:o + n]

        def copy(o, i, *w, scale=None):
            if scale is None:
                return AC(lambda e: e.activation(o, i, ACT.Copy), *w)
            return AC(lambda e: e.activation(o, i, ACT.Copy, scale=scale), *w)

        def act(o, i, f, *w, **kw):
            return AC(lambda e: e.activation(o, i, f, **kw), *w)

        def tt(o, a, b, op, *w, q=None):
            return (q or DV)(lambda e: e.tensor_tensor(o, a, b, op), *w)

        def ts(o, a, s1, s2, op0, op1, *w, q=None):
            if s2 is None:
                return (q or DV)(lambda e: e.tensor_scalar(o, a, s1, None, op0), *w)
            return (q or DV)(lambda e: e.tensor_scalar(o, a, s1, s2, op0, op1), *w)

        def stt(o, a, s, b, op0, op1, *w):
            return DV(lambda e: e.scalar_tensor_tensor(out=o, in0=a, scalar=s, in1=b, op0=op0, op1=op1), *w)

        def mm(o, l, r, st, sp, *w, skip=False):
            return PE(lambda e: e.matmul(o, l, r, start=st, stop=sp, skip_group_check=skip), *w)

        def tr(o, i, *w):
            return PE(lambda e: e.transpose(o, i, ident[:, :]), *w)

        t_ident = SP.dma(chan("d_ident"), lambda e: e.dma_start(ident[:, :], ident_d))
        t_vec = SP.dma(chan("d_vec"), lambda e: e.dma_start(vec[:, :], vecs))
        t_ones = PO(lambda e: e.memset(ones[:, :], 1.0))
        mhalf = small[:, 0:8]
        t_mh = PO(lambda e: e.memset(mhalf, -0.5))

        raw_ch = [chan(f"d_raw{i}") for i in range(NW)]
        n_units = len(UNITS)
        load_tok, split_tok, done_tok = {}, {}, {}
        hi_by = [AC]
        at_unit = [0]

        def u_split():
            q = len(split_tok)
            while len(load_tok) <= q:
                u_load()
            s = slice(q % NW * 1024, q % NW * 1024 + 1024)
            raw, hi, lo = RAW[:, s], WH[:, s], WL[:, s]
            if hi_by[0] is AC:
                th = copy(hi, raw, load_tok[q], done_tok.get(q - NW))
            else:
                th = ts(hi, raw, 1.0, 0.0, ALU.mult, ALU.add, load_tok[q], done_tok.get(q - NW), q=PO)
            tl = tt(lo, raw, hi.bitcast(F32), ALU.subtract, load_tok[q], th, q=PO)
            split_tok[q] = (hi, lo, th, tl)
            now["pool"] += 2.3

        def u_advance(j):
            while len(load_tok) < min(n_units, j + NW) and (len(load_tok) < NW or len(load_tok) - NW in done_tok):
                u_load()
            while len(split_tok) < min(n_units, j + 3, len(load_tok)):
                u_split()

        def u_load():
            q = len(load_tok)
            raw = RAW[:, q % NW * 1024:q % NW * 1024 + 1024]
            load_tok[q] = SP.dma(raw_ch[q % NW], lambda e: e.dma_start(raw, wall[q, :, :]), done_tok.get(q - NW))

        def u_get(*kind):
            j = at_unit[0]
            assert UNITS[j] == kind, (UNITS[j], kind)
            at_unit[0] += 1
            u_advance(j)
            return (j,) + split_tok[j]

        def u_done(j, tok):
            done_tok[j] = tok
            u_advance(at_unit[0] - 1)

        bg, bg2 = [], []
        credit = [0.0]
        rate = [0.5]
        turn = [0]

        def tick(us):
            credit[0] += rate[0] * us
            while credit[0] >= 1.0 and (bg or bg2):
                credit[0] -= 1.0
                step()
            if not (bg or bg2):
                credit[0] = min(credit[0], 1.0)
            now["pe"] += us
            for lane in lanes:
                while lanes[lane] and now[lane] < now["pe"] + AHEAD:
                    lane_step(lane)

        lanes = {"dve": [], "pool": []}
        now = {"pe": 0.0, "dve": 0.0, "pool": 0.0}

        def lane_add(lane, work):
            if not lanes[lane]:
                now[lane] = max(now[lane], now["pe"])
            lanes[lane].append(work)

        def lane_step(lane):
            try:
                now[lane] += next(lanes[lane][0])
            except StopIteration:
                lanes[lane].pop(0)

        def lanes_step():
            lane = min((x for x in lanes if lanes[x]), key=lambda x: now[x])
            lane_step(lane)

        def step():
            turn[0] += 1
            lane = bg2 if (bg2 and turn[0] % 2) or not bg else bg
            step_in(lane)

        def step_in(lane):
            try:
                next(lane[0])
            except StopIteration:
                lane.pop(0)

        def drain(upto=0):
            while len(bg) > upto:
                step()
            while bg2 and not upto:
                step_in(bg2)

        PASS = 0.2133

        def gemm(outs, w, wt, rhs, rt, nk):
            hi, lo, th, tl = w
            toks = {}
            for k in range(nk):
                for n, (a, b, ta) in enumerate(((hi, 0, th), (hi, 1, th), (lo, 0, tl))):
                    for h, ps, free in outs:
                        toks[h] = mm(ps, wt(a, k), rhs(b, k, h), k == 0 and n == 0, k == nk - 1 and n == 2,
                                     ta, rt(b, k, h), free)
                tick(3 * PASS * len(outs))
            return toks

        def unit_k(a, k):
            return a[:, k * 128:(k + 1) * 128]

        hbt = {}

        def hb(part, k, h=None):
            o = part * 8 * T + k * T
            return HB[:, o:o + T] if h is None else HB[:, o + h * 512:o + h * 512 + 512]

        def hb_tok(part, k, h):
            return hbt[k, h][part]

        def gemm_units(ws, outs, wt, rhs, rt, nk):
            toks = [None] * len(ws)
            for k in range(nk):
                for u, ((hi, lo, th, tl), (h, ps, free)) in enumerate(zip(ws, outs)):
                    for n, (a, b, ta) in enumerate(((hi, 0, th), (hi, 1, th), (lo, 0, tl))):
                        toks[u] = mm(ps, wt(a, k), rhs(b, k, h), k == 0 and n == 0, k == nk - 1 and n == 2,
                                     ta, rt(b, k, h), free)
                    tick(3 * PASS)
            return toks

        def project(kind, evac, before=None):
            j, *w = u_get(*kind)
            held = []
            for h in range(2):
                i, bank, free = G.take()
                tok = gemm([(h, bank, free)], w, unit_k, hb, hb_tok, 8)[h]
                if before is None:
                    G.free[i] = evac(h, bank, tok)
                else:
                    held.append((h, bank, tok, i))
            u_done(j, tok)
            if before is not None:
                before()
                for h, bank, tok, i in held:
                    G.free[i] = evac(h, bank, tok)
            return tok

        def cut(x, h):
            return x[:, h * 512:(h + 1) * 512]

        def one_unit(kind, tiles, rhs, rt, nk, evac):
            j, *w = u_get(*kind)
            for f, wt in tiles:
                got = [(h,) + B.take() for h in range(2)]
                toks = gemm([(h, bank, free) for h, i, bank, free in got], w, wt, rhs, rt, nk)
                if (f, wt) == tiles[-1]:
                    u_done(j, toks[1])
                for h, i, bank, free in got:
                    B.free[i] = evac(f, h, bank, toks[h])
            return toks[1]

        def by_halves(units, rhs, rt, nk, evac, between=None, outer=False):
            got = [u_get(*kind) for kind, _ in units]
            for h in range(2):
                if outer:
                    bs = [B.take() for _ in got]
                    toks = gemm_units([w for j, *w in got], [(h, bank, free) for i, bank, free in bs], unit_k, rhs, rt, nk)
                    for (j, *w), (kind, tiles), (i, bank, free), tok in zip(got, units, bs, toks):
                        B.free[i] = evac(tiles[0][0], h, bank, tok)
                        if h:
                            u_done(j, tok)
                else:
                    for (j, *w), (kind, tiles) in zip(got, units):
                        for f, wt in tiles:
                            i, bank, free = B.take()
                            tok = gemm([(h, bank, free)], w, wt, rhs, rt, nk)[h]
                            B.free[i] = evac(f, h, bank, tok)
                        if h:
                            u_done(j, tok)
                if h == 0 and between:
                    between()
            return tok

        def sums(acc, tacc, tiles=range(NT), into=None, first=True, last=True):
            i, bank, free = into or S.take()
            for t in tiles:
                tok = mm(bank[:, t:t + 1], acc[:, t * 128:(t + 1) * 128], ones[:, 0:1],
                         first and (into is None or t == tiles[0]), last, tacc, t_ones, free, skip=True)
            now["pe"] += PASS * len(tiles)
            return i, bank[:, tiles[0]:tiles[-1] + 1], tok

        def inv_root(o, i, div, *w):
            n = o.shape[1]
            a = ts(o, i, 1.0 / div, EPS, ALU.mult, ALU.add, *w)
            return a, PO(lambda e: e.tensor_tensor(o, o, mhalf[:, 0:n], ALU.pow), a, t_mh)

        def spread(r, tr_, dg, take, *w):
            n = r.shape[1]
            td = tt(dg.rearrange("p (c n) -> p c n", c=n), ident[:, :].unsqueeze(1).to_broadcast([128, n, 128]),
                    r.unsqueeze(2).to_broadcast([128, n, 128]), ALU.mult, tr_, t_ident, *w)
            i, ps, free = take()
            for h in range(n // 4):
                tok = mm(ps[:, h * 512:h * 512 + 512], ones[:, :], dg[:, h * 512:h * 512 + 512], True, True,
                         td, t_ones, free)
            return i, ps, tok

        xr = [RES[:, k * T:(k + 1) * T] for k in range(8)]
        o = x0
        R = at("R", 1024, F32, o)
        sq = [at(f"p0sq{i}", 1024, F32, o + i * K4) for i in (1, 2, 4, 5)]
        acc0, acc1 = at("p0acc0", 1024, F32, o + 3 * K4), at("p0acc1", 1024, F32, o + 6 * K4)
        dg0 = at("p0dg", 1024, F32, o + 4 * K4)
        macc, msq, mdg, mtm = (at(f"mem{i}", 256, F32, o + 8 * K4 + i * 1024) for i in range(4))
        mraw = at("mraw", 8 * 256, F32, o + 9 * K4)
        mhi = at("mhi", 8 * 256, F32R, o + 11 * K4)
        mlo = at("mlo", 8 * 256, F32R, o + 15 * K4)
        mst = at("mst", 448, F32, o + 17 * K4)
        gupt = at("gupt", 512, F32, o + 17 * K4 + 2048)

        x_ch = [chan(f"d_x{k}") for k in range(8)]
        t_x = [None] * 8

        def load_x(k):
            t_x[k] = SP.dma(x_ch[k], lambda e: e.dma_start(xr[k], xT[:, k, :]))

        load_x(0)
        u_load()
        load_x(1)
        load_x(2)
        u_load()
        for k in range(3, 8):
            load_x(k)
        t_mem = SP.dma(chan("d_mem"), lambda e: e.dma_start(mraw[:, :], memT))
        u_load()
        t_mst = SP.dma(chan("d_mask"), lambda e: e.dma_start(mst[:, :], masks_d))
        t_gup = SP.dma(chan("d_gup"), lambda e: e.dma_start(gupt[0:16, :], gup))
        u_load()

        sqf, ta = [None] * 4, [None, None]
        for k in range(8):
            w = vcol("norm_w", k)
            if k % 2:
                th = ts(hb(0, k), xr[k], w, 0.0, ALU.mult, ALU.add, t_x[k], t_vec, q=PO)
            else:
                th = copy(hb(0, k), xr[k], t_x[k], t_vec, scale=w)
            tl = stt(hb(1, k), xr[k], w, hb(0, k).bitcast(F32), ALU.mult, ALU.subtract, th)
            hbt[k, 0] = hbt[k, 1] = (th, tl)
            if k in (0, 2):
                u_split()
            a, q = k % 2, (DV, PO)[k % 2]
            acc = (acc0, acc1)[a]
            if k < 2:
                ta[a] = act(acc[:, :], xr[k], ACT.Square, t_x[k])
                continue
            i = 2 * a + k // 2 % 2
            t = act(sq[i][:, :], xr[k], ACT.Square, t_x[k], sqf[i])
            ta[a] = sqf[i] = tt(acc[:, :], acc[:, :], sq[i][:, :], ALU.add, t, ta[a], q=q)
        hi_by[0] = PO
        last_x = [hbt[6, 0], hbt[7, 0], ta]
        xr_r = small[:, 16:24]
        t_R = [None]

        def x_stats():
            into = S.take()
            sums(acc0, ta[0], range(8), into, True, False)
            i, ss, tp = sums(acc1, ta[1], range(8), into, False, True)
            S.free[i], tr_ = inv_root(xr_r, ss, D, tp)
            for _ in range(4):
                yield
            td = tt(dg0[:, :].rearrange("p (c n) -> p c n", c=8), ident[:, :].unsqueeze(1).to_broadcast([128, 8, 128]),
                    xr_r.unsqueeze(2).to_broadcast([128, 8, 128]), ALU.mult, tr_, t_ident)
            yield
            yield
            for h in range(2):
                oi, ob, free = S.take()
                tok = mm(ob[:, :], ones[:, :], dg0[:, h * 512:h * 512 + 512], True, True, td, t_ones, free)
                t_R[0] = S.free[oi] = copy(R[:, h * 512:h * 512 + 512], ob[:, :], tok)

        for l in range(7):
            t_mask = DV(lambda e, l=l: e.tensor_copy(masks[:, l * 256:(l + 1) * 256].rearrange("p (c n) -> p c n", c=4),
                                                     mst[:, l * 64:(l + 1) * 64].unsqueeze(1).to_broadcast([128, 4, 64])),
                        t_mst)

        mt = [None] * 8

        def mem_norm():
            ta = None
            for k in range(8):
                m = mraw[:, k * 256:(k + 1) * 256]
                if k == 0:
                    ta = act(macc[:, :], m, ACT.Square, t_mem)
                else:
                    tq = act(msq[:, :], m, ACT.Square, ta)
                    ta = tt(macc[:, :], macc[:, :], msq[:, :], ALU.add, tq, ta)
            yield
            yield
            si, bank, free = S.take()
            for t in range(2):
                tp = mm(bank[:, t:t + 1], macc[:, t * 128:(t + 1) * 128], ones[:, 0:1], True, True, ta, t_ones, free)
            mr = small[:, 8:10]
            t1 = ts(mr, bank[:, 0:2], 1.0 / D, EPS, ALU.mult, ALU.add, tp)
            S.free[si] = t1
            t2 = PO(lambda e: e.tensor_tensor(mr, mr, mhalf[:, 0:2], ALU.pow), t1, t_mh)
            yield
            yield
            yield
            td = tt(mdg[:, :].rearrange("p (c n) -> p c n", c=2), ident[:, :].unsqueeze(1).to_broadcast([128, 2, 128]),
                    mr.unsqueeze(2).to_broadcast([128, 2, 128]), ALU.mult, t2, t_ident)
            yield
            si, bank, free = S.take()
            tR = mm(bank[:, 0:256], ones[:, :], mdg[:, :], True, True, td, free)
            tl = None
            for k in range(8):
                m = mraw[:, k * 256:(k + 1) * 256]
                h_, l_ = mhi[:, k * 256:(k + 1) * 256], mlo[:, k * 256:(k + 1) * 256]
                t1 = stt(mtm[:, :], m, vcol("mem_nw", k), bank[:, 0:256], ALU.mult, ALU.mult, tR, t_vec, tl)
                th = copy(h_, mtm[:, :], t1)
                tl = tt(l_, mtm[:, :], h_.bitcast(F32), ALU.subtract, th)
                mt[k] = (th, tl)
            S.free[si] = tl

        o = x0 + K4
        KT_ = at("KT", 1024, F32, o + 0 * K4)
        VB = [at(f"VB{i}", 2048, F32, o + (1 + 2 * i) * K4) for i in range(2)]
        ST = at("ST", 768, F32, o + 5 * K4)
        GLR = at("GLR", 1024, F32, o + 6 * K4)
        DUMP = at("DUMP", 256, F32, x0 + 18 * K4)
        o = x0 + 36 * 1024
        OSB = at("OSB", 2048, F32, o)
        OT = [at(f"OT{i}", 512, F32, o + 8192 + i * 2048) for i in range(4)]
        MK = at("MK", 1024, F32, o + 4 * K4)
        MV = at("MV", 1024, F32, o + 5 * K4)
        PP = at("PP", 768, F32, o + 6 * K4)
        PT = at("PT", 512, F32, o + 6 * K4 + 3072)
        sets = [[at(f"set{i}{n}", 1024, F32, res0 + (3 * i + a) * K4) for a, n in enumerate("qkg")] for i in range(2)]
        TB = at("TB", 1024, F32, res0 + 6 * K4)
        AB = at("AB", 1024, F32, res0 + 7 * K4)

        S = Ring(BANKS[3:5])
        rate[0] = 0.8
        j0, *w0 = u_get("glr")
        j1, *w1 = u_get("gq", 0)
        got = [G.take(), G.take(), G.take(), O.take()]
        toks = gemm_units([w0, w0, w1, w1], [(n % 2, bank, free) for n, (i, bank, free) in enumerate(got)],
                          unit_k, hb, hb_tok, 8)
        u_done(j0, toks[1])
        u_done(j1, toks[3])
        bg2 += [x_stats(), mem_norm()]
        step()
        j2, *w2 = u_get("gk", 0)
        got += [O.take(), (2, BANKS[5], None)]
        for h in range(2):
            toks.append(gemm([(h,) + got[4 + h][1:]], w2, unit_k, hb, hb_tok, 8)[h])
        u_done(j2, toks[5])
        while t_R[0] is None or len(bg2) > 1:
            step()
        tq0, tk0 = [None] * 2, [None] * 2
        q, k, g = sets[0]
        for h in range(2):
            t_glr = G.free[h] = tt(cut(GLR[0:16, :], h), got[h][1][0:16, :], cut(R[0:16, :], h), ALU.mult, toks[h],
                                   t_R, last_x)
        for h in range(2):
            tq0[h] = stt(cut(q, h), got[2 + h][1], SCALE, cut(R, h), ALU.mult, ALU.mult, toks[2 + h], last_x)
            tk0[h] = tt(cut(k, h), got[4 + h][1], cut(R, h), ALU.mult, toks[4 + h], last_x)
        G.free[2], O.free[0], O.free[1] = tq0[0], tq0[1], tk0[0]
        S_free = S.free
        S = Ring(BANKS[3:6])
        S.free = S_free + [tk0[1]]
        p0_done = [last_x, t_R[0], t_glr]

        ot_ring = Ring(OT)
        ot_ch = [chan(f"d_ot{i}") for i in range(4)]
        ot_out = {}
        st = {"A": [p0_done] * 2, "T": [p0_done] * 2, "KT": p0_done, "OSB": [p0_done] * 2, "ST": [p0_done] * 3,
              "SS": [None] * 2, "PP": [p0_done] * 3, "PT": [p0_done] * 2}
        SS = small[:, 32:40]
        RS = small[:, 40:48]
        fin_n = [0, 0]

        def finish(hh, dv, nw, e0, t_ss, t_o):
            cs = slice(4 * hh, 4 * hh + 4)
            a, tr_ = inv_root(RS[:, cs], SS[:, cs], dv, t_ss, st["SS"][hh])
            for _ in range(LATER[0]):
                yield
            tsc = []
            for i in range(4):
                c = 4 * hh + i
                ob = OSB[:, c * dv:(c + 1) * dv]
                tsc.append(ts(ob, ob, RS[:, c:c + 1], None, ALU.mult, None, tr_, t_o[i], t_ss))
            st["SS"][hh] = tsc[-1]
            for _ in range(LATER[1]):
                yield
            for f in range(dv // 128):
                oi, ot, ofree = ot_ring.take()
                si, bank, free = S.take()
                for i in range(4):
                    c = 4 * hh + i
                    tp = tr(bank[:, i * 128:(i + 1) * 128], OSB[:, c * dv + f * 128:c * dv + f * 128 + 128],
                            tsc[i], t_ident, free)
                te = copy(ot[:, :], bank[:, :], tp, ofree, t_vec, scale=nw(f))
                S.free[si] = te
                e = e0 + f
                ot_out[e, hh] = SP.dma(ot_ch[oi], lambda g, e=e, ot=ot: g.dma_start(
                    oscr[e, :, hh * 512:(hh + 1) * 512], ot[:, :]), te)
                ot_ring.free[oi] = ot_out[e, hh]
                if f == dv // 128 - 1:
                    st["OSB"][hh] = tp
                    fin_n[hh] += 1
                yield

        started = [0, 0]

        def finish_later(hh, *a):
            started[hh] += 1
            bg2.append(finish(hh, *a))

        def osb_ready(hh):
            while fin_n[hh] < started[hh]:
                step_in(bg2)

        def linear(s, tq, tk, tg, vb, v0, dv, tv, nw, e0, freed):
            q, k, g = sets[s]

            def ch(b, c):
                return b[:, c * 128:(c + 1) * 128]

            def half(b, hh):
                return b[:, hh * 512:(hh + 1) * 512]

            t_a, t_q, t_k, t_t = [None] * 2, [None] * 2, list(tk), [tg, tg]
            tcur = [half(g, 0), half(g, 1)]
            toff = [0, 512]
            for hh in range(2):
                si, bank, free = S.take()
                for i in range(4):
                    c = 4 * hh + i
                    tp = mm(ch(bank, i), ch(k, c), ch(q, c), True, True, tq[hh], tk[hh], free)
                t_q[hh] = tt(half(q, hh), half(q, hh), half(g, hh), ALU.mult, tp, tg, tq[hh])
                t_a[hh] = tt(half(AB, hh).rearrange("p (c n) -> p c n", c=4),
                             bank[:, :].rearrange("p (c n) -> p c n", c=4),
                             ident[:, :].unsqueeze(1).to_broadcast([128, 4, 128]), ALU.mult, tp, t_ident, st["A"][hh])
                S.free[si] = t_a[hh]
                yield
            for l in range(7):
                H = 1 << l
                nb = 256 // H
                for hh in range(2):
                    si, bank, free = S.take()
                    for i in range(4):
                        c = 4 * hh + i
                        rhs = ch(q, c).rearrange("p (n t h) -> p n t h", t=2, h=H)[:, :, 1, :]
                        m = 64 if l == 6 else 128
                        tp = mm(bank[0:m, i * 64:(i + 1) * 64], ch(k, c)[:, 0:m], rhs, True, True, t_q[hh], t_k[hh], free)
                    tv2 = tcur[hh].rearrange("p (n t) -> p n t", t=2)
                    qv = half(q, hh).rearrange("p (n t h) -> p n t h", t=2, h=H)[:, :, 1, :]
                    kv = half(k, hh).rearrange("p (n t h) -> p n t h", t=2, h=H)[:, :, 0, :]
                    t_q[hh] = tt(qv, qv, tv2[:, :, 0:1].to_broadcast([128, nb, H]), ALU.mult, tp, t_q[hh], t_t[hh])
                    t_k[hh] = tt(kv, kv, tv2[:, :, 1:2].to_broadcast([128, nb, H]), ALU.mult, tp, t_k[hh], t_t[hh])
                    nxt = TB[:, toff[hh]:toff[hh] + nb]
                    t_t[hh] = tt(nxt.unsqueeze(2), tv2[:, :, 0:1], tv2[:, :, 1:2], ALU.mult, t_t[hh], st["T"][hh])
                    tcur[hh], toff[hh] = nxt, toff[hh] + nb
                    av = half(AB, hh).rearrange("p (n t h) -> p n t h", t=2, h=H)[:, :, 1, :]
                    mv = masks[:, l * 256:(l + 1) * 256].rearrange("p (n h) -> p n h", h=H)
                    bv = bank[:, 0:256].rearrange("p (n h) -> p n h", h=H)
                    if l == 6:
                        t_a[hh] = DV(lambda e, av=av, bv=bv: e.tensor_copy(av[0:64], bv[0:64]), tp, t_a[hh])
                    else:
                        t_a[hh] = DV(lambda e, av=av, mv=mv, bv=bv: e.copy_predicated(av, mv, bv), tp, t_a[hh], t_mask)
                    S.free[si] = t_a[hh]
                    yield
            t_kt = [None] * 2
            for hh in range(2):
                si, bank, free = S.take()
                for i in range(4):
                    tp = tr(ch(bank, i), ch(k, 4 * hh + i), t_k[hh], t_ident, free)
                t_kt[hh] = copy(half(KT_, hh), bank[:, :], tp, st["KT"])
                S.free[si] = t_kt[hh]
                yield
            t_s, s_old, t_o, t_ss = None, None, [], None
            for c in range(8):
                hh = c // 4
                if c % 4 == 0:
                    osb_ready(hh)
                    t_o = []
                vc = vb[:, c * 256 + v0:c * 256 + v0 + dv]
                if c < 7:
                    oi, kvb, free = O.take()
                    tkv = mm(kvb[:, 0:dv], ch(KT_, c), vc, True, True, t_kt[hh], tv, free)
                    new = ST[:, (c % 3) * 256:(c % 3) * 256 + dv]
                    if c == 0:
                        t_n = DV(lambda e, new=new, kvb=kvb: e.tensor_copy(new, kvb[:, 0:dv]), tkv, st["ST"][0])
                    else:
                        t_n = stt(new, s_old, tcur[hh][:, c % 4:c % 4 + 1], kvb[:, 0:dv], ALU.mult, ALU.add, tkv, t_s,
                                  t_t[hh], st["ST"][c % 3])
                    O.free[oi] = t_n
                oi, ob, free = O.take()
                tp = mm(ob[:, 0:dv], ch(AB, c), vc, True, c == 0, t_a[hh], tv, free)
                if c:
                    tp = mm(ob[:, 0:dv], ch(q, c), s_old, False, True, t_s, t_q[hh])
                    st["ST"][(c - 1) % 3] = [tp, t_n if c < 7 else None]
                if c < 7:
                    s_old, t_s = new, t_n
                os_ = OSB[:, c * dv:(c + 1) * dv]
                t_c = copy(os_, ob[:, 0:dv], tp, st["OSB"])
                O.free[oi] = t_c
                t_ss = AC(lambda e, os_=os_, c=c: e.activation(DUMP[:, 0:dv], os_, ACT.Square,
                                                               accum_out=SS[:, c:c + 1]), t_c, st["SS"][hh], p0_done)
                t_o.append(t_c)
                st["A"][hh] = tp
                if c % 4 == 3:
                    finish_later(hh, dv, nw, e0, t_ss, t_o)
                yield
            st["KT"], st["T"] = tkv, [[t_t, t_n]] * 2
            freed(tp)

        def cross(h, s, tq):
            q = sets[s][0]
            NM = small[:, 48:56]
            SE = small[:, 56:64]
            got = {}

            def scores(t):
                si, bank, free = S.take()
                tp = mm(bank[:, 0:256], q[:, t * 128:(t + 1) * 128], MK[:, h * 256:(h + 1) * 256], True, True,
                        tq[t // 4], t_mk[h], free)
                nm, se = NM[:, t:t + 1], SE[:, t:t + 1]
                t2 = DV(lambda e: e.tensor_reduce(nm, bank[:, 0:256], AXX, ALU.min), tp, st["SS"])
                p = PP[:, t % 3 * 256:t % 3 * 256 + 256]
                te = AC(lambda e: e.activation(p, bank[:, 0:256], ACT.Exp, bias=nm, scale=-1.0, accum_out=se),
                        t2, st["PP"][t % 3], st["SS"])
                S.free[si] = te
                t3 = DV(lambda e: e.reciprocal(se, se), te)
                got[t] = (p, te, t3, se)
                return tp

            def turned(t):
                p, te, t3, se = got[t]
                pt = PT[:, t % 2 * 256:t % 2 * 256 + 256]
                si, bank, free = S.take()
                for m in range(2):
                    tp = tr(bank[:, m * 128:(m + 1) * 128], p[:, m * 128:(m + 1) * 128], te, t_ident, free)
                st["PP"][t % 3] = tp
                tpt = copy(pt, bank[:, 0:256], tp, st["PT"][t % 2])
                S.free[si] = tpt
                got[t] = (pt, tpt, t3, se)

            def values_of(t, t_o):
                pt, tpt, t3, se = got[t]
                oi, ob, free = O.take()
                for m in range(2):
                    tp = mm(ob[:, 0:128], pt[:, m * 128:(m + 1) * 128], MV[:, m * 512 + h * 128:m * 512 + h * 128 + 128],
                            m == 0, m == 1, tpt, t_mv, free)
                st["PT"][t % 2] = tp
                os_ = OSB[:, t * 128:(t + 1) * 128]
                t4 = copy(os_, ob[:, 0:128], tp, t3, st["OSB"], scale=se)
                O.free[oi] = t4
                t_ss = AC(lambda e: e.activation(DUMP[:, 0:128], os_, ACT.Square, accum_out=SS[:, t:t + 1]),
                          t4, st["SS"])
                t_o.append(t4)
                return t_ss

            for t in range(8 + SKEW[1]):
                v = t - SKEW[1]
                if v >= 0:
                    if v in (0, 4):
                        osb_ready(v // 4)
                        t_o = []
                    t_ss = values_of(v, t_o)
                    if v in (3, 7):
                        finish_later(v // 4, 128, lambda f: vcol("x_nw"), 12 + h, t_ss, t_o)
                    yield
                if 0 <= t - SKEW[0] < 8:
                    turned(t - SKEW[0])
                if t < 8:
                    tp = scores(t)
                yield
            set_free[s] = tp

        set_free = [p0_done, p0_done]
        v_free = [p0_done, p0_done]

        def values(name, i, vslot):
            ja, *wa = u_get(name, i, 0)
            jb, *wb = u_get(name, i, 1)
            vb = VB[vslot]
            for hf in range(4):
                gi, ps, free = G.take()
                for tl_ in range(2):
                    t = 2 * hf + tl_
                    for k in range(8):
                        hi, lo, th, tl = wa if k < 4 else wb
                        for n, (a, b, tb) in enumerate(((0, hi, th), (1, hi, th), (0, lo, tl))):
                            tok = mm(ps[:, tl_ * 256:(tl_ + 1) * 256], hb(a, k)[:, t * 128:(t + 1) * 128],
                                     b[:, (k % 4) * 256:(k % 4 + 1) * 256], k == 0 and n == 0, k == 7 and n == 2,
                                     tb, hbt[k, 0][a], free)
                        tick(3 * PASS / 2)
                if hf == 3:
                    u_done(ja, tok)
                    u_done(jb, tok)
                for tl_ in range(2):
                    t = 2 * hf + tl_
                    tv = copy(vb[:, t * 256:(t + 1) * 256], ps[:, tl_ * 256:(tl_ + 1) * 256], tok, v_free[vslot], t_R,
                              scale=xr_r[:, t:t + 1])
                G.free[gi] = tv
            return tv

        t_mk, t_mv = [], []

        def memory():
            while bg2:
                step_in(bg2)
            def m_rhs(part, k):
                return (mhi, mlo)[part][:, k * 256:(k + 1) * 256]

            
            mk_w = [mt, t_mask]
            for h in range(4):
                j, hi, lo, th, tl = u_get("mk", h)
                gi, ps, free = G.take()
                for k in range(8):
                    tick(3 * PASS / 2)
                    for n, (a, b) in enumerate(((hi, 0), (hi, 1), (lo, 0))):
                        tok = mm(ps[:, 0:256], unit_k(a, k), m_rhs(b, k), k == 0 and n == 0, k == 7 and n == 2,
                                 th if a is hi else tl, mt[k], free)
                u_done(j, tok)
                G.free[gi] = copy(MK[:, h * 256:(h + 1) * 256], ps[:, 0:256], tok, last_x, mk_w)
                t_mk.append(G.free[gi])
            mv_b = [G.take() for m in range(2)]
            for u in range(4):
                j, hi, lo, th, tl = u_get("mv", u)
                for kk in range(2):
                    k = 2 * u + kk
                    for m in range(2):
                        tick(3 * PASS)
                        for n, (a, b) in enumerate(((0, hi), (1, hi), (0, lo))):
                            tok = mm(mv_b[m][1],
                                     (mhi, mlo)[a][:, k * 256 + m * 128:k * 256 + m * 128 + 128],
                                     b[:, kk * 512:(kk + 1) * 512], k == 0 and n == 0, k == 7 and n == 2,
                                     th if b is hi else tl, mt[k], mv_b[m][2])
                u_done(j, tok)
            for m in range(2):
                G.free[mv_b[m][0]] = copy(cut(MV, m), mv_b[m][1], tok, last_x, mk_w)
            mem_done = [tok, mt]
            t_mv.append([G.free[i] for i, bank, free in mv_b])
            ot_ring.free = [[p0_done, mem_done]] * 4
            st["OSB"] = [[p0_done, mem_done]] * 2
            st["PP"], st["PT"] = [mem_done] * 3, [mem_done] * 2

        rate[0] = RATE[0]
        nset = 0
        for h in range(4):
            s = nset % 2
            nset += 1
            q, k, g = sets[s]

            def q_out(hf, bank, tok):
                return stt(cut(q, hf), bank, SCALE, cut(R, hf), ALU.mult, ALU.mult, tok, set_free[s], t_R)

            def k_out(hf, bank, tok):
                return tt(cut(k, hf), bank, cut(R, hf), ALU.mult, tok, set_free[s], t_R)

            tqs, tks, ups = [None] * 2, [None] * 2, []

            def keep(into, f):
                def evac(hf, bank, tok):
                    into[hf] = f(hf, bank, tok)
                    return into[hf]
                return evac

            if h == 0:
                tqs, tks = tq0, tk0
            else:
                project(("gq", h), keep(tqs, q_out), lambda: drain(1))
            b = vcol("b_gate", h)
            for hf in range(2):
                gi, ps, free = G.take()
                tok = mm(ps, gupt[0:16, h * 128:(h + 1) * 128], GLR[0:16, hf * 512:(hf + 1) * 512], True, True,
                         t_glr, t_gup, free)
                t1 = act(cut(g, hf), ps, ACT.Abs, tok, set_free[s], bias=b)
                t2 = ts(ps, ps, b, 0.0, ALU.add, ALU.min, tok, t1)
                ups.append((gi, ps, t1, t2))
            t1 = act(g[:, :], g[:, :], ACT.Exp, ups[0][2], t1, scale=-1.0)
            t1 = act(g[:, :], g[:, :], ACT.Ln, t1, bias=1.0)
            for hf, (gi, ps, _, t2) in enumerate(ups):
                t3 = G.free[gi] = tt(cut(g, hf), ps, cut(g, hf), ALU.subtract, t2, t1)
            tg = act(g[:, :], g[:, :], ACT.Exp, t3, scale=1.0 / 16.0)
            if h:
                project(("gk", h), keep(tks, k_out))
            tv = values("gv", h, h % 2)
            if h == 0:
                memory()

            def freed(tok, s=s, v=h % 2):
                set_free[s] = tok
                v_free[v] = tok

            bg.append(linear(s, tqs, tks, tg, VB[h % 2], 0, 256, tv, lambda f: vcol("gla_nw", f), 2 * h, freed))

        lbw = small[:, 64:80]
        lb_ = vcols("lb", 4)
        ex, pr, om, fl = (lbw[:, 4 * i:4 * i + 4] for i in range(4))
        t1 = tt(ex, lb_, lb_, ALU.subtract, t_vec)
        t1 = act(ex, ex, ACT.Exp, t1)
        t2 = DV(lambda e: e.reciprocal(pr, ex), t1)
        t2 = tt(pr, pr, ex, ALU.mult, t2)
        t2 = tt(ex, pr, pr, ALU.subtract, t2)
        t_fl = ts(fl, ex, FLOOR, None, ALU.max, None, t2)
        t_om = ts(om, ex, -1.0, 1.0, ALU.mult, ALU.add, t2)
        rate[0] = RATE[1]
        for pr_ in range(2):
            got = []
            for i in range(2):
                h = 2 * pr_ + i
                s = nset % 2
                nset += 1
                q, k, g = sets[s]
                tqs, tzs = [None] * 2, [None] * 2

                def h_out(o, into):
                    def evac(hf, bank, tok):
                        into[hf] = tt(cut(o, hf), bank, cut(R, hf), ALU.mult, tok, set_free[s], t_R)
                        return into[hf]
                    return evac

                project(("hq", h), h_out(q, tqs), lambda: drain(1 if i == 0 else 0))
                project(("hf", h), h_out(g, tzs))
                tz = tzs
                t2 = act(k[:, :], g[:, :], ACT.Sigmoid, tz, set_free[s], scale=-1.0)
                t1 = act(g[:, :], g[:, :], ACT.Sigmoid, tz, t2)
                tg = ts(g[:, :], g[:, :], om[:, h:h + 1], fl[:, h:h + 1], ALU.mult, ALU.add, t1, t_om, t_fl)
                tk = ts(k[:, :], k[:, :], om[:, h:h + 1], None, ALU.mult, None, t2, t_om)
                got.append((s, tqs, [tk, tk], tg))
            tv = values("hi", pr_, pr_)
            for i in range(2):
                s, tq, tk, tg = got[i]

                def freed(tok, s=s, v=pr_, i=i):
                    set_free[s] = tok
                    if i:
                        v_free[v] = tok

                bg.append(linear(s, tq, tk, tg, VB[pr_], i * 128, 128, tv, lambda f: vcol("hgrn_nw"),
                                 8 + 2 * pr_ + i, freed))
        rate[0] = RATE[2]
        for h in range(4):
            s = nset % 2
            nset += 1
            tqs = [None] * 2

            def xq_out(hf, bank, tok):
                tqs[hf] = stt(cut(sets[s][0], hf), bank, -SCALE, cut(R, hf), ALU.mult, ALU.mult, tok, set_free[s], t_R)
                return tqs[hf]

            project(("xq", h), xq_out, lambda: drain(1))
            bg.append(cross(h, s, tqs))

        while len(bg) > 1:
            step()
        p2_done = [st["A"], st["KT"], st["T"], v_free, t_glr]
        tail = [None]
        xo = x0 + K4
        NM_ = 5
        GA = [at(f"GA{i}", 1024, F32, xo + i * K4) for i in range(2)]
        OI = [at(f"OI{i}", 1024, F32, xo + (2 + i) * K4) for i in range(2)]
        MX = [(at(f"MXH{i}", 1024, F32R, xo + (4 + 2 * i) * K4), at(f"MXL{i}", 1024, F32R, xo + (5 + 2 * i) * K4))
              for i in range(NM_)]
        MACC = [at(f"MACC{i}", 512, F32, xo + 14 * K4 + i * 2048) for i in range(2)]
        MRAW = at("MODRAW", 1536, F32, xo + 14 * K4 + 4096)
        ga_free, oi_free = [p2_done] * 2, [p2_done] * 2
        mx_free = [p2_done] * 2 + [None] * 3
        oi_ch = [chan("d_oi0"), chan("d_oi1")]
        mx_tok = {}

        def after_cross():
            drain()
            tail[0] = [list(ot_out.values()), st["OSB"], st["PP"], st["PT"], st["SS"], set_free]
            for i in range(2, NM_):
                mx_free[i] = [p2_done, tail[0]]

        oi_tok = {}

        def oi_load(e):
            if e < 16:
                s = e % 2
                oi_tok[e] = SP.dma(oi_ch[s], lambda g: g.dma_start(OI[s][:, :], oscr[e, :, :]), oi_free[s],
                                   ot_out[e, 0], ot_out[e, 1])

        def mixed(e, ring):
            j, *w = u_get("gate", e)
            s, m = e % 2, e % NM_
            t_oi = oi_tok[e]
            ga, oi, (hi, lo) = GA[s], OI[s], MX[m]
            freed, used = [], []
            for h in range(2):
                i, bank, free = ring.take()
                tok = gemm([(h, bank, free)], w, unit_k, hb, hb_tok, 8)[h]
                t1 = ring.free[i] = tt(cut(ga, h), bank, cut(R, h), ALU.mult, tok, ga_free[s], t_R)
                t1 = act(cut(ga, h), cut(ga, h), ACT.Silu, t1)
                t2 = tt(cut(ga, h), cut(ga, h), cut(oi, h), ALU.mult, t1, t_oi)
                th = copy(cut(hi, h), cut(ga, h), t2, mx_free[m])
                tl = tt(cut(lo, h), cut(ga, h), cut(hi, h).bitcast(F32), ALU.subtract, t2, th, mx_free[m], q=PO)
                used.append(t2)
                freed.append(tl)
                mx_tok[e, h] = (th, tl)
            u_done(j, tok)
            oi_free[s], ga_free[s] = used, freed
            oi_load(e + 2)
            return tok

        modcol = modv[:, 0:48]
        t_mod = {}
        sc = small[:, 24:32]
        mod_ch = [chan(f"d_mod{i}") for i in range(3)]
        mod_free = [None] * 3
        mod_tok = {}
        mod_st = {"acc": [None, None], "n": 0, "done": None}

        def mod_load(n):
            if n < 96:
                dst = MRAW[:, n % 3 * 512:n % 3 * 512 + 512]
                mod_tok[n] = SP.dma(mod_ch[n % 3], lambda e: e.dma_start(dst, wmod[n, :, :]), mod_free[n % 3])

        def mod_sum(last=1):
            if mod_st["done"] is None:
                return
            c, t, n = mod_st["done"]
            if n < last:
                mod_st["done"] = (c, t, n + 1)
                return
            mod_st["done"] = None
            si, bank, free = S.take()
            for f in range(4):
                tp = mm(bank[:, f:f + 1], MACC[c % 2][:, f * 128:(f + 1) * 128], ones[:, 0:1], True, True, t, free)
            cs = slice(c * 4, c * 4 + 4)
            S.free[si] = t_mod[c] = tt(modcol[:, cs], bank[:, 0:4], vcols("b_mod", 48)[:, cs], ALU.add, tp)
            mod_st["acc"][c % 2] = tp

        def mods(count):
            mod_sum()
            for n in range(mod_st["n"], min(96, mod_st["n"] + count)):
                c, k = n // 8, n % 8
                src = MRAW[:, n % 3 * 512:n % 3 * 512 + 512]
                acc, old = MACC[c % 2], mod_st["acc"][c % 2]
                if k == 0:
                    t = ts(acc[:, :], src, sc[:, 0:1], None, ALU.mult, None, mod_tok[n], t_sc, old)
                else:
                    t = stt(acc[:, :], src, sc[:, k:k + 1], acc[:, :], ALU.mult, ALU.add, mod_tok[n], old)
                mod_st["acc"][c % 2] = mod_free[n % 3] = t
                mod_load(n + 3)
                if k == 7:
                    mod_st["done"] = (c, t, 0)
            mod_st["n"] = min(96, mod_st["n"] + count)

        x_tok = [None] * 8
        res = [RES[:, f * T:(f + 1) * T] for f in range(8)]

        def rh(f, h):
            return RES[:, f * T + h * 512:f * T + h * 512 + 512]

        rt_ = {}

        def load_res(f):
            rt_[f, 0] = rt_[f, 1] = SP.dma(x_ch[f], lambda e, f=f: e.dma_start(res[f], xT[:, f, :]), p2_done, tail[0])

        sqn = {"free": [None] * 4, "n": 0, "buf": None, "late": []}

        def add_late():
            for f in sqn["late"]:
                f()
            sqn["late"] = []

        def add_sq(acc, f, h, t_acc, *w, scale=None):
            kw = {} if scale is None else {"scale": scale}
            cs = slice(h * 512, (h + 1) * 512)
            if t_acc[h] is None:
                t_acc[h] = act(acc[:, cs], rh(f, h), ACT.Square, *w, **kw)
                return
            i = sqn["n"] % len(sqn["buf"])
            sqn["n"] += 1
            b = sqn["buf"][i]
            q = act(b[:, :], rh(f, h), ACT.Square, *w, sqn["free"][i], **kw)

            def add():
                sqn["free"][i] = t_acc[h] = tt(acc[:, cs], acc[:, cs], b[:, :], ALU.add, q, t_acc[h])

            sqn["late"].append(add)

        def pair(j2):
            return [(2 * j2 + ff, lambda a, k, ff=ff: a[:, k * 256 + ff * 128:k * 256 + ff * 128 + 128]) for ff in range(2)]

        ACC1 = at("ACC1", 1024, F32, xo + 2 * K4)
        ACC2 = at("ACC2", 1024, F32, xo + 3 * K4)
        SQP = [at(f"SQP{i}", 512, F32, xo + i * 2048) for i in range(4)]
        sta, stb = [None, None], [None, None]

        def wo_rhs(g):
            return lambda part, k, h: MX[(4 * g + k) % NM_][part][:, h * 512:(h + 1) * 512]

        def wo_tok(g):
            return lambda part, k, h: mx_tok[4 * g + k, h][part]

        def wo_evac(g):
            def evac(f, h, bank, tok):
                t = rt_[f, h] = tt(rh(f, h), rh(f, h), bank, ALU.add, tok, rt_[f, h])
                add_late()
                if g == NG - 1:
                    add_sq(ACC1, f, h, sta, t, ga_free, oi_free)
                    add_sq(ACC2, f, h, stb, t, ga_free, oi_free, scale=vcol("fin_w", f))
                return t
            return evac

        rate[0] = RATE[3]
        t_sc = act(sc, vcols("c", 8), ACT.Silu, t_vec)
        oi_load(0)
        oi_load(1)
        mixed(0, G)
        mixed(1, G)
        after_cross()
        mod_free[:] = [tail[0]] * 3
        mod_st["acc"] = [tail[0], tail[0]]
        for n in range(3):
            mod_load(n)
        for e in range(2, 5):
            for f in range(3 * e - 6, min(8, 3 * e - 3)):
                load_res(f)
            mods(4)
            mixed(e, G)
        B = Ring(BANKS[0:6])
        B.free = G.free + S.free
        S = O

        R1, R2, RR, W1 = small[:, 80:88], small[:, 88:96], small[:, 96:104], small[:, 104:112]
        DG = at("DG", 1024, F32, xo + 14 * K4)
        TM = [at(f"TM{i}", 512, F32, xo + 6 * K4 + i * 2048) for i in range(4)]
        A1 = small[:, 112:120]
        tm_free, tm_n = [None] * 4, [0]
        hb_free = [None]

        def hs(x, h):
            return x[:, 4 * h:4 * h + 4]

        def modulated(h, TM, scol, shift, Rb, tR, *w):
            low = None
            for k in range(8):
                i = tm_n[0] % len(TM)
                tm_n[0] += 1
                tm, sh = TM[i], shift[:, k:k + 1]
                t1 = stt(tm[:, :], rh(k, h), scol[:, k:k + 1], Rb, ALU.mult, ALU.mult, tR, tm_free[i], rt_[k, h], *w)
                if low:
                    low()
                th = act(hb(0, k, h), tm[:, :], ACT.Identity, t1, hb_free[0], bias=sh)

                def low(k=k, tm=tm, sh=sh, i=i, t1=t1, th=th):
                    tl = stt(hb(1, k, h), tm[:, :], sh, hb(0, k, h).bitcast(F32), ALU.add, ALU.subtract, t1, th, hb_free[0])
                    tm_free[i] = tl
                    hbt[k, h] = (th, tl)

                if k == 7:
                    low()
                yield t1

        def between_blocks(h):
            for _ in range(WAIT[0] + h):
                yield
            add_late()
            si, ss, tp = sums(ACC1, sta[h], range(4 * h, 4 * h + 4))
            S.free[si], tr1 = inv_root(hs(R1, h), ss, D, tp)
            si, ss2, tp2 = sums(ACC2, stb[h], range(4 * h, 4 * h + 4))
            t1 = tt(hs(RR, h), hs(R1, h), hs(R1, h), ALU.mult, tr1)
            t2 = tt(hs(R2, h), hs(RR, h), ss2, ALU.mult, t1, tp2)
            S.free[si] = t2
            _, tr2 = inv_root(hs(R2, h), hs(R2, h), D, t2)
            t_rr = tt(hs(RR, h), hs(R1, h), hs(R2, h), ALU.mult, tr2, t2)
            for _ in range(WAIT[1]):
                yield
            si, Rb, tR = spread(hs(RR, h), t_rr, DG[:, h * 512:(h + 1) * 512], S.take, mod_st["acc"])
            for t1 in modulated(h, TM, W1, modcol[:, 0:8], Rb, tR, t_w1, t_mod[0], t_mod[1], mx_free[1]):
                yield
            S.free[si] = t1
            t_r1[h] = tr1

        t_r1 = [None] * 2

        for g in range(NG):
            if g == NG - 1:
                sqn["buf"], sqn["free"] = SQP, [None] * 4
            if g < NG - 1:
                for j2 in range(4):
                    tok = one_unit(("wo", g, j2), pair(j2), wo_rhs(g), wo_tok(g), 4, wo_evac(g))
                    mods(4)
            else:
                mods(96)
                mod_sum(0)
                ta = ts(A1, modcol[:, 8:16], 1.0, None, ALU.add, None, t_mod[2], t_mod[3])
                ta = tt(A1, A1, vcols("n1", 8), ALU.mult, ta)
                t_w1 = tt(W1, A1, vcols("fin_w", 8), ALU.mult, ta)
                one_unit(("wo", g, 0), pair(0), wo_rhs(g), wo_tok(g), 4, wo_evac(g))
                rate[0] = 1.0
                tok = by_halves([(("wo", g, j2), pair(j2)) for j2 in (1, 2, 3)], wo_rhs(g), wo_tok(g), 4, wo_evac(g),
                                lambda: bg.append(between_blocks(0)))
            for k in range(4):
                mx_free[(4 * g + k) % NM_] = tok
            for e in range(4 * g + 5, min(4 * g + 9, 16)):
                hb_free[0] = mixed(e, B)
                mods(4)
        drain()

        p4 = [None]
        xo = x0
        CO = [at(f"CO{f}", 1024, F32, xo + f * K4) for f in range(8)]
        UPW = NSEG * SEGP
        UP = [at(f"UP{i}", UPW, F32, xo + 8 * K4 + i * UPW * 4) for i in range(4)]
        po = xo + 8 * K4 + 4 * UPW * 4
        SG = CO[7]
        PR = [at(f"PR{i}", 1024, F32, po + i * K4) for i in range(3)]
        UPH, UPL = at("UPH", UPW, F32R, hb0), at("UPL", UPW, F32R, hb0 + UPW * 4)
        DGH = [at(f"DGH{i}", 128, F32R, hb0 + (12 + i) * 1024) for i in range(TAPS)]
        DGL = [at(f"DGL{i}", 128, F32R, hb0 + (12 + i) * 1024 + 512) for i in range(TAPS)]
        WTH, WTL = at("WTH", 32, F32R, hb0 + 43 * 1024), at("WTL", 32, F32R, hb0 + 43 * 1024 + 128)
        DGV0 = [at(f"DGV0{h}", 512, F32, hb0 + (44 + 4 * h) * 1024) for h in range(2)]
        DGR1 = [at(f"DGR1{h}", 512, F32, hb0 + (52 + 4 * h) * 1024) for h in range(2)]
        YT = [at(f"YT{i}", 512, F32, hb0 + (46 + 4 * i) * 1024) for i in range(4)]
        M3B = [at(f"M3B{h}", 512, F32, hb0 + (60 + 2 * h) * 1024) for h in range(2)]
        R1B = at("R1B", 1024, F32, xo + 17 * K4 + 2048)

        def seg(b):
            return b[:, :].rearrange("p (s t) -> p s t", s=NSEG)

        up_ring = Ring(UP)
        co_tok = {}
        conv_state = {}

        def tap(up, k):
            return seg(up)[:, :, k:k + SEG]

        def wcol(f, k):
            return vcol("w_dw", f * TAPS + k)

        def parts(f):
            return [(0, 8), (8, 16)] if f in BY_HALVES else [(0, 16)]

        def finished(f, a, b, t):
            for h in range(a // 8, b // 8):
                co_tok[f, h] = t

        def conv_dve(f, ui, up, tu):
            for a, b in parts(f):
                co, other = seg(CO[f])[:, a:b, :], seg(PR[2])[:, a:b, :]

                def src(k):
                    return tap(up, k)[:, a:b, :]

                cost = 1.2 if b - a == 16 else 0.67
                ta = ts(co, src(0), wcol(f, 0), vcol("b_dw", f), ALU.mult, ALU.add, tu, p4)
                if f in FROM_MEAN:
                    m = M3B[a // 8][:, :].rearrange("p (s t) -> p s t", s=8)
                    tb = stt(other, src(1), wcol(f, 1), m, ALU.mult, ALU.subtract, tu, conv_state["dve"], ln["mb"])
                else:
                    tb = ts(other, src(1), wcol(f, 1), None, ALU.mult, None, tu, conv_state["dve"])
                for k in range(2, TAPS):
                    yield cost
                    dst = co if k % 2 == 0 else other
                    t = stt(dst, src(k), wcol(f, k), dst, ALU.mult, ALU.add, ta if k % 2 == 0 else tb)
                    if k % 2 == 0:
                        ta = t
                    else:
                        tb = t
                conv_state["dve"] = t2 = tt(co, co, other, ALU.add, ta, tb)
                finished(f, a, b, t2)
                yield cost
            up_ring.free[ui] = t

        def conv_pool(f, ui, up, tu):
            n = 0
            for a, b in parts(f):
                co = seg(CO[f])[:, a:b, :]
                t = act(co, tap(up, 0)[:, a:b, :], ACT.Identity, tu, p4, scale=wcol(f, 0), bias=vcol("b_dw", f))
                for k in range(1, TAPS):
                    i, n = n % 2, n + 1
                    pr = seg(PR[i])[:, a:b, :]
                    tp_ = act(pr, tap(up, k)[:, a:b, :], ACT.Copy, tu, conv_state["pool"][i], scale=wcol(f, k))
                    t = tt(co, co, pr, ALU.add, tp_, t, q=PO)
                    conv_state["pool"][i] = t
                    yield 2.35 * (b - a) / 16
                finished(f, a, b, t)
            up_ring.free[ui] = tp_

        def pe_operands(f, up, tus, free_hb):
            w = vcols("w_dw", 8 * TAPS)[:, f * TAPS:(f + 1) * TAPS]
            tw = copy(WTH[:, 0:TAPS], w, t_vec, free_hb)
            twl = tt(WTL[:, 0:TAPS], w, WTH[:, 0:TAPS].bitcast(F32), ALU.subtract, tw)
            tu = []
            for h in range(2):
                sl = slice(h * UPW // 2, (h + 1) * UPW // 2)
                th = copy(UPH[:, sl], up[:, sl], tus, free_hb)
                tu.append((th, tt(UPL[:, sl], up[:, sl], UPH[:, sl].bitcast(F32), ALU.subtract, th)))
            return tw, twl, tu

        diag = {}

        def conv_pe(f, h, tw, twl, tu, at_tap, beside=()):
            i, bank, free = B.take()
            for k in range(TAPS):
                if k not in diag:
                    diag[k] = (act(DGH[k][:, :], ident[:, :], ACT.Copy, tw, scale=WTH[:, k:k + 1].bitcast(F32)),
                               act(DGL[k][:, :], ident[:, :], ACT.Copy, twl, scale=WTL[:, k:k + 1].bitcast(F32)))
                tdh, tdl = diag[k]
                for n, (d, u, td) in enumerate(((DGH[k], UPH, tdh), (DGH[k], UPL, tdh), (DGL[k], UPH, tdl))):
                    tok = mm(bank, d[:, :], tap(u, k)[:, h * 8:(h + 1) * 8, :], k == 0 and n == 0,
                             k == TAPS - 1 and n == 2, td, tu[h], free)
                tick(3 * PASS)
                if k in at_tap:
                    at_tap[k]()
                for start, steps, work in beside:
                    for _ in range(steps if k >= start else 0):
                        next(work, None)
            return i, bank, tok

        def take_up():
            ui, up, ufree = up_ring.take()
            while ufree is None:
                lanes_step()
                ufree = up_ring.free[ui]
            up_ring.free[ui] = None
            return ui, up, ufree

        rate[0] = 1.0
        got = [u_get("pa", 0), u_get("pg", 0), u_get("pa", 1)]
        banks = {}
        bg.append(between_blocks(1))
        for h in range(2):
            if h == 1:
                drain()
            bs = [B.take() for _ in got]
            toks = gemm_units([w for j, *w in got], [(h, bank, free) for i, bank, free in bs], unit_k, hb, hb_tok, 8)
            for n, ((j, *w), (i, bank, free)) in enumerate(zip(got, bs)):
                banks[n, h] = (i, bank, toks[n])
                if h:
                    u_done(j, toks[n])
        p4[0] = [rt_[7, 0], rt_[7, 1], hbt[7, 0], hbt[7, 1], tm_free, sqn["free"], sta, stb, t_r1]
        conv_state.update(sg=p4, dve=p4, pool=[p4, p4])
        for i in range(4):
            pads = [seg(UP[i])[:, :, 0:PAD], seg(UP[i])[:, :, PAD + SEG:SEGP]]
            up_ring.free[i] = [DV(lambda e, p=p: e.memset(p, 0.0), p4) for p in pads]
        hi_by[0] = AC

        def product(*kind):
            j, *w = u_get(*kind)
            out_ = []
            for h in range(2):
                i, bank, free = B.take()
                out_.append((i, bank, gemm([(h, bank, free)], w, unit_k, hb, hb_tok, 8)[h]))
            u_done(j, out_[1][2])
            return out_

        DL, RV, D2, DR = (small[:, 128 + 8 * i:136 + 8 * i] for i in range(4))
        ln = {"n": 0, "bank": {}, "open": {}, "v": [None, None]}
        y_free = [None] * 4
        y_tok = {}

        def first_mean():
            while not all((f, h) in co_tok for f in MEAN_OF for h in range(2)):
                lanes_step()
            banks3 = [B.take() for h in range(2)]
            for f in MEAN_OF:
                for h, (i, bank, free) in enumerate(banks3):
                    tok = mm(bank, ones[:, :], cut(CO[f], h), f == MEAN_OF[0], f == MEAN_OF[-1], co_tok[f, h], free)
                    yield
            ln["sum"] = [(i, bank, tok) for i, bank, _ in banks3]

        def mean_rows(free_hb):
            ln["mb"] = []
            for h, (i, bank, tok) in enumerate(ln["sum"]):
                B.free[i] = copy(M3B[h][:, :], bank, tok, free_hb, scale=1.0 / (len(MEAN_OF) * 128))
                ln["mb"].append(B.free[i])

        def first_norm_rows():
            for h in range(2):
                i, Rb, tR = spread(hs(R1, h), t_r1[h], DGR1[h][:, :], S.take, last_pw1)
                S.free[i] = copy(cut(R1B, h), Rb, tR, p4)
                t_r1b.append(S.free[i])

        t_r1b = []

        def shift(f, h):
            c = cut(CO[f], h)
            y_tok[f, h] = tt(c, c, M3B[h][:, :], ALU.subtract, ln["mb"], co_tok[f, h])

        def shifts(tiles):
            for f in tiles:
                for h in range(2):
                    shift(f, h)
                    yield 0.6

        def stats(f, h, last=False):
            i = ln["n"] % 4
            ln["n"] += 1
            y, src = YT[i], cut(CO[f], h)
            q = act(y[:, :], src, ACT.Square, y_tok[f, h], y_free[i], last_pw1)
            for c, a, t in (("y", src, y_tok[f, h]), ("yy", y[:, :], q)):
                if c == "y" and f in MEAN_OF:
                    continue
                _, _, bank, free = ln["bank"][h, c]
                tp = mm(bank, ones[:, :], a, (h, c) not in ln["open"], last, t, free)
                ln["open"][h, c] = True
                now["pe"] += 4 * PASS
                yield
            y_free[i] = ln["v"][h] = tp

        def columns(h):
            rows, toks = ROWS[h], {}
            free = [list(co_tok.values()), t_pe] if h else [t_r1b]
            for n, c in enumerate(("yy", "y")):
                ring, i, bank, _ = ln["bank"][h, c]
                toks[c] = ring.free[i] = copy(rows[n][0:1, :], bank[0:1, :], ln["v"][h], free)
            i, bank, free = S.take()
            for n, c in enumerate(("yy", "y")):
                for t in range(4):
                    tok = mm(bank[:, 4 * n + t:4 * n + t + 1], rows[n][0:1, t * 128:(t + 1) * 128],
                             ones[0:1, 0:1], n == 0 and t == 0, True, toks[c], free, skip=True)
            return i, bank, tok

        def early_stats(h):
            while not all((f, h) in y_tok for f in range(4)):
                lanes_step()
            for f in range(4):
                yield from stats(f, h)

        def last_stats(h, pe_bank):
            while not all((f, h) in co_tok for f in range(7)):
                lanes_step()
            now["dve"] = now["pe"]
            for f in (4, 5):
                shift(f, h)
            y_tok[6, h] = co_tok[6, h]
            i, bank, t_pe = pe_bank
            y_tok[7, h] = B.free[i] = stt(cut(CO[7], h), bank, vcol("b_dw", 7), M3B[h][:, :], ALU.add, ALU.subtract,
                                          t_pe, ln["mb"], conv_state["sg"])
            for f in (4, 5, 6, 7):
                yield from stats(f, h, f == 7)

        lo_ = xo + 8 * K4
        DGV, DGD = [DGV0[0], at("DGV", 512, F32, lo_)], [DGR1[0], at("DGD", 512, F32, lo_ + 2048)]
        ROWS = [[DGV0[1], DGR1[1]], [at(f"ROW{i}", 512, F32, lo_ + K4 + i * 2048) for i in range(2)]]
        z_tok = {}

        def normed(h):
            i, bank, tok = columns(h)
            t1 = ts(hs(DL, h), bank[:, 4:8], 1.0 / D, None, ALU.mult, None, tok)
            t2 = S.free[i] = ts(hs(RV, h), bank[:, 0:4], 1.0 / D, EPS, ALU.mult, ALU.add, tok)
            t1 = tt(hs(D2, h), hs(DL, h), hs(DL, h), ALU.mult, t1)
            t2 = tt(hs(RV, h), hs(RV, h), hs(D2, h), ALU.subtract, t1, t2)
            t_rv = PO(lambda e: e.tensor_tensor(hs(RV, h), hs(RV, h), mhalf[:, 0:4], ALU.pow), t2, t_mh)
            t_dr = tt(hs(DR, h), hs(DL, h), hs(RV, h), ALU.mult, t_rv)
            for _ in range(WAIT[2]):
                yield
            free = [list(co_tok.values()), t_pe] if h else [ln["mb"], t_r1b]
            ri, Rb, tR = spread(hs(RV, h), t_rv, DGV[h][:, :], B.take, free)
            di, Db, tD = spread(hs(DR, h), t_dr, DGD[h][:, :], B.take, free)
            for f in range(8):
                c = cut(CO[f], h)
                t1 = tt(c, c, Rb, ALU.mult, tR, y_tok[f, h], ln["v"][h])
                t2 = tt(c, c, Db, ALU.subtract, tD, t1)
                z_tok[f, h] = act(c, c, ACT.Silu, t2, scale=vcol("ln_g", f), bias=vcol("ln_b", f))
                split_z(f, h)
                yield
            B.free[ri], B.free[di] = t1, t2

        def split_z(f, h):
            th = copy(hb(0, f, h), cut(CO[f], h), z_tok[f, h], hb_free[0])
            tl = tt(hb(1, f, h), cut(CO[f], h), hb(0, f, h).bitcast(F32), ALU.subtract, th, hb_free[0], q=PO)
            hbt[f, h] = (th, tl)

        for f in range(8):
            ui, up, ufree = take_up()
            a_b = [banks[2 * f, h] for h in range(2)] if f < 2 else product("pa", f)
            if f == 7:
                rate[0] = 0.8
                bg.append(first_mean())
            g_b = [banks[1, h] for h in range(2)] if f == 0 else product("pg", f)
            tus = []
            for h in range(2):
                (ai, ab, atok), (gi, gb, gtok) = a_b[h], g_b[h]
                t1 = B.free[gi] = act(cut(SG, h), gb, ACT.Sigmoid, gtok, conv_state["sg"], bias=vcol("b_pw1", 8 + f))
                tu = B.free[ai] = stt(seg(up)[:, 8 * h:8 * h + 8, PAD:PAD + SEG], ab.rearrange("p (s t) -> p s t", s=8),
                                      vcol("b_pw1", f), seg(SG)[:, 8 * h:8 * h + 8, :], ALU.add, ALU.mult,
                                      atok, t1, ufree)
                tus.append(tu)
            conv_state["sg"] = tus
            now["dve"] += 1.4
            if CONV[f] != "pe":
                lane_add(CONV[f], {"dve": conv_dve, "pool": conv_pool}[CONV[f]](f, ui, up, tus))
        last_pw1 = g_b[1][2]
        hi_by[0] = PO
        pe_ops = pe_operands(7, up, tus, last_pw1)
        drain()

        def means_out():
            mean_rows(last_pw1)

        def take_sums():
            first_norm_rows()
            for h, ring in enumerate((S, B)):
                for c in ("y", "yy"):
                    ln["bank"][h, c] = (ring,) + ring.take()

        rate[0] = 1.0
        early = early_stats(0)
        b0 = conv_pe(7, 0, *pe_ops, {1: means_out, 4: take_sums, SHIFT_AT: lambda: lanes["dve"].insert(0, shifts(range(4)))},
                     [(LN_AT[0], 1, early)])
        first = normed(0)
        more, late = early_stats(1), last_stats(0, b0)
        b1 = conv_pe(7, 1, *pe_ops, {}, [(0, 1, early), (0, 1, more), (LN_AT[1], 1, late)])
        t_pe = b1[2]
        for work in (early, more, late):
            for _ in work:
                pass
        hb_free[0] = [last_pw1, t_pe]
        while len(lanes["dve"]) and now["dve"] < now["pe"] + LN_AT[2]:
            lane_step("dve")
        for n, _ in enumerate(first):
            if n < WAIT[2] and lanes["dve"]:
                lane_step("dve")
            elif n == WAIT[2]:
                while lanes["dve"] or lanes["pool"]:
                    lanes_step()
                for _ in last_stats(1, b1):
                    pass
                second = normed(1)
        while len(split_tok) < len(load_tok):
            u_split()
        hb_free[0] = [last_pw1, t_pe, ln["v"]]
        next(second)
        bg.append(second)
        conv_done = [list(co_tok.values()), list(y_tok.values()), t_pe, conv_state["pool"]]
        p5 = [conv_done]

        GBV = small[:, 120:128]
        tgb = tt(GBV, modcol[:, 16:24], vcols("b_pw2", 8), ALU.mult, t_mod[4], t_mod[5])
        ACC3 = at("ACC3", 1024, F32, xo + 10 * K4)
        sqn["buf"], sqn["free"], sqn["n"] = [at(f"SQ3{i}", 512, F32, xo + 11 * K4 + i * 2048) for i in range(4)], [p5] * 4, 0
        EV = [at(f"EV{i}", 512, F32, xo + 13 * K4 + i * 2048) for i in range(4)]
        ev_free, ev_n = [p5] * 4, [0]
        st3 = [None, None]

        def pw2_evac(f, h, bank, tok):
            i = ev_n[0] % 4
            ev_n[0] += 1
            ev = EV[i]
            t1 = act(ev[:, :], bank, ACT.Identity, tok, ev_free[i], tgb, scale=modcol[:, 16 + f:17 + f],
                     bias=GBV[:, f:f + 1])
            t2 = stt(rh(f, h), rh(f, h), vcol("fin_w", f), cut(R1B, h), ALU.mult, ALU.mult, t_r1b, rt_[f, h])
            ev_free[i] = rt_[f, h] = tt(rh(f, h), rh(f, h), ev[:, :], ALU.add, t1, t2)
            add_late()
            add_sq(ACC3, f, h, st3, rt_[f, h], p5)
            return t1

        R3, A2 = small[:, 160:168], small[:, 168:176]
        ta = ts(A2, modcol[:, 32:40], 1.0, None, ALU.add, None, t_mod[8], t_mod[9])
        t_a2 = tt(A2, A2, vcols("n2", 8), ALU.mult, ta)
        DG3 = at("DG3", 1024, F32, xo + 15 * K4)
        TN = [at(f"TN{i}", 512, F32, xo + i * 2048) for i in range(4)]

        def before_mlp(h):
            for _ in range(WAIT[0] + h):
                yield
            add_late()
            si, ss, tp = sums(ACC3, st3[h], range(4 * h, 4 * h + 4))
            S.free[si], tr_ = inv_root(hs(R3, h), ss, D, tp)
            for _ in range(WAIT[2]):
                yield
            si, Rb, tR = spread(hs(R3, h), tr_, DG3[:, h * 512:(h + 1) * 512], S.take, p5)
            for t1 in modulated(h, TN, A2, modcol[:, 24:32], Rb, tR, t_a2, t_mod[6], t_mod[7], p5):
                yield
            S.free[si] = t1
            mlp_in[h] = t1

        mlp_in = [None, None]

        def plain(f):
            return [(f, unit_k)]

        rate[0] = 1.0

        def normed_all():
            drain()
            p5[0] = [conv_done, list(hbt.values()), list(z_tok.values())]

        tok = by_halves([(("pw2", f), plain(f)) for f in range(3)], hb, hb_tok, 8, pw2_evac, normed_all, True)
        for f in (3, 4):
            one_unit(("pw2", f), plain(f), hb, hb_tok, 8, pw2_evac)

        def first_half_done():
            hb_half[0] = PE.ops[-1][0]
            hb_free[0] = hb_half[0]
            bg.append(before_mlp(0))

        hb_half = [None]
        tok = by_halves([(("pw2", f), plain(f)) for f in (5, 6, 7)], hb, hb_tok, 8, pw2_evac, first_half_done)
        drain()
        hb_free[0] = tok

        NH = 2 * GT
        HID = [(at(f"HIDH{i}", 1024, F32R, xo + (2 * i) * K4), at(f"HIDL{i}", 1024, F32R, xo + (2 * i + 1) * K4))
               for i in range(NH)]
        RL = at("RL", 512, F32, xo + 2 * NH * K4)
        hid_tok = {}
        rl_free = [None]
        p6 = [None]
        hid_free = [None] * NH

        def hid_evac(i, h, bank, tok):
            s = i % NH
            hi, lo = HID[s]
            cs = slice(h * 512, (h + 1) * 512)
            t1 = act(RL[:, :], bank, ACT.Relu, tok, rl_free[0], p6)
            t2 = stt(bank, bank, 0.0, RL[:, :], ALU.max, ALU.mult, t1)
            th = copy(hi[:, cs], bank, t2, hid_free[s], p6)
            tl = tt(lo[:, cs], bank, hi[:, cs].bitcast(F32), ALU.subtract, th, t2, hid_free[s], p6)
            rl_free[0] = t2
            hid_tok[i, h] = (th, tl)
            return tl

        FIN = [at(f"FIN{i}", 1024, F32, hb0 + i * K4) for i in range(8)]
        SQ4 = [at(f"SQ4{i}", 512, F32, hb0 + i * 2048) for i in range(4)]
        ACC4, DG4 = FIN[2], FIN[3]
        st4 = [None, None]
        t_w1 = None

        def w2_rhs(g):
            return lambda part, k, h: HID[(GT * g + k) % NH][part][:, h * 512:(h + 1) * 512]

        def w2_tok(g):
            return lambda part, k, h: hid_tok[GT * g + k, h][part]

        def w2_evac(g):
            def evac(f, h, bank, tok):
                t = rt_[f, h] = stt(rh(f, h), bank, modcol[:, 40 + f:41 + f], rh(f, h), ALU.mult, ALU.add, tok,
                                    t_mod[10], t_mod[11], rt_[f, h], mlp_in)
                add_late()
                if g == HG - 1:
                    add_sq(ACC4, f, h, st4, t, hb_free[0])
                return t
            return evac

        R4 = small[:, 160:168]
        o_ch = [chan(f"d_out{i}") for i in range(16)]
        outs = []

        def last_norm(h):
            for _ in range(WAIT[0] + h):
                yield
            add_late()
            si, ss, tp = sums(ACC4, st4[h], range(4 * h, 4 * h + 4))
            S.free[si], tr_ = inv_root(hs(R4, h), ss, D, tp)
            for _ in range(WAIT[2]):
                yield
            si, Rb, tR = spread(hs(R4, h), tr_, DG4[:, h * 512:(h + 1) * 512], S.take, hb_free[0])
            for k in range(8):
                t1 = stt(rh(k, h), rh(k, h), vcol("fin_g", k), Rb, ALU.mult, ALU.mult, tR, rt_[k, h], st4[h])
                outs.append(SP.dma(o_ch[8 * h + k], lambda e, k=k: e.dma_start(
                    out[k * 128:(k + 1) * 128, h * 512:(h + 1) * 512], rh(k, h)), t1))

        bg.append(before_mlp(1))
        got = [u_get("w1", i) for i in range(3)]
        held = []
        for h in range(2):
            if h == 1:
                drain()
                p6[0] = [mlp_in, hbt[7, 0], hbt[7, 1], tm_free, st3, sqn["free"], ev_free]
                for i, hh, bank, bi, tok in held:
                    B.free[bi] = hid_evac(i, hh, bank, tok)
            bs = [B.take() for _ in got]
            toks = gemm_units([w for j, *w in got], [(h, bank, free) for bi, bank, free in bs], unit_k, hb, hb_tok, 8)
            for n, ((j, *w), (bi, bank, free), tok) in enumerate(zip(got, bs, toks)):
                if h == 0:
                    held.append((n, h, bank, bi, tok))
                else:
                    B.free[bi] = hid_evac(n, h, bank, tok)
                    u_done(j, tok)
        for i in range(3, GT):
            t_w1 = one_unit(("w1", i), plain(i), hb, hb_tok, 8, hid_evac)
        for g in range(HG):
            if g + 1 < HG:
                for i in range(GT):
                    n = (g + 1) * GT + i
                    t_w1 = one_unit(("w1", n), plain(n), hb, hb_tok, 8, hid_evac)
                for j2 in range(4):
                    tok = one_unit(("w2", g, j2), pair(j2), w2_rhs(g), w2_tok(g), GT, w2_evac(g))
            else:
                hb_free[0] = t_w1
                sqn["buf"], sqn["free"] = SQ4, [t_w1] * 4
                one_unit(("w2", g, 0), pair(0), w2_rhs(g), w2_tok(g), GT, w2_evac(g))
                by_halves([(("w2", g, j2), pair(j2)) for j2 in (1, 2, 3)], w2_rhs(g), w2_tok(g), GT, w2_evac(g),
                          lambda: bg.append(last_norm(0)))
                drain()
                bg.append(last_norm(1))
                drain()
            for k in range(GT):
                hid_free[(GT * g + k) % NH] = tok

        for q in (PE, AC, DV, PO, SP):
            q.number()
        block = es.enter_context(nc.Block())

        @block.tensor
        def _(eng):
            PE.emit(eng)

        @block.scalar
        def _(eng):
            AC.emit(eng)

        @block.vector
        def _(eng):
            DV.emit(eng)

        @block.gpsimd
        def _(eng):
            PO.emit(eng)

        @block.sync
        def _(eng):
            SP.emit(eng)
            for w in list(ot_out.values()) + outs:
                eng.wait_ge(w.sem, w.count)


def lay_out(inputs):
    f = {n: np.asarray(a) for n, a in inputs.items()}
    w_in, w_out = f["w_in"][0], f["w_out"][0]
    kv, pw1, pw2 = f["w_mem_kv"][0], f["conv_w_pw1_2"][0], f["conv_w_pw2_2"][0]
    w1, w2 = f["mlp_w1_2"][0], f["mlp_w2_2"][0]
    OFF = {}
    at = 0
    for n, c in (("gq", 512), ("gk", 512), ("gv", 1024), ("glr", 16), ("hq", 512), ("hf", 512), ("hi", 512),
                 ("xq", 512), ("gate", 2048)):
        OFF[n] = at
        at += c

    def cols(w, c0, n, k0=0, nk=8):
        return w[k0 * 128:(k0 + nk) * 128, c0:c0 + n].reshape(nk, 128, n).transpose(1, 0, 2)

    wall = np.zeros((len(UNITS), 128, 1024), np.float32)
    for i, u in enumerate(UNITS):
        n = u[0]
        if n == "mk":
            t = cols(kv, u[1] * 128, 128)
        elif n == "mv":
            t = cols(kv, 512, 512, 2 * u[1], 2)
        elif n == "glr":
            wall[i].reshape(128, 8, 128)[:, :, 0:16] = cols(w_in, OFF["glr"], 16)
            continue
        elif n in ("gv", "hi"):
            t = cols(w_in, OFF[n] + u[1] * 256, 256, 4 * u[2], 4)
        elif n in OFF:
            t = cols(w_in, OFF[n] + u[1] * 128, 128)
        elif n == "wo":
            t = cols(w_out, u[2] * 256, 256, 4 * u[1], 4)
        elif n == "pa":
            t = cols(pw1, u[1] * 128, 128)
        elif n == "pg":
            t = cols(pw1, 1024 + u[1] * 128, 128)
        elif n == "pw2":
            t = cols(pw2, u[1] * 128, 128)
        elif n == "w1":
            t = cols(w1, u[1] * 128, 128)
        elif n == "w2":
            t = cols(w2, u[2] * 256, 256, GT * u[1], GT)
        wall[i].reshape(t.shape)[...] = t
    wm = f["w_mod_2"][0]
    wmod = np.ascontiguousarray(wm.reshape(8, 128, 12, 512).transpose(2, 0, 1, 3)).reshape(96, 128, 512)

    def col(a):
        return a.reshape(-1, 128).T

    dw = f["conv_w_dw_2"][0].T.reshape(8, 128, TAPS).transpose(1, 0, 2).reshape(128, 8 * TAPS)
    parts = {"norm_w": f["norm_w"], "b_gate": f["gla_b_gate"], "gla_nw": f["gla_norm_w"], "lb": f["hgrn_lower_bounds"],
             "hgrn_nw": f["hgrn_norm_w"], "mem_nw": f["mem_norm_w"], "x_nw": f["xattn_norm_w"],
             "fin_w": f["final_norm_w"], "c": f["c_2"], "b_mod": f["b_mod_2"], "n1": f["norm1_g_2"],
             "n2": f["norm2_g_2"], "fin_g": f["final_g_2"], "b_pw1": f["conv_b_pw1_2"], "b_dw": f["conv_b_dw_2"],
             "ln_g": f["conv_ln_g_2"], "ln_b": f["conv_ln_b_2"], "b_pw2": f["conv_b_pw2_2"]}
    vecs = np.concatenate([dw if n == "w_dw" else col(parts[n]) for n, _ in VECS], axis=1)
    xT = f["x"][0].T.reshape(8, 128, T).transpose(1, 0, 2)
    memT = f["mem"][0].T.reshape(8, 128, 256).transpose(1, 0, 2).reshape(128, 2048)
    ident = np.eye(128, dtype=np.float32)
    masks = np.zeros((128, 7, 64), np.float32)
    for l in range(7):
        H = 1 << l
        for b in range(64 // H):
            masks[b * 2 * H:b * 2 * H + H, l, b * H:(b + 1) * H] = 1
    masks = masks.reshape(128, 448)
    arrays = {"wall": wall, "wmod": wmod, "xT": xT, "memT": memT, "vecs": vecs, "gup": f["gla_w_gate_up"][0],
              "ident": ident, "masks": masks}
    return {n: np.ascontiguousarray(a) for n, a in arrays.items()}


def kernel(**inputs):
    import concourse.bacc as bacc
    from concourse.bass_utils import run_bass_kernel_spmd

    nc = bacc.Bacc("TRN2", target_bir_lowering=False, num_devices=1)
    arrays = lay_out(inputs)
    aps = [nc.dram_tensor(n, a.shape, mybir.dt.from_np(a.dtype), kind="ExternalInput").ap() for n, a in arrays.items()]
    out = nc.dram_tensor("outT", (D, T), F32, kind="ExternalOutput").ap()
    oscr = nc.dram_tensor("oscr", (16, 128, T), F32, kind="Internal").ap()
    build_program(nc, *aps, out, oscr)
    r = run_bass_kernel_spmd(nc, [arrays], core_ids=[0])
    return np.ascontiguousarray(r.results[0]["outT"].T)[None]
```
